# Optimizing a Trainium2 kernel written in Bass

```python
import jax, jax.numpy as jnp
from jax import lax
import numpy as np

D_MODEL = 1024
BATCH = 1
SEQ = 512
DEPTH = 1
DEC_BATCH = 8
DEC_SEQ = 4
PAST_LEN = 2048
PAGE_SIZE = 128

H_A = 8
NOPE_DIM = 64
ROPE_DIM = 32
V_DIM = 64
Q_LORA = 768
KV_LORA = 256
MLA_THETA = 10000.0
H_B = 8
HD_B = 64
ROT_B = HD_B // 4
ROPE_THETA = 500000.0
DILATIONS = ((128, 1), (512, 4), (2048, 16))
WIN_MAX = 2048
BAND_BLOCK = 128
Q_BLOCK = 128
D_FF = -(-8 * D_MODEL // (3 * 256)) * 256
PLE_DIM = 256
EPS = 1e-6
NEG_INF = -1e30
B_WIDTH = H_B * HD_B
_A_END = Q_LORA + KV_LORA + ROPE_DIM
SPLIT_POINTS = (Q_LORA, Q_LORA + KV_LORA, _A_END, _A_END + B_WIDTH, _A_END + 2 * B_WIDTH)
IN_WIDTH = _A_END + 3 * B_WIDTH
MIX_WIDTH = H_A * V_DIM + H_B * HD_B

kernel_name = 'hybrid_mla_dilated_swa_decoder_step'

def rmsnorm(x, g):
    xf = x.astype(jnp.float32)
    y = xf * lax.rsqrt(jnp.mean(xf * xf, axis=-1, keepdims=True) + EPS)
    return (y * g.astype(jnp.float32)).astype(x.dtype)

def rope(x, pos, theta):
    half = x.shape[-1] // 2
    inv = theta ** (-jnp.arange(half, dtype=jnp.float32) / half)
    ang = pos.astype(jnp.float32)[:, None] * inv[None, :]
    cos, sin = jnp.cos(ang), jnp.sin(ang)
    if x.ndim == 4:
        cos, sin = cos[:, None], sin[:, None]
    xf = x.astype(jnp.float32)
    x1, x2 = xf[..., :half], xf[..., half:]
    return jnp.concatenate([x1 * cos - x2 * sin, x2 * cos + x1 * sin], axis=-1).astype(x.dtype)

def partial_rope(x, pos):
    return jnp.concatenate([rope(x[..., :ROT_B], pos, ROPE_THETA), x[..., ROT_B:]], axis=-1)

def softmax_stats(s):
    m = jnp.max(s, axis=-1, keepdims=True)
    e = jnp.exp(s - m)
    den = jnp.sum(e, axis=-1, keepdims=True)
    return e / den, (m + jnp.log(den))[..., 0]

def project_mixers(h, pos, lw):
    lead = h.shape[:-1]
    a = rmsnorm(h, lw['g_attn'])
    cq, ckv, kr, qs, ks, vs = jnp.split(a @ lw['w_in'], SPLIT_POINTS, axis=-1)
    q = (rmsnorm(cq, lw['g_qa']) @ lw['w_qb']).reshape(*lead, H_A, NOPE_DIM + ROPE_DIM)
    q_nope = rmsnorm(q[..., :NOPE_DIM], lw['g_qn'])
    q_rope = rope(rmsnorm(q[..., NOPE_DIM:], lw['g_qr']), pos, MLA_THETA)
    latent = rmsnorm(ckv, lw['g_kva'])
    k_rope = rope(rmsnorm(kr, lw['g_kr']), pos, MLA_THETA)
    qs = partial_rope(rmsnorm(qs.reshape(*lead, H_B, HD_B), lw['g_qs']), pos)
    ks = partial_rope(rmsnorm(ks.reshape(*lead, H_B, HD_B), lw['g_ks']), pos)
    vs = vs.reshape(*lead, H_B, HD_B)
    return q_nope, q_rope, latent, k_rope, qs, ks, vs

def decompress(latent, lw):
    kv = (latent @ lw['w_kvb']).reshape(*latent.shape[:-1], H_A, NOPE_DIM + V_DIM)
    return rmsnorm(kv[..., :NOPE_DIM], lw['g_kn']), kv[..., NOPE_DIM:]

def mla_prompt(q_nope, q_rope, latent, k_rope, lw):
    B, S = q_nope.shape[:2]
    k_nope, v = decompress(latent, lw)
    scale = (NOPE_DIM + ROPE_DIM) ** -0.5
    nq = S // Q_BLOCK
    qn_b = q_nope.reshape(B, nq, Q_BLOCK, H_A, NOPE_DIM).transpose(1, 0, 2, 3, 4)
    qr_b = q_rope.reshape(B, nq, Q_BLOCK, H_A, ROPE_DIM).transpose(1, 0, 2, 3, 4)
    kpos = jnp.arange(S)

    def block(args):
        qn, qr, i = args
        s = (jnp.einsum('bqhd,bkhd->bhqk', qn, k_nope)
             + jnp.einsum('bqhr,bkr->bhqk', qr, k_rope)).astype(jnp.float32) * scale
        qpos = i * Q_BLOCK + jnp.arange(Q_BLOCK)
        s = jnp.where(kpos[None, :] <= qpos[:, None], s, NEG_INF)
        p, _ = softmax_stats(s)
        return jnp.einsum('bhqk,bkhd->bqhd', p.astype(v.dtype), v)

    o = lax.map(block, (qn_b, qr_b, jnp.arange(nq)))
    return o.transpose(1, 0, 2, 3, 4).reshape(B, S, H_A * V_DIM)

def mla_sample(q_nope, q_rope, lat_new, kr_new, cache_latent, cache_krope, layer, page_table, lw):
    DB, DS = q_nope.shape[:2]
    past = page_table.shape[1] * PAGE_SIZE
    scale = (NOPE_DIM + ROPE_DIM) ** -0.5
    mask = jnp.arange(past + DS)[None, :] <= past + jnp.arange(DS)[:, None]

    def one(args):
        pt, qn, qr, lat_n, kr_n = args
        lat = jnp.concatenate([cache_latent[layer, pt].reshape(past, KV_LORA).astype(lat_n.dtype), lat_n], 0)
        kr = jnp.concatenate([cache_krope[layer, pt].reshape(past, ROPE_DIM).astype(kr_n.dtype), kr_n], 0)
        k_nope, v = decompress(lat, lw)
        s = (jnp.einsum('qhd,khd->hqk', qn, k_nope)
             + jnp.einsum('qhr,kr->hqk', qr, kr)).astype(jnp.float32) * scale
        s = jnp.where(mask[None], s, NEG_INF)
        p, _ = softmax_stats(s)
        return jnp.einsum('hqk,khd->qhd', p.astype(v.dtype), v)

    o = lax.map(one, (page_table, q_nope, q_rope, lat_new, kr_new))
    return o.reshape(DB, DS, H_A * V_DIM)

def merge_dilations(outs, lses):
    w = jax.nn.softmax(jnp.stack(lses, 0), axis=0)
    o = jnp.einsum('gbsh,gbshd->bshd', w, jnp.stack(outs, 0).astype(jnp.float32))
    return o.astype(outs[0].dtype)

def dilated_prompt_one(q, k, v, d, steps):
    B, S, H, Dh = q.shape
    M = S // d
    nb = -(-M // BAND_BLOCK)
    Mp = nb * BAND_BLOCK
    n = B * d

    def to_strided(x):
        x = x.reshape(B, M, d, H, Dh).transpose(0, 2, 1, 3, 4).reshape(n, M, H, Dh)
        return jnp.pad(x, ((0, 0), (0, Mp - M), (0, 0), (0, 0)))

    def to_band(x):
        x = jnp.pad(x, ((0, 0), (BAND_BLOCK, 0), (0, 0), (0, 0))).reshape(n, nb + 1, BAND_BLOCK, H, Dh)
        return jnp.concatenate([x[:, :-1], x[:, 1:]], axis=2)

    qb = to_strided(q).reshape(n, nb, BAND_BLOCK, H, Dh)
    kb = to_band(to_strided(k))
    vb = to_band(to_strided(v))
    s = jnp.einsum('nbqhd,nbkhd->nbhqk', qb, kb).astype(jnp.float32) * (Dh ** -0.5)
    qi = jnp.arange(BAND_BLOCK)[:, None]
    ki = jnp.arange(2 * BAND_BLOCK)[None, :]
    dist = qi + BAND_BLOCK - ki
    kidx = jnp.arange(nb)[:, None, None] * BAND_BLOCK + ki[None] - BAND_BLOCK
    valid = (dist >= 0) & (dist <= steps) & (kidx >= 0)
    s = jnp.where(valid[None, :, None], s, NEG_INF)
    p, lse = softmax_stats(s)
    o = jnp.einsum('nbhqk,nbkhd->nbqhd', p.astype(vb.dtype), vb).reshape(n, Mp, H, Dh)[:, :M]
    o = o.reshape(B, d, M, H, Dh).transpose(0, 2, 1, 3, 4).reshape(B, S, H, Dh)
    lse = lse.transpose(0, 1, 3, 2).reshape(n, Mp, H)[:, :M]
    lse = lse.reshape(B, d, M, H).transpose(0, 2, 1, 3).reshape(B, S, H)
    return o, lse

def dilated_prompt(q, k, v):
    outs, lses = [], []
    for window, d in DILATIONS:
        o, lse = dilated_prompt_one(q, k, v, d, window // d)
        outs.append(o)
        lses.append(lse)
    return merge_dilations(outs, lses)

def dilated_sample(q, k_new, v_new, k_buf, v_buf):
    DS = q.shape[1]
    L = k_buf.shape[1]
    K = jnp.concatenate([k_buf.astype(k_new.dtype), k_new], axis=1)
    V = jnp.concatenate([v_buf.astype(v_new.dtype), v_new], axis=1)
    outs, lses = [], []
    for window, d in DILATIONS:
        steps = window // d
        idx = L + jnp.arange(DS)[:, None] - d * jnp.arange(steps + 1)[None, :]
        valid = idx >= 0
        idx_c = jnp.clip(idx, 0)
        kg = K[:, idx_c]
        vg = V[:, idx_c]
        s = jnp.einsum('bqhd,bqnhd->bhqn', q, kg).astype(jnp.float32) * (HD_B ** -0.5)
        s = jnp.where(valid[None, None], s, NEG_INF)
        p, lse = softmax_stats(s)
        outs.append(jnp.einsum('bhqn,bqnhd->bqhd', p.astype(vg.dtype), vg))
        lses.append(lse.transpose(0, 2, 1))
    keep = min(WIN_MAX, L + DS)
    return merge_dilations(outs, lses), K[:, -keep:], V[:, -keep:]

def layer_tail(h, o_a, o_b, p_l, lw):
    lead = h.shape[:-1]
    mixed = jnp.concatenate([rmsnorm(o_a, lw['g_oa']),
                             rmsnorm(o_b.reshape(*lead, B_WIDTH), lw['g_ob'])], axis=-1)
    h = h + mixed @ lw['w_o']
    f = rmsnorm(h, lw['g_ffn'])
    h = h + (jax.nn.silu(f @ lw['w_gate']) * (f @ lw['w_up'])) @ lw['w_down']
    gate = jax.nn.sigmoid(rmsnorm(h, lw['g_ple']) @ lw['w_ple_gate'] + lw['b_ple_gate'])
    return h + gate * (p_l @ lw['w_ple_proj'])

def setup_inputs(seed: int = 0) -> dict:
    key = jax.random.key(seed)
    keys = list(jax.random.split(key, 40))
    f32 = jnp.float32

    def nrm(shape, scale=1.0):
        return jax.random.normal(keys.pop(), shape, f32) * scale

    def gain(n):
        return 1.0 + 0.05 * jax.random.normal(keys.pop(), (DEPTH, n), f32)

    def dense(i, o):
        return nrm((DEPTH, i, o), i ** -0.5)

    n_pages = PAST_LEN // PAGE_SIZE
    n_used = DEC_BATCH * n_pages
    n_pool = n_used + max(1, n_used // 4)
    win_buf = min(WIN_MAX, PAST_LEN)
    page_table = jax.random.permutation(keys.pop(), n_pool)[:n_used].reshape(DEC_BATCH, n_pages).astype(jnp.int32)
    return {
        'x_prompt': nrm((BATCH, SEQ, D_MODEL)),
        'x_sample': nrm((DEC_BATCH, DEC_SEQ, D_MODEL)),
        'cache_latent': nrm((DEPTH, n_pool, PAGE_SIZE, KV_LORA)),
        'cache_krope': nrm((DEPTH, n_pool, PAGE_SIZE, ROPE_DIM)),
        'cache_swa_k': nrm((DEPTH, DEC_BATCH, win_buf, H_B, HD_B)),
        'cache_swa_v': nrm((DEPTH, DEC_BATCH, win_buf, H_B, HD_B)),
        'page_table': page_table,
        'p_prompt': nrm((DEPTH, BATCH, SEQ, PLE_DIM)),
        'p_sample': nrm((DEPTH, DEC_BATCH, DEC_SEQ, PLE_DIM)),
        'g_attn': gain(D_MODEL),
        'w_in': dense(D_MODEL, IN_WIDTH),
        'g_qa': gain(Q_LORA),
        'w_qb': dense(Q_LORA, H_A * (NOPE_DIM + ROPE_DIM)),
        'g_kva': gain(KV_LORA),
        'w_kvb': dense(KV_LORA, H_A * (NOPE_DIM + V_DIM)),
        'g_qn': gain(NOPE_DIM),
        'g_qr': gain(ROPE_DIM),
        'g_kn': gain(NOPE_DIM),
        'g_kr': gain(ROPE_DIM),
        'g_qs': gain(HD_B),
        'g_ks': gain(HD_B),
        'g_oa': gain(H_A * V_DIM),
        'g_ob': gain(B_WIDTH),
        'w_o': dense(MIX_WIDTH, D_MODEL),
        'g_ffn': gain(D_MODEL),
        'w_gate': dense(D_MODEL, D_FF),
        'w_up': dense(D_MODEL, D_FF),
        'w_down': dense(D_FF, D_MODEL),
        'g_ple': gain(D_MODEL),
        'w_ple_gate': dense(D_MODEL, D_MODEL),
        'b_ple_gate': nrm((DEPTH, D_MODEL), 0.02),
        'w_ple_proj': dense(PLE_DIM, D_MODEL),
    }

def reference(x_prompt, x_sample, cache_latent, cache_krope, cache_swa_k, cache_swa_v, page_table,
              p_prompt, p_sample, g_attn, w_in, g_qa, w_qb, g_kva, w_kvb, g_qn, g_qr, g_kn, g_kr,
              g_qs, g_ks, g_oa, g_ob, w_o, g_ffn, w_gate, w_up, w_down, g_ple, w_ple_gate,
              b_ple_gate, w_ple_proj):
    past = page_table.shape[1] * PAGE_SIZE
    pos_p = jnp.arange(x_prompt.shape[1])
    pos_s = past + jnp.arange(x_sample.shape[1])
    hp, hs = x_prompt, x_sample
    lat_p, kr_p, swk_p, swv_p = [], [], [], []
    lat_s, kr_s, swk_s, swv_s = [], [], [], []
    for l in range(DEPTH):
        lw = {'g_attn': g_attn[l], 'w_in': w_in[l], 'g_qa': g_qa[l], 'w_qb': w_qb[l],
              'g_kva': g_kva[l], 'w_kvb': w_kvb[l], 'g_qn': g_qn[l], 'g_qr': g_qr[l],
              'g_kn': g_kn[l], 'g_kr': g_kr[l], 'g_qs': g_qs[l], 'g_ks': g_ks[l],
              'g_oa': g_oa[l], 'g_ob': g_ob[l], 'w_o': w_o[l], 'g_ffn': g_ffn[l],
              'w_gate': w_gate[l], 'w_up': w_up[l], 'w_down': w_down[l], 'g_ple': g_ple[l],
              'w_ple_gate': w_ple_gate[l], 'b_ple_gate': b_ple_gate[l], 'w_ple_proj': w_ple_proj[l]}
        qn, qr, lat, kr, qs, ks, vs = project_mixers(hp, pos_p, lw)
        o_a = mla_prompt(qn, qr, lat, kr, lw)
        o_b = dilated_prompt(qs, ks, vs)
        keep = min(WIN_MAX, ks.shape[1])
        lat_p.append(lat)
        kr_p.append(kr)
        swk_p.append(ks[:, -keep:])
        swv_p.append(vs[:, -keep:])
        hp = layer_tail(hp, o_a, o_b, p_prompt[l], lw)
        qn, qr, lat, kr, qs, ks, vs = project_mixers(hs, pos_s, lw)
        o_a = mla_sample(qn, qr, lat, kr, cache_latent, cache_krope, l, page_table, lw)
        o_b, k_buf, v_buf = dilated_sample(qs, ks, vs, cache_swa_k[l], cache_swa_v[l])
        lat_s.append(lat)
        kr_s.append(kr)
        swk_s.append(k_buf)
        swv_s.append(v_buf)
        hs = layer_tail(hs, o_a, o_b, p_sample[l], lw)
    return (hp, hs, jnp.stack(lat_p), jnp.stack(kr_p), jnp.stack(swk_p), jnp.stack(swv_p),
            jnp.stack(lat_s), jnp.stack(kr_s), jnp.stack(swk_s), jnp.stack(swv_s))


_drawn_inputs = setup_inputs


def setup_inputs(seed=0):
    import zlib

    import numpy as np

    out = dict(_drawn_inputs(seed))
    spreads = {}
    factors = {'g_qr': 5.034, 'g_kn': 2.971, 'g_ple': 8.0, 'b_ple_gate': 52.78}
    for name, (base, spread) in spreads.items():
        noise = np.random.default_rng([zlib.crc32(name.encode()), seed]).standard_normal(out[name].shape)
        drawn = base * np.exp(spread * noise) if base else spread * noise
        out[name] = __import__('jax').numpy.asarray(drawn.astype(out[name].dtype))
    for name, factor in factors.items():
        out[name] = (out[name] * factor).astype(out[name].dtype)
    return out
```

```python
from contextlib import ExitStack

import concourse.bass as bass
from concourse import mybir

F32 = mybir.dt.float32
I32 = mybir.dt.int32
ACT = mybir.ActivationFunctionType
ALU = mybir.AluOpType
AX = mybir.AxisListType
ADD_ALL = bass.bass_isa.ReduceOp.add
MAX_ALL = bass.bass_isa.ReduceOp.max

P = 128
D = 1024
KD = D // P
NP_ = 512
NB, NQ = 8, 4
NS = NB * NQ
T = NP_ + NS
HT = T // 2
H = 8
NOPE, ROPE, HQ = 64, 32, 96
QL, KVL = 768, 256
KQ, KC = QL // P, KVL // P
DFF = 2816
KF = DFF // P
HD = 64
HP = H // 2
PAST, PAGE = 2048, 128
NPG = PAST // PAGE
POOL = 160
PLE = 256
EPS = 1e-6
NEG = -1e30
SC_A = HQ ** -0.5
SC_B = HD ** -0.5
NIN = 17
U_CQ, U_LAT, U_KR, U_QS, U_KS = 0, 6, 8, 9, 13
RING = 4
SLOT = 11 * P
REC = 512
STR = (PAST - REC) // 16
LOOP_LINKS = 9
NT_W = 9
PR = 8

C_ONE, C_B64, C_B96, C_RS, C_RQ, C_ID = (i * P for i in range(6))
C_MA = 6 * P
C_MB = C_MA + 512
C_CS = C_MB + 512
C_SS = C_CS + T
C_CQ = C_SS + T
C_SQ = C_CQ + T
C_MN = C_SQ + T
C_MW = C_MN + NB * 32
C_MX = C_MW + 8 * 32
NC_ = C_MX + NB * 32
G_ATT, G_FFN, G_PLE, B_PLE, G_QA, G_KVA, G_Q, G_K, G_QS, G_KS, G_OA, G_OB, G_EPS, NG = (
    0, 8, 16, 24, 32, 38, 40, 41, 42, 43, 44, 48, 52, 53)

W_IN, W_QB = 0, NIN
W_O = W_QB + H
W_GU = W_O + KD
W_DN = W_GU + 2 * KF
W_PL = W_DN + 2 * KD
W_END = W_PL + KD


def build(nc, x, cst, gains, win, wvs, wqb, wk, wv, wkt, wo, wgu, wdn, wpl, plt, pgt, pgk, pgl, ck, cv, pt,
          y, o_lat, o_kr, o_ks, o_vs, o_ck, o_cv):
    with ExitStack() as ctx:
        def sb(name, shape, dt=F32):
            return ctx.enter_context(nc.sbuf_tensor(name, shape, dt))

        def sem(name):
            return ctx.enter_context(nc.semaphore(name))

        hT = sb("hT", [P, KD, T])
        aT = sb("aT", [P, KD, T])
        big = sb("big", [P, (NIN + H) * T])
        uT = big[:, 0:NIN * T].rearrange("p (t n) -> p t n", n=T)
        QT = big[:, NIN * T:].rearrange("p (t n) -> p t n", n=T)
        hid = big[:, 0:KF * T].rearrange("p (t n) -> p t n", n=T)
        plT = big[:, KF * T:(KF + 2) * T].rearrange("p (t n) -> p t n", n=T)
        pgT = big[:, 0:PR * 256].rearrange("p (s n) -> p s n", s=PR)
        pgR = big[:, PR * 256:PR * 384].rearrange("p (s n) -> p s n", s=PR)
        cK = big[:, NIN * T:NIN * T + HP * 896].rearrange("p (c n) -> p c n", c=HP)
        kv1 = sb("kv1", [P, H * T])
        KT = kv1[:, :].rearrange("p (t n) -> p t n", n=T)
        wvS = kv1[:, 0:KD * 512].rearrange("p (k n) -> p k n", k=KD)
        pgL = kv1[:, 0:NPG * KVL].rearrange("p (t n) -> p t n", n=KVL)
        kv2 = sb("kv2", [P, 8 * 512])
        vA = kv2[:, 0:2048].rearrange("p (t n) -> p t n", n=512)
        vB = kv2[:, 2048:4096].rearrange("p (t n) -> p t n", n=512)
        wkT = kv2[0:NOPE, 0:2048].rearrange("p (h n) -> p h n", h=H)
        cVr = kv2[:, 0:2048].rearrange("p (j n) -> p j n", j=4)
        cVs = kv2[0:STR, 2048:4096].rearrange("p (r n) -> p r n", r=4)
        vNew = sb("vNew", [NS, 512])
        latNew = sb("latNew", [NS, KVL])
        ring = sb("ring", [P, RING, SLOT])
        C = sb("C", [P, NC_])
        G = sb("G", [P, NG])
        wK = sb("wK", [P, KC, 512])
        wV = sb("wV", [P, KC, 512])
        sq = sb("sq", [P, 2, T])
        R = sb("R", [P, 2, T])
        tmp = sb("tmp", [P, 2, T])
        att = sb("att", [P, 4, 512])
        pr = att[:, 0:2, :]
        prT = att[:, 2:4, :]
        sqK = att[:, 0:2, :]
        sRaw = att[:, 2:4, :].rearrange("p a (t c) -> p (a t) c", c=64)
        S = sq[:, :, :].rearrange("p a n -> p (a n)")[:, 0:544].rearrange("p (t c) -> p t c", c=32)
        E = sq[:, :, :].rearrange("p a n -> p (a n)")[:, 544:1088].rearrange("p (t c) -> p t c", c=32)
        Rf = R[:, :, :].rearrange("p a n -> p (a n)")
        Sw = Rf[:, 0:288].rearrange("p (t c) -> p t c", c=32)
        Ew = Rf[:, 288:576].rearrange("p (t c) -> p t c", c=32)
        qrAll = Rf[:, 576:832].rearrange("p (b c) -> p b c", b=NB)
        qwAll = Rf[:, 832:1088].rearrange("p (b c) -> p b c", b=NB)
        tf = tmp[:, :, :].rearrange("p a n -> p (a n)")
        qaAll = tf[:, 0:512].rearrange("p (b c) -> p b c", b=NB)
        oAbs = tf[:, 512:1024].rearrange("p (c h n) -> p c h n", c=KC, h=H)
        qa = sb("qa", [P, 64])
        qr = sb("qr", [P, 32])
        qw = sb("qw", [P, 32])
        qg = sb("qg", [NOPE, H, NS])
        ssq = sb("ssq", [P, P])
        rkN = sb("rkN", [NS, H])
        sN = sb("sN", [NS, 32])
        mx = sb("mx", [P, 2, 32])
        mxa = sb("mxa", [P, 2, 32])
        es = sb("es", [P, 2, 32])
        rd = sb("rd", [P, 2, 32])
        st = sb("st", [P, 8])
        ptab = sb("ptab", [1, NB * NPG], I32)

        ps = [ctx.enter_context(nc.psum_tensor(f"ps{i}", [P, 2, 512], F32)) for i in range(4)]

        s_c, s_x, s_g, s_wvs, s_wk, s_wkt, s_plt, s_pt = (sem(n) for n in (
            "const_in", "x_in", "gains_in", "wvs_in", "wkv_in", "wkt_in", "plt_in", "ptab_in"))
        w_in_ = [sem(f"w_in{i}") for i in range(RING)]
        w_used = sem("unit_done")
        n_sq, n_squ, n_rt, n_out, n_rot, n_nc, n_rope = (sem(n) for n in (
            "norm_sq", "norm_summed", "norm_root", "norm_out", "rot_mm", "rope_cos", "rope_out"))
        vs_mm, in_ev, qb_ev, k_mm, k_ev, v_mm, v_ev = (sem(n) for n in (
            "vs_mm", "in_ev", "qb_ev", "k_mm", "k_ev", "v_mm", "v_ev"))
        kr_b, tn_mm, tn_ev, kn_sq, kn_ss = (sem(n) for n in (
            "krope_spread", "latnew_mm", "latnew_ev", "knew_sq", "knew_ssq"))
        a_s, a_sm, a_e, a_p, a_t, a_tc, a_pv, a_o, a_nm = (sem(n) for n in (
            "att_scores", "att_max", "att_exp", "att_probs", "att_turned", "att_turned_sb", "att_pv", "att_out",
            "att_negmax"))
        dve = sem("dve_chain")
        p_set, p_qg, p_ab, p_all = (sem(n) for n in ("prep_zero", "prep_qg", "prep_absorb_mm", "prep_all"))
        q_st, k_raw, k_sq, k_ss, r_used, m_sc, m_cp, w_sc = (sem(n) for n in (
            "queries_staged", "kraw_mm", "kraw_sq", "kraw_ssq", "page_used", "mla_scores", "mla_scores_cp",
            "swa_scores"))
        k_rt, m_mx, m_ar, m_sub, m_e, m_es, m_pv, m_o = (sem(n) for n in (
            "key_root", "mla_max", "mla_allmax", "mla_shifted", "mla_exp", "mla_expsum", "mla_pv", "mla_out"))
        w_mx, w_ar, w_sub, w_e, w_es, w_pv, w_o = (sem(n) for n in (
            "swa_max", "swa_allmax", "swa_shifted", "swa_exp", "swa_expsum", "swa_pv", "swa_out"))
        pg_in = [sem(f"page_in{i}") for i in range(PR)]
        pl_in, ck_in, cv_in = sem("pages_in"), sem("ck_in"), sem("cv_in")
        passed = sem("pool_passed")
        oa_mm, oa_ev = sem("oa_mm"), sem("oa_ev")
        wo_ev, gu_act, pl_act, pl_mul = (sem(n) for n in ("wo_ev", "silu", "ple_gate", "ple_gated"))
        gu_ev, dn_ev, pl_ev = ([sem(f"{n}{j}") for j in range(2)] for n in ("hidden", "down_ev", "ple_ev"))
        out_c, out_s, out_y = sem("copies_out"), sem("states_out"), sem("y_out")

        def cm(off, rows=slice(0, P), n=P):
            return C[rows, off:off + n]

        FULL, LO, MID = slice(0, P), slice(0, HQ), slice(NOPE, HQ)
        groups = []

        def group(tiles, rows, ones, n, gain, w=T, rope=None, dst=None):
            groups.append(dict(src=tiles, dst=dst or tiles, rows=rows, ones=ones, n=n, gain=gain, w=w, rope=rope))
            return len(groups) - 1

        def hcol(buf, k):
            return buf[:, k, :]

        g_x = group([hT[:, k, :] for k in range(KD)], FULL, cm(C_ONE), D, G_ATT, dst=[aT[:, k, :] for k in range(KD)])
        g_cq = group([uT[:, k, :] for k in range(KQ)], FULL, cm(C_ONE), QL, G_QA)
        g_lat = group([uT[:, U_LAT + k, :] for k in range(KC)], FULL, cm(C_ONE), KVL, G_KVA)
        g_kr = group([uT[MID, U_KR, :]], MID, C[MID, C_B96 + NOPE:C_B96 + HQ], ROPE, G_K, rope=(C_RQ, C_CQ, C_SQ))
        g_qs = [group([uT[:, U_QS + i, :]], FULL, cm(C_B64), HD, G_QS, rope=(C_RS, C_CS, C_SS)) for i in range(HP)]
        g_ks = [group([uT[:, U_KS + i, :]], FULL, cm(C_B64), HD, G_KS, rope=(C_RS, C_CS, C_SS)) for i in range(HP)]
        g_qh = [group([QT[LO, h, :]], LO, C[LO, C_B96:C_B96 + HQ], None, G_Q, rope=(C_RQ, C_CQ, C_SQ)) for h in range(H)]
        LOW = slice(0, NOPE)
        g_kh = [group([KT[LOW, h, 0:NP_]], LOW, C[LOW, C_B96:C_B96 + NOPE], NOPE, G_K, w=NP_) for h in range(H)]
        g_oa = group([aT[:, k, :] for k in range(HP)], FULL, cm(C_ONE), H * HD, G_OA)
        g_ob = group([aT[:, HP + k, :] for k in range(HP)], FULL, cm(C_ONE), H * HD, G_OB)
        g_f = group([hT[:, k, :] for k in range(KD)], FULL, cm(C_ONE), D, G_FFN, dst=[aT[:, k, :] for k in range(KD)])
        g_p = group([hT[:, k, :] for k in range(KD)], FULL, cm(C_ONE), D, G_PLE, dst=[aT[:, k, :] for k in range(KD)])
        tiles_before = [sum(len(g["src"]) for g in groups[:i]) for i in range(len(groups) + 1)]
        ropes_before = [sum(g["rope"] is not None for g in groups[:i]) for i in range(len(groups) + 1)]

        def norm_squares(g):
            q = groups[g]
            rows, w = q["rows"], q["w"]
            for j, src in enumerate(q["src"]):
                k = tiles_before[g] + j
                if k >= 2:
                    nc.scalar.wait_ge(n_squ, k - 1)
                nc.scalar.activation(sq[rows, k % 2, 0:w], src, ACT.Square).then_inc(n_sq, 1)

        def norm_root(g):
            q = groups[g]
            rows, w = q["rows"], q["w"]
            nc.scalar.wait_ge(n_squ, tiles_before[g + 1])
            if g >= 2:
                nc.scalar.wait_ge(n_out, g - 1)
            scale = 1.0 / q["n"] if rows == FULL else 1.0
            nc.scalar.activation(R[rows, g % 2, 0:w].rearrange("p (a n) -> p a n", a=2),
                                 ps[2 + g % 2][rows, :, 0:w // 2], ACT.Sqrt, scale=scale,
                                 bias=G[rows, G_EPS:G_EPS + 1]).then_inc(n_rt, 1)

        def act_norms(gs):
            norm_squares(gs[0])
            for i, g in enumerate(gs):
                if i + 1 < len(gs):
                    norm_squares(gs[i + 1])
                norm_root(g)

        def pe_norm(g):
            q = groups[g]
            rows, hw = q["rows"], q["w"] // 2
            if g >= 2:
                nc.tensor.wait_ge(n_rt, g - 1)
            for j in range(len(q["src"])):
                k = tiles_before[g] + j
                nc.tensor.wait_ge(n_sq, k + 1)
                for a in range(2):
                    last = nc.tensor.matmul(ps[2 + g % 2][rows, a, 0:hw], q["ones"], sq[rows, k % 2, a * hw:(a + 1) * hw],
                                            start=(j == 0), stop=(j == len(q["src"]) - 1))
                last.then_inc(n_squ, 1)

        def pe_rot(g):
            q = groups[g]
            rows, w, i = q["rows"], q["w"], ropes_before[g]
            nc.tensor.wait_ge(n_out, g + 1)
            if i >= 1:
                nc.tensor.wait_ge(n_rope, i)
            for a in range(2):
                last = nc.tensor.matmul(ps[1][rows, a, 0:HT], C[rows, q["rope"][0] + rows.start:q["rope"][0] + rows.stop],
                                        q["dst"][0][:, a * HT:(a + 1) * HT], start=True, stop=True)
            last.then_inc(n_rot, 1)

        def pe_norms(gs):
            for i, g in enumerate(gs):
                pe_norm(g)
                if i and groups[gs[i - 1]]["rope"]:
                    pe_rot(gs[i - 1])
            if groups[gs[-1]]["rope"]:
                pe_rot(gs[-1])

        def pool_cos(g):
            q = groups[g]
            rows, i = q["rows"], ropes_before[g]
            nc.gpsimd.wait_ge(n_out, g + 1)
            if i >= 1:
                nc.gpsimd.wait_ge(n_rope, i)
            nc.gpsimd.tensor_tensor(tmp[rows, 0, :], q["dst"][0], C[rows, q["rope"][1]:q["rope"][1] + T],
                                    ALU.mult).then_inc(n_nc, 1)

        chain = dict(base=0, n=0)

        def link(ins):
            chain["n"] += 1
            ins.then_inc(dve, 1)
            nc.vector.wait_ge(dve, chain["base"] + chain["n"])

        def dve_scale(g):
            q = groups[g]
            rows, w = q["rows"], q["w"]
            nc.vector.wait_ge(n_rt, g + 1)
            link(nc.vector.reciprocal(R[rows, g % 2, 0:w], R[rows, g % 2, 0:w]))
            for j, (src, dst) in enumerate(zip(q["src"], q["dst"])):
                gc = q["gain"] + (j if len(q["src"]) > 1 else 0)
                last = nc.vector.scalar_tensor_tensor(out=dst, in0=src, scalar=G[rows, gc:gc + 1], in1=R[rows, g % 2, 0:w],
                                                      op0=ALU.mult, op1=ALU.mult)
            last.then_inc(n_out, 1)

        def dve_rope(g):
            q = groups[g]
            rows, i = q["rows"], ropes_before[g]
            nc.vector.wait_ge(n_rot, i + 1)
            link(nc.vector.tensor_tensor(tmp[rows, 1, :].rearrange("p (a n) -> p a n", a=2), ps[1][rows, :, 0:HT],
                                         C[rows, q["rope"][2]:q["rope"][2] + T].rearrange("p (a n) -> p a n", a=2),
                                         ALU.mult))
            nc.vector.wait_ge(n_nc, i + 1)
            nc.vector.tensor_tensor(q["dst"][0], tmp[rows, 0, :], tmp[rows, 1, :], ALU.add).then_inc(n_rope, 1)

        def dve_norms(gs):
            for i, g in enumerate(gs):
                dve_scale(g)
                if i and groups[gs[i - 1]]["rope"]:
                    dve_rope(gs[i - 1])
            if groups[gs[-1]]["rope"]:
                dve_rope(gs[-1])

        RUN1 = [g_cq, g_lat, g_kr]
        RUN2 = g_qs + g_ks
        RUN3 = g_qh + g_kh

        def pe_weight(u, i=None, per=0):
            n = 16 * (u // RING + 1)
            nc.tensor.wait_ge(w_in_[u % RING], n if i is None else n + i * (16 * per // RING))
            return ring[:, u % RING, :]

        def sp_weight(u, src):
            if u >= RING:
                nc.sync.wait_ge(w_used, u - RING + 1)
            nc.sync.dma_start(ring[:, u % RING, 0:src.shape[-1]], src).then_inc(w_in_[u % RING], 16)

        def sp_weight_loop(u0, n, src):
            with nc.sync.Fori(0, n // RING) as i:
                for j in range(RING):
                    nc.sync.wait_ge(w_used, i * RING + (u0 + j - RING + 1))
                    nc.sync.dma_start(ring[:, (u0 + j) % RING, 0:src.shape[-1]],
                                      src[bass.ds(i * RING + j, 1), :, :].rearrange("a p n -> p (a n)")
                                      ).then_inc(w_in_[(u0 + j) % RING], 16)

        units = [(h, i) for h in range(2 * H) for i in range(4)]

        def heads(h):
            if h < H:
                return QT[LO, h, :], KT[LO, h, :], vA
            r = slice((h % 2) * HD, (h % 2) * HD + HD)
            c = (h - H) // 2
            return uT[r, U_QS + c, :], uT[r, U_KS + c, :], vB

        block = ctx.enter_context(nc.Block())

        @block.sync
        def _(sp):
            sp.dma_start(hT[:, :, :], x).then_inc(s_x, 16)
            sp.dma_start(G[:, :], gains).then_inc(s_g, 16)
            sp.dma_start(C[:, :], cst).then_inc(s_c, 16)
            for u in range(RING):
                sp_weight(W_IN + u, win[u])
            sp.dma_start(wvS, wvs).then_inc(s_wvs, 16)
            sp.dma_start(wK[:, :, :], wk).then_inc(s_wk, 16)
            sp.dma_start(wV[:, :, :], wv).then_inc(s_wk, 16)
            sp.dma_start(ptab[:, :], pt).then_inc(s_pt, 16)
            for u in range(RING, NIN):
                sp_weight(W_IN + u, win[u])
            for u in range(H):
                sp_weight(W_QB + u, wqb[u])
            for u in range(RING):
                sp_weight(W_O + u, wo[u])
            sp.wait_ge(a_o, H)
            sp.dma_start(wkT, wkt).then_inc(s_wkt, 16)
            sp.wait_ge(s_pt, 16)
            with sp.Fori(0, NB) as b:
                page = []

                def load_page_T(t):
                    src = bass.ds(page[t], 1)
                    sp.dma_start(pgT[:, t % PR, :], pgt[src, :, :].rearrange("a p n -> p (a n)")).then_inc(pg_in[t % PR], 16)
                    sp.dma_start(pgR[MID, t % PR, :], pgk[src, :, :].rearrange("a p n -> p (a n)")).then_inc(pg_in[t % PR], 16)

                sp.wait_ge(m_sc, b)
                for t in range(NPG):
                    page.append(sp.value_load(ptab[0:1, bass.ds(b * NPG + t, 1)], min_val=0, max_val=POOL - 1))
                for t in range(PR):
                    load_page_T(t)
                sp.wait_ge(m_pv, b)
                for t in range(NPG):
                    sp.dma_start(pgL[:, t, :], pgl[bass.ds(page[t], 1), :, :].rearrange("a p n -> p (a n)")).then_inc(pl_in, 16)
                for t in range(PR, NPG):
                    sp.wait_ge(r_used, b * NPG + (t - PR + 1))
                    load_page_T(t)
                sp.wait_ge(w_pv, b)
                sp.wait_ge(out_s, 80)
                sp.wait_ge(p_all, 1)
                sp.dma_start(cK, ck[bass.ds(b, 1), :, :, PAST - 896:PAST].rearrange("a c p n -> p (a c) n")).then_inc(ck_in, 16)
                sp.dma_start(cVr, cv[bass.ds(b, 1), PAST - REC:PAST, :].rearrange("a (j p) n -> p (a j) n", p=P)).then_inc(cv_in, 16)
                sp.dma_start(cVs, cv[bass.ds(b, 1), 0:PAST - REC, :].rearrange("a (g r) n -> g (a r) n", r=16)[:, 0:4, :]).then_inc(cv_in, 16)
            for u in range(RING, KD):
                sp_weight(W_O + u, wo[u])
            sp.wait_ge(w_pv, NB)
            sp.dma_start(plT, plt).then_inc(s_plt, 16)
            sp_weight_loop(W_GU, 2 * KF, wgu)
            sp_weight_loop(W_DN, 2 * KD, wdn)
            sp_weight_loop(W_PL, KD, wpl)
            for m in range(KD):
                sp.wait_ge(pl_ev[m % 2], m // 2 + 1)
                sp.dma_start(y[m], hT[:, m, :]).then_inc(out_y, 16)
            sp.wait_ge(out_y, 16 * KD)

        @block.gpsimd
        def _(pool):
            for b in range(NB):
                pool.dma_start(o_ck[b].rearrange("c p n -> (c p n)").rearrange("(a n) -> a n", a=64),
                               ck[b].rearrange("c p n -> (c p n)").rearrange("(a n) -> a n", a=64)).then_inc(out_c, 16)
                pool.dma_start(o_cv[b, 0:PAST - NQ, :], cv[b, NQ:PAST, :]).then_inc(out_c, 16)
            pool.wait_ge(s_c, 16)
            pool_cos(g_kr)
            for g in RUN2:
                pool_cos(g)
            for g in g_qh:
                pool_cos(g)
            pool.wait_ge(n_rope, 1 + len(RUN2))
            pool.dma_start(o_lat, uT[:, U_LAT:U_LAT + KC, :]).then_inc(out_s, 16)
            pool.dma_start(o_kr, uT[MID, U_KR, :]).then_inc(out_s, 16)
            pool.dma_start(o_ks, uT[:, U_KS:U_KS + HP, :]).then_inc(out_s, 16)
            pool.wait_ge(in_ev, NIN + 5)
            pool.dma_start(o_vs.rearrange("(t p) n -> p t n", p=P), vB).then_inc(out_s, 16)
            pool.dma_start(o_cv[:, PAST - NQ:PAST, :].rearrange("b q n -> b (q n)"),
                           vNew[:, :]).then_inc(out_s, 16)
            pool.wait_ge(out_s, 80)
            pool.wait_ge(p_all, 1)
            with pool.Fori(0, NB) as b:
                pool.wait_ge(w_sc, b)
                pool.tensor_copy(qa[:, :], qaAll[:, bass.ds(b, 1), :].rearrange("p a n -> p (a n)")).then_inc(q_st, 1)
                pool.wait_ge(q_st, b * 3 + 1)
                pool.tensor_copy(qr[MID, :], qrAll[MID, bass.ds(b, 1), :].rearrange("p a n -> p (a n)")).then_inc(q_st, 1)
                pool.wait_ge(q_st, b * 3 + 2)
                pool.tensor_copy(qw[:, :], qwAll[:, bass.ds(b, 1), :].rearrange("p a n -> p (a n)")).then_inc(q_st, 1)
                pool.wait_ge(q_st, b * 3 + 3)
                pool.wait_ge(m_mx, b + 1)
                pool.sem_inc(passed, 1)
                pool.partition_all_reduce(mxa[:, 0, :], mx[:, 0, :], P, MAX_ALL).then_inc(m_ar, 1)
                pool.wait_ge(m_ar, b + 1)
                pool.wait_ge(w_mx, b + 1)
                pool.sem_inc(passed, 1)
                pool.partition_all_reduce(mxa[:, 1, :], mx[:, 1, :], P, MAX_ALL).then_inc(w_ar, 1)
            pool.wait_ge(out_c, 32 * NB)

        @block.scalar
        def _(act):
            act.wait_ge(s_x, 16)
            act.wait_ge(s_g, 16)
            act.wait_ge(s_c, 16)
            act_norms([g_x])

            def in_copy(m):
                if m < NIN:
                    act.wait_ge(w_used, W_IN + m + 1)
                else:
                    act.wait_ge(vs_mm, m - NIN + 1)
                if m < NIN:
                    rows = MID if m == U_KR else FULL
                    act.activation(uT[rows, m, :].rearrange("p (a n) -> p a n", a=2), ps[m % 2][rows, :, 0:HT],
                                   ACT.Copy).then_inc(in_ev, 1)
                elif m < NIN + 4:
                    act.activation(vB[:, m - NIN, :], ps[m % 2][:, 0, :], ACT.Copy).then_inc(in_ev, 1)
                else:
                    act.activation(vNew[:, :], ps[m % 2][0:NS, 0, :], ACT.Copy).then_inc(in_ev, 1)

            for m in range(U_QS):
                in_copy(m)
            act.wait_ge(in_ev, U_QS)
            act_norms(RUN1)
            for m in range(U_QS, NIN + 5):
                in_copy(m)
            act.wait_ge(in_ev, NIN + 5)
            act_norms(RUN2)
            for h in range(H):
                act.wait_ge(w_used, W_QB + h + 1)
                act.activation(QT[LO, h, :].rearrange("p (a n) -> p a n", a=2), ps[(NIN + 5 + h) % 2 * 3][LO, :, 0:HT],
                               ACT.Copy).then_inc(qb_ev, 1)
            for h in range(H):
                act.wait_ge(k_mm, h + 1)
                act.activation(KT[LOW, h, 0:NP_], ps[0][LOW, h % 2, :], ACT.Copy).then_inc(k_ev, 1)
            for t in range(4):
                act.wait_ge(v_mm, t + 1)
                act.activation(vA[:, t, :], ps[0][:, t % 2, :], ACT.Copy).then_inc(v_ev, 1)
            act.wait_ge(v_mm, 5)
            act.wait_ge(n_rope, ropes_before[RUN2[-1] + 1])
            act.activation(tmp[0:NS, 0, 0:512], ps[0][0:NS, 0, :], ACT.Square).then_inc(kn_sq, 1)
            act.wait_ge(tn_mm, 1)
            act.activation(latNew[:, :], ps[0][0:NS, 1, 0:KVL], ACT.Copy).then_inc(tn_ev, 1)
            act.wait_ge(k_ev, H)
            act.wait_ge(qb_ev, H)
            act_norms(RUN3)
            act.wait_ge(kn_ss, 1)
            act.activation(rkN[:, :], rkN[:, :], ACT.Sqrt, scale=1.0 / NOPE, bias=G[0:NS, G_EPS:G_EPS + 1]).then_inc(k_rt, 1)

            for n in range(len(units) + 2):
                if n < len(units):
                    w = (units[n][1] + 1) * P
                    act.wait_ge(a_nm, n + 1)
                    act.activation(pr[:, n % 2, 0:w], pr[:, n % 2, 0:w], ACT.Exp, bias=st[:, n % 2:n % 2 + 1],
                                   accum_out=st[:, 2 + n % 2:3 + n % 2]).then_inc(a_e, 1)
                if n >= 1 and n - 1 < len(units):
                    m = n - 1
                    w = (units[m][1] + 1) * P
                    act.wait_ge(a_t, m + 1)
                    if m >= 2:
                        act.wait_ge(a_pv, m - 1)
                    act.activation(prT[:, m % 2, 0:w], ps[1][:, m % 2, 0:w], ACT.Copy).then_inc(a_tc, 1)

            with act.Fori(0, NB) as b:
                for t in range(NPG):
                    act.wait_ge(k_raw, b * NPG + (t + 1))
                    if t >= 2:
                        act.wait_ge(k_ss, b * NPG + (t - 1))
                    else:
                        act.wait_ge(k_ss, b * NPG)
                    act.activation(sqK[:, t % 2, :], ps[0][:, t % 2, :], ACT.Square).then_inc(k_sq, 1)
                act.wait_ge(k_ss, b * NPG + NPG)
                act.activation(ssq[:, :], ssq[:, :], ACT.Sqrt, scale=1.0 / NOPE, bias=G[:, G_EPS:G_EPS + 1]).then_inc(k_rt, 1)
                act.wait_ge(m_sub, b + 1)
                act.activation(E, S, ACT.Exp, scale=SC_A).then_inc(m_e, 1)
                act.wait_ge(w_sub, b + 1)
                act.activation(Ew, Sw, ACT.Exp, scale=SC_B).then_inc(w_e, 1)
            act.wait_ge(oa_mm, 1)
            act.activation(aT[:, 0:HP, NP_:T], ps[0][:, 0, 0:HP * NS].rearrange("p (c n) -> p c n", c=HP), ACT.Copy).then_inc(oa_ev, 1)
            act.wait_ge(oa_ev, 1)
            act.wait_ge(w_o, NB)
            act_norms([g_oa, g_ob])
            act.wait_ge(wo_ev, KD)
            act_norms([g_f])
            with act.Fori(0, KF // 2) as i:
                for j in range(2):
                    act.wait_ge(w_used, i * 4 + (W_GU + 2 * j + 2))
                    act.wait_ge(gu_ev[j], i)
                    act.activation(tmp[:, j, :].rearrange("p (a n) -> p a n", a=2), ps[2 * j][:, :, 0:HT],
                                   ACT.Silu).then_inc(gu_act, 1)
            for j in range(2):
                act.wait_ge(dn_ev[j], KD // 2)
            act_norms([g_p])
            with act.Fori(0, KD // 4) as i:
                for j in range(4):
                    act.wait_ge(w_used, i * 4 + (W_PL + j + 1))
                    act.wait_ge(pl_ev[j % 2], i * 2 + j // 2)
                    act.activation(tmp[:, j % 2, :].rearrange("p (a n) -> p a n", a=2), ps[2 * (j % 2)][:, :, 0:HT],
                                   ACT.Sigmoid, bias=G[:, bass.ds(i * 4 + (B_PLE + j), 1)]).then_inc(pl_act, 1)

        @block.tensor
        def _(pe):
            mm = nc.tensor.matmul
            pe.wait_ge(s_c, 16)
            pe_norms([g_x])
            pe.wait_ge(n_out, 1)

            def in_tile(m):
                if m >= 2:
                    pe.wait_ge(in_ev, m - 1)
                if m < NIN:
                    w = pe_weight(W_IN + m)
                    cols, rows = (HQ, LO) if m == U_KR else (P, FULL)
                    for k in range(KD):
                        for a in range(2):
                            last = mm(ps[m % 2][rows, a, 0:HT], w[:, k * P:k * P + cols], aT[:, k, a * HT:(a + 1) * HT],
                                      start=(k == 0), stop=(k == KD - 1))
                    last.then_inc(w_used, 1)
                else:
                    t = m - NIN
                    n = P if t < 4 else NS
                    if t == 0:
                        pe.wait_ge(s_wvs, 16)
                    for k in range(KD):
                        last = mm(ps[m % 2][0:n, 0, :], aT[:, k, t * P:t * P + n], wvS[:, k, :], start=(k == 0), stop=(k == KD - 1))
                    last.then_inc(vs_mm, 1)

            for m in range(U_QS):
                in_tile(m)
            for g in RUN1:
                pe_norm(g)
            for m in range(U_QS, NIN + 5):
                in_tile(m)
            pe.wait_ge(in_ev, NIN + 5)
            pe_rot(g_kr)
            pe_norms(RUN2)
            for h in range(H):
                bank = ps[(NIN + 5 + h) % 2 * 3]
                if h >= 2:
                    pe.wait_ge(qb_ev, h - 1)
                elif h == 1:
                    pe.wait_ge(n_rt, RUN2[-1] + 1)
                w = pe_weight(W_QB + h)
                for k in range(KQ):
                    for a in range(2):
                        last = mm(bank[LO, a, 0:HT], w[:, k * HQ:(k + 1) * HQ], uT[:, U_CQ + k, a * HT:(a + 1) * HT],
                                  start=(k == 0), stop=(k == KQ - 1))
                last.then_inc(w_used, 1)
            pe.wait_ge(s_wk, 32)
            pe.wait_ge(qb_ev, H)
            for h in range(H):
                if h >= 2:
                    pe.wait_ge(k_ev, h - 1)
                for k in range(KC):
                    last = mm(ps[0][LOW, h % 2, :], wK[:, k, h * NOPE:(h + 1) * NOPE], uT[:, U_LAT + k, 0:NP_],
                              start=(k == 0), stop=(k == KC - 1))
                last.then_inc(k_mm, 1)
            for t in range(5):
                pe.wait_ge(k_ev, H) if t < 2 else pe.wait_ge(v_ev, t - 1)
                n = P if t < 4 else NS
                for k in range(KC):
                    last = mm(ps[0][0:n, t % 2, :], uT[:, U_LAT + k, t * P:t * P + n], (wV if t < 4 else wK)[:, k, :],
                              start=(k == 0), stop=(k == KC - 1))
                last.then_inc(v_mm, 1)
            pe.wait_ge(v_ev, 4)
            for k in range(KC):
                last = pe.transpose(ps[0][0:NS, 1, k * P:(k + 1) * P], uT[:, U_LAT + k, NP_:T], cm(C_ID))
            last.then_inc(tn_mm, 1)
            pe_norms(RUN3)

            pe.wait_ge(kr_b, 1)
            pe.wait_ge(n_rope, ropes_before[-1])
            pe.wait_ge(n_out, g_kh[-1] + 1)
            pe.wait_ge(tn_ev, 1)
            pe.wait_ge(kn_sq, 1)
            for n in range(len(units) + 2):
                if n < len(units):
                    h, i = units[n]
                    q, k, _v = heads(h)
                    if n >= 2:
                        pe.wait_ge(a_sm, n - 1)
                    mm(ps[0][:, n % 2, 0:(i + 1) * P], q[:, i * P:(i + 1) * P], k[:, 0:(i + 1) * P],
                       start=True, stop=True).then_inc(a_s, 1)
                if n >= 1 and n - 1 < len(units):
                    m = n - 1
                    h, i = units[m]
                    pe.wait_ge(a_p, m + 1)
                    if m >= 2:
                        pe.wait_ge(a_tc, m - 1)
                    for j in range(i + 1):
                        last = pe.transpose(ps[1][:, m % 2, j * P:(j + 1) * P], pr[:, m % 2, j * P:(j + 1) * P], cm(C_ID))
                    last.then_inc(a_t, 1)
                if n >= 2:
                    m = n - 2
                    h, i = units[m]
                    _q, _k, v = heads(h)
                    pe.wait_ge(a_tc, m + 1)
                    if i == 0 and h % 2 == 0 and h >= 4:
                        pe.wait_ge(a_o, h // 2 - 1)
                    r = slice((h % 2) * HD, (h % 2) * HD + HD)
                    for j in range(i + 1):
                        last = mm(ps[2][r, (h // 2) % 2, i * P:(i + 1) * P], v[:, j, (h % H) * HD:(h % H + 1) * HD],
                                  prT[:, m % 2, j * P:(j + 1) * P], start=(j == 0), stop=(j == i))
                    last.then_inc(a_pv, 1)

            pe.wait_ge(s_wkt, 16)
            pe.wait_ge(p_qg, 1)
            for c in range(KC):
                for h in range(H):
                    o = (c * H + h) * NS
                    last = mm(ps[3][:, 0, o:o + NS], wkT[:, h, c * P:(c + 1) * P], qg[:, h, :], start=True, stop=True)
            last.then_inc(p_ab, 1)
            pe.wait_ge(a_o, H)
            pe.wait_ge(p_all, 1)

            with pe.Fori(0, NB) as b:
                pe.wait_ge(q_st, b * 3 + 3)
                for t in range(NPG + 1):
                    new = t == NPG
                    grp = t // 4
                    n = NS if new else P
                    if not new:
                        pe.wait_ge(pg_in[t % PR], b * 64 + (32 if t < PR else 64))
                        if t < 2:
                            pe.wait_ge(k_sq, b * NPG)
                        else:
                            pe.wait_ge(k_sq, b * NPG + (t - 1))
                        for c in range(KC):
                            last = mm(ps[0][:, t % 2, :], pgT[:, t % PR, c * P:(c + 1) * P], wK[:, c, :],
                                      start=(c == 0), stop=(c == KC - 1))
                        last.then_inc(k_raw, 1)
                    if t % 4 == 0:
                        pe.wait_ge(m_cp, b * 5 + max(grp - 1, 0))
                    o = (t % 4) * 64
                    bank = ps[1][0:n, grp % 2, :]
                    for c in range(KC):
                        lhs = uT[:, U_LAT + c, NP_:T] if new else pgT[:, t % PR, c * P:(c + 1) * P]
                        mm(bank[:, o:o + 32], lhs, qa[:, c * 32:(c + 1) * 32], start=(c == 0), stop=(c == KC - 1))
                    lhs = uT[MID, U_KR, NP_:T] if new else pgR[MID, t % PR, :]
                    last = mm(bank[:, o + 32:o + 64], lhs, qr[MID, :], start=True, stop=True)
                    if not new:
                        last.then_inc(r_used, 1)
                    else:
                        last.then_inc(m_sc, 1)
                pe.wait_ge(ck_in, b * 16 + 16)
                pe.wait_ge(w_o, b)
                for t in range(NT_W):
                    for c in range(HP):
                        if t < 8:
                            lo = t * STR if t < 4 else 4 * STR + (t - 4) * P
                            lhs, n = cK[:, c, lo:lo + P], P
                        else:
                            lhs, n = uT[:, U_KS + c, NP_:T], NS
                        last = mm(ps[2][0:n, 0, t * 32 + c * 8:t * 32 + c * 8 + 8], lhs, qw[:, c * 8:c * 8 + 8], start=True, stop=True)
                last.then_inc(w_sc, 1)
                pe.wait_ge(pl_in, b * (16 * NPG) + 16 * NPG)
                pe.wait_ge(m_es, b + 1)
                for c in range(KC):
                    for t in range(NPG + 1):
                        lhs, rhs = (pgL[:, t, c * P:(c + 1) * P], E[:, t, :]) if t < NPG else (
                            latNew[:, c * P:(c + 1) * P], E[0:NS, t, :])
                        mm(ps[3][:, 0, c * 32:(c + 1) * 32], lhs, rhs, start=(t == 0), stop=(t == NPG))
                mm(ps[3][:, 0, 64:96], cm(C_ONE), es[:, 0, :], start=True, stop=True).then_inc(m_pv, 1)
                pe.wait_ge(cv_in, b * 32 + 32)
                pe.wait_ge(w_es, b + 1)
                for c in range(HP):
                    for t in range(NT_W):
                        cs = slice(c * P, (c + 1) * P)
                        if t < 4:
                            lhs, rhs = cVs[:, t, cs], Ew[0:STR, t, :]
                        elif t < 8:
                            lhs, rhs = cVr[:, t - 4, cs], Ew[:, t, :]
                        else:
                            lhs, rhs = vNew[:, cs], Ew[0:NS, t, :]
                        mm(ps[3][:, 1, c * 32:(c + 1) * 32], lhs, rhs, start=(t == 0), stop=(t == NT_W - 1))
                mm(ps[3][:, 1, 128:160], cm(C_ONE), es[:, 1, :], start=True, stop=True).then_inc(w_pv, 1)

            pe.wait_ge(m_o, 2 * NB)
            for h in range(H):
                r = slice((h % 2) * HD, (h % 2) * HD + HD)
                for c in range(KC):
                    last = mm(ps[0][r, 0, (h // 2) * NS:(h // 2 + 1) * NS], wV[:, c, h * HD:(h + 1) * HD], oAbs[:, c, h, :],
                              start=(c == 0), stop=(c == KC - 1))
            last.then_inc(oa_mm, 1)
            pe_norms([g_oa, g_ob])
            pe.wait_ge(n_out, g_ob + 1)

            for m in range(KD):
                w = pe_weight(W_O + m)
                if m >= 2:
                    pe.wait_ge(wo_ev, m - 1)
                for k in range(KD):
                    for a in range(2):
                        last = mm(ps[m % 2][:, a, 0:HT], w[:, k * P:(k + 1) * P], aT[:, k, a * HT:(a + 1) * HT],
                                  start=(k == 0), stop=(k == KD - 1))
                last.then_inc(w_used, 1)
            pe_norms([g_f])
            pe.wait_ge(n_out, g_f + 1)
            with pe.Fori(0, KF // 2) as i:
                for j in range(2):
                    pe.wait_ge(gu_ev[j], i)
                    for z in range(2):
                        w = pe_weight(W_GU + 2 * j + z, i, 4)
                        for k in range(KD):
                            for a in range(2):
                                last = mm(ps[2 * j + z][:, a, 0:HT], w[:, k * P:(k + 1) * P], aT[:, k, a * HT:(a + 1) * HT],
                                          start=(k == 0), stop=(k == KD - 1))
                        last.then_inc(w_used, 1)
            for j in range(2):
                pe.wait_ge(gu_ev[j], KF // 2)
            with pe.Fori(0, KD // 2) as i:
                for j in range(2):
                    pe.wait_ge(dn_ev[j], i)
                    for z in range(2):
                        w = pe_weight(W_DN + 2 * j + z, i, 4)
                        for k in range(11):
                            kk = 11 * z + k
                            for a in range(2):
                                last = mm(ps[j][:, a, 0:HT], w[:, k * P:(k + 1) * P], hid[:, kk, a * HT:(a + 1) * HT],
                                          start=(kk == 0), stop=(kk == KF - 1))
                        last.then_inc(w_used, 1)
            pe_norms([g_p])
            pe.wait_ge(n_out, g_p + 1)
            pe.wait_ge(s_plt, 16)
            with pe.Fori(0, KD // 4) as i:
                for j in range(4):
                    w = pe_weight(W_PL + j, i, 4)
                    pe.wait_ge(pl_ev[j % 2], i * 2 + j // 2)
                    for k in range(KD):
                        for a in range(2):
                            mm(ps[2 * (j % 2)][:, a, 0:HT], w[:, k * P:(k + 1) * P], aT[:, k, a * HT:(a + 1) * HT],
                               start=(k == 0), stop=(k == KD - 1))
                    for k in range(2):
                        for a in range(2):
                            last = mm(ps[2 * (j % 2) + 1][:, a, 0:HT], w[:, (KD + k) * P:(KD + k + 1) * P],
                                      plT[:, k, a * HT:(a + 1) * HT], start=(k == 0), stop=(k == 1))
                    last.then_inc(w_used, 1)

        @block.vector
        def _(v):
            v.wait_ge(s_x, 16)
            v.wait_ge(s_g, 16)
            v.wait_ge(s_c, 16)
            dve_norms([g_x])
            v.wait_ge(in_ev, U_QS)
            for g in RUN1[:-1]:
                dve_scale(g)
            dve_scale(g_kr)
            v.wait_ge(in_ev, NIN + 5)
            dve_rope(g_kr)
            dve_norms(RUN2)
            v.wait_ge(n_rope, 1)
            v.wait_ge(s_wvs, 16)
            v.wait_ge(vs_mm, 5)
            v.tensor_copy(KT[MID, :, 0:NP_], uT[MID, U_KR:U_KR + 1, 0:NP_].broadcast_to([ROPE, H, NP_])).then_inc(kr_b, 1)
            v.wait_ge(kn_sq, 1)
            v.tensor_reduce(rkN[:, :], tmp[0:NS, 0, 0:512].rearrange("p (h d) -> p h d", h=H), AX.X, ALU.add).then_inc(kn_ss, 1)
            v.wait_ge(qb_ev, H)
            v.wait_ge(k_ev, H)
            dve_norms(RUN3)
            v.wait_ge(k_rt, 1)
            link(v.reciprocal(rkN[:, :], rkN[:, :]))
            for n in range(len(units) + 2):
                if n < len(units):
                    h, i = units[n]
                    w = (i + 1) * P
                    mask = (C_MA if h < H else C_MB) + (3 - i) * P
                    v.wait_ge(a_s, n + 1)
                    if n >= 2:
                        v.wait_ge(a_t, n - 1)
                    v.tensor_tensor_reduce(pr[:, n % 2, 0:w], ps[0][:, n % 2, 0:w], C[:, mask:mask + w],
                                           SC_A if h < H else SC_B, NEG * 4, ALU.add, ALU.max,
                                           st[:, 4 + n % 2:5 + n % 2]).then_inc(a_sm, 1)
                    v.wait_ge(a_sm, n + 1)
                    v.tensor_scalar(st[:, n % 2:n % 2 + 1], st[:, 4 + n % 2:5 + n % 2], -1.0, None, ALU.mult).then_inc(a_nm, 1)
                if n >= 1 and n - 1 < len(units):
                    m = n - 1
                    w = (units[m][1] + 1) * P
                    v.wait_ge(a_e, m + 1)
                    link(v.reciprocal(st[:, 6 + m % 2:7 + m % 2], st[:, 2 + m % 2:3 + m % 2]))
                    v.tensor_scalar(pr[:, m % 2, 0:w], pr[:, m % 2, 0:w], st[:, 6 + m % 2:7 + m % 2], None, ALU.mult).then_inc(a_p, 1)
                if n >= 2:
                    h, i = units[n - 2]
                    if i == 3 and h % 2 == 1:
                        c = h // 2
                        v.wait_ge(a_pv, n - 1)
                        v.tensor_copy(aT[:, c, 0:NP_], ps[2][:, c % 2, :]).then_inc(a_o, 1)
            v.wait_ge(n_rope, ropes_before[-1])
            v.tensor_scalar(qg[:, :, :], QT[LOW, :, NP_:T], G[LOW, G_K:G_K + 1], None, ALU.mult).then_inc(p_qg, 1)
            link(v.memset(S, NEG))
            link(v.memset(Sw, NEG))
            link(v.memset(qwAll, 0.0))
            link(v.tensor_copy(qrAll[MID, :, :].rearrange("p b (h q) -> p h b q", h=H),
                               QT[MID, :, NP_:T].rearrange("p h (b q) -> p h b q", q=NQ)))
            for z in range(2):
                r = slice(z * HD, (z + 1) * HD)
                link(v.tensor_copy(qwAll[r, :, :].rearrange("p b (c z q) -> p c z b q", c=HP, z=2)[:, :, z],
                                   uT[r, U_QS:U_QS + HP, NP_:T].rearrange("p c (b q) -> p c b q", q=NQ)))
            v.wait_ge(p_ab, 1)
            v.tensor_copy(qaAll.rearrange("p b (c q) -> p c b q", q=NQ),
                          ps[3][:, 0, :].rearrange("p (c b q) -> p c b q", b=NB, q=NQ)).then_inc(p_all, 1)

            before = chain["n"]
            with v.Fori(0, NB) as b:
                chain["base"], chain["n"] = b * LOOP_LINKS + before, 0
                for t in range(NPG):
                    v.wait_ge(k_sq, b * NPG + (t + 1))
                    v.tensor_reduce(ssq[:, t * H:(t + 1) * H], sqK[:, t % 2, :].rearrange("p (h d) -> p h d", h=H), AX.X,
                                    ALU.add).then_inc(k_ss, 1)
                    if t % 4 == 3:
                        g = t // 4
                        v.wait_ge(r_used, b * NPG + (t + 1))
                        v.tensor_copy(sRaw[:, 4 * g:4 * g + 4, :], ps[1][:, g % 2, 0:256].rearrange("p (t c) -> p t c", c=64)).then_inc(m_cp, 1)
                v.wait_ge(m_sc, b + 1)
                link(v.tensor_tensor(sN[:, :].rearrange("p (h q) -> p h q", q=NQ),
                                     ps[1][0:NS, 0, 0:32].rearrange("p (h q) -> p h q", q=NQ),
                                     rkN[:, :].unsqueeze(2).broadcast_to([NS, H, NQ]), ALU.mult))
                link(v.tensor_tensor(sN[:, :], ps[1][0:NS, 0, 32:64], sN[:, :], ALU.add))
                v.tensor_tensor(S[0:NS, NPG, :], sN[:, :], C[0:NS, bass.ds(b * 32 + C_MN, 32)], ALU.add).then_inc(m_cp, 1)
                v.wait_ge(k_rt, b + 2)
                link(v.reciprocal(ssq[:, :], ssq[:, :]))
                v.wait_ge(m_cp, b * 5 + 5)
                link(v.tensor_tensor(S[:, 0:NPG, :].rearrange("p t (h q) -> p t h q", q=NQ),
                                     sRaw[:, :, 0:32].rearrange("p t (h q) -> p t h q", q=NQ),
                                     ssq[:, :].rearrange("p (t h) -> p t h", h=H).unsqueeze(3).broadcast_to([P, NPG, H, NQ]), ALU.mult))
                link(v.tensor_tensor(S[:, 0:NPG, :], S[:, 0:NPG, :], sRaw[:, :, 32:64], ALU.add))
                v.tensor_reduce(mx[:, 0, :], S.rearrange("p t c -> p c t"), AX.X, ALU.max).then_inc(m_mx, 1)
                v.wait_ge(w_sc, b + 1)
                link(v.tensor_tensor(Sw[:, 0:8, :], ps[2][:, 0, 0:256].rearrange("p (t c) -> p t c", c=32),
                                     C[:, C_MW:C_MW + 256].rearrange("p (t c) -> p t c", c=32), ALU.add))
                link(v.tensor_tensor(Sw[0:NS, 8, :], ps[2][0:NS, 0, 256:288], C[0:NS, bass.ds(b * 32 + C_MX, 32)], ALU.add))
                v.tensor_reduce(mx[:, 1, :], Sw.rearrange("p t c -> p c t"), AX.X, ALU.max).then_inc(w_mx, 1)
                v.wait_ge(m_ar, b + 1)
                v.tensor_tensor(S, S, mxa[:, 0:1, :].broadcast_to([P, NPG + 1, 32]), ALU.subtract).then_inc(m_sub, 1)
                v.wait_ge(w_ar, b + 1)
                v.tensor_tensor(Sw, Sw, mxa[:, 1:2, :].broadcast_to([P, NT_W, 32]), ALU.subtract).then_inc(w_sub, 1)
                v.wait_ge(m_e, b + 1)
                v.tensor_reduce(es[:, 0, :], E.rearrange("p t c -> p c t"), AX.X, ALU.add).then_inc(m_es, 1)
                v.wait_ge(w_e, b + 1)
                v.tensor_reduce(es[:, 1, :], Ew.rearrange("p t c -> p c t"), AX.X, ALU.add).then_inc(w_es, 1)
                v.wait_ge(m_pv, b + 1)
                link(v.reciprocal(rd[:, 0, :], ps[3][:, 0, 64:96]))
                for c in range(KC):
                    v.tensor_tensor(oAbs[:, c, :, bass.ds(b * NQ, NQ)],
                                    ps[3][:, 0, c * 32:(c + 1) * 32].rearrange("p (h q) -> p h q", q=NQ),
                                    rd[:, 0, :].rearrange("p (h q) -> p h q", q=NQ), ALU.mult).then_inc(m_o, 1)
                v.wait_ge(w_pv, b + 1)
                link(v.reciprocal(rd[:, 1, :], ps[3][:, 1, 128:160]))
                for z in range(2):
                    r = slice(z * HD, (z + 1) * HD)
                    o = ps[3][r, 1, 0:160].rearrange("p (c n) -> p c n", n=40)[:, :, 4 * z:4 * z + NQ]
                    last = v.tensor_tensor(aT[r, HP:KD, bass.ds(b * NQ + NP_, NQ)], o,
                                           rd[r, 1, :].rearrange("p (c n) -> p c n", c=HP)[:, :, 4 * z:4 * z + NQ], ALU.mult)
                last.then_inc(w_o, 1)
                assert chain["n"] == LOOP_LINKS, chain
            chain["base"], chain["n"] = before + NB * LOOP_LINKS, 0
            v.wait_ge(oa_ev, 1)
            dve_norms([g_oa, g_ob])
            for m in range(KD):
                v.wait_ge(w_used, W_O + m + 1)
                v.tensor_tensor(hT[:, m, :].rearrange("p (a n) -> p a n", a=2), ps[m % 2][:, :, 0:HT],
                                hT[:, m, :].rearrange("p (a n) -> p a n", a=2), ALU.add).then_inc(wo_ev, 1)
            v.wait_ge(wo_ev, KD)
            dve_norms([g_f])
            v.wait_ge(out_s, 80)
            with v.Fori(0, KF // 2) as i:
                for j in range(2):
                    v.wait_ge(gu_act, i * 2 + (j + 1))
                    v.tensor_tensor(hid[:, bass.ds(i * 2 + j, 1), :].rearrange("p t (a n) -> p (t a) n", a=2),
                                    ps[2 * j + 1][:, :, 0:HT], tmp[:, j, :].rearrange("p (a n) -> p a n", a=2),
                                    ALU.mult).then_inc(gu_ev[j], 1)
            with v.Fori(0, KD // 2) as i:
                for j in range(2):
                    v.wait_ge(w_used, i * 4 + (W_DN + 2 * j + 2))
                    h2 = hT[:, bass.ds(i * 2 + j, 1), :].rearrange("p t (a n) -> p (t a) n", a=2)
                    v.tensor_tensor(h2, ps[j][:, :, 0:HT], h2, ALU.add).then_inc(dn_ev[j], 1)
            for j in range(2):
                v.wait_ge(dn_ev[j], KD // 2)
            dve_norms([g_p])
            with v.Fori(0, KD // 4) as i:
                for j in range(4):
                    v.wait_ge(pl_act, i * 4 + (j + 1))
                    t2 = tmp[:, j % 2, :].rearrange("p (a n) -> p a n", a=2)
                    v.tensor_tensor(t2, ps[2 * (j % 2) + 1][:, :, 0:HT], t2, ALU.mult).then_inc(pl_mul, 1)
                    v.wait_ge(pl_mul, i * 4 + (j + 1))
                    h2 = hT[:, bass.ds(i * 4 + j, 1), :].rearrange("p t (a n) -> p (t a) n", a=2)
                    v.tensor_tensor(h2, t2, h2, ALU.add).then_inc(pl_ev[j % 2], 1)


def constants():
    import numpy as np
    c = np.zeros((P, NC_), np.float32)
    i = np.arange(P)
    c[:, C_ONE:C_ONE + P] = 1
    c[:, C_B64:C_B64 + P] = i[:, None] // 64 == i[None] // 64
    b96 = c[:, C_B96:C_B96 + P]
    b96[:64, :64] = 1 / 64
    b96[64:96, 64:96] = 1 / 32
    c[:, C_ID:C_ID + P] = np.eye(P)
    pos = np.concatenate([np.arange(NP_), np.tile(PAST + np.arange(NQ), NB)]).astype(np.float32)

    def rope(rot, cs, sn, starts, half, theta):
        inv = np.float32(theta) ** (-np.arange(half, dtype=np.float32) / np.float32(half))
        ang = pos[None] * inv[:, None]
        c[:, cs:cs + T] = 1
        for s0 in starts:
            for j in range(half):
                a, b = s0 + j, s0 + half + j
                c[b, rot + a] = -1
                c[a, rot + b] = 1
                c[a, cs:cs + T] = c[b, cs:cs + T] = np.cos(ang[j])
                c[a, sn:sn + T] = c[b, sn:sn + T] = np.sin(ang[j])

    rope(C_RS, C_CS, C_SS, (0, 64), 8, 500000.0)
    rope(C_RQ, C_CQ, C_SQ, (64,), 16, 10000.0)

    def multiplicity(dist):
        n = sum((dist >= 0) & (dist <= w) & (dist % d == 0) for w, d in ((128, 1), (512, 4), (2048, 16)))
        return np.where(n > 0, np.log(np.maximum(n, 1)) / SC_B, NEG)

    for blk in range(4):
        dist = (3 - blk) * P + i[:, None] - i[None]
        c[:, C_MA + blk * P:C_MA + (blk + 1) * P] = np.where(dist >= 0, 0, NEG)
        c[:, C_MB + blk * P:C_MB + (blk + 1) * P] = multiplicity(dist)
    q = np.arange(NQ)
    for t in range(8):
        key = 16 * i + t if t < 4 else PAST - REC + P * (t - 4) + i
        m = multiplicity(PAST + q[None] - key[:, None])
        if t < 4:
            m[STR:] = NEG
        c[:, C_MW + t * 32:C_MW + (t + 1) * 32] = np.tile(m, (1, H))
    for b in range(NB):
        same = (np.arange(NS)[:, None] // NQ == b)
        dist = q[None] - np.arange(NS)[:, None] % NQ
        c[:, C_MN + b * 32:C_MN + (b + 1) * 32] = NEG
        c[:, C_MX + b * 32:C_MX + (b + 1) * 32] = NEG
        c[:NS, C_MN + b * 32:C_MN + (b + 1) * 32] = np.tile(np.where(same & (dist >= 0), 0, NEG), (1, H))
        c[:NS, C_MX + b * 32:C_MX + (b + 1) * 32] = np.tile(np.where(same, multiplicity(dist), NEG), (1, H))
    return c


def kernel(**inputs):
    import numpy as np
    import concourse.bacc as bacc
    from concourse.bass_utils import run_bass_kernel_spmd as run

    a = {k: np.asarray(v) for k, v in inputs.items()}

    def tiles(w, width, start=0):
        k = w.shape[0] // P
        return w[:, start:start + width].reshape(k, P, width).transpose(1, 0, 2).reshape(P, k * width)

    def feat(x):
        return x.T.reshape(-1, P, x.shape[0]).transpose(1, 0, 2)

    w_in, w_kvb = a["w_in"][0], a["w_kvb"][0].reshape(KVL, H, 2, NOPE)
    a_end = QL + KVL + ROPE
    starts = [P * m for m in range(8)] + [a_end - HQ] + [a_end + P * m for m in range(8)]
    gate, up = a["w_gate"][0], a["w_up"][0]
    down = a["w_down"][0]
    gains = np.zeros((P, NG), np.float32)
    for name, col in (("g_attn", G_ATT), ("g_ffn", G_FFN), ("g_ple", G_PLE), ("b_ple_gate", B_PLE), ("g_qa", G_QA),
                      ("g_kva", G_KVA), ("g_oa", G_OA), ("g_ob", G_OB)):
        g = a[name][0].reshape(-1, P).T
        gains[:, col:col + g.shape[1]] = g
    gains[:NOPE, G_Q], gains[NOPE:HQ, G_Q] = a["g_qn"][0], a["g_qr"][0]
    gains[:NOPE, G_K], gains[NOPE:HQ, G_K] = a["g_kn"][0], a["g_kr"][0]
    for name, col in (("g_qs", G_QS), ("g_ks", G_KS)):
        gains[:HD, col] = gains[HD:, col] = a[name][0]
    gains[:, G_EPS] = EPS

    lat = a["cache_latent"][0]
    ck = a["cache_swa_k"][0].reshape(NB, PAST, HP, P)
    old = np.arange(PAST - REC).reshape(STR, 16).T
    order = np.concatenate([old[4:].ravel(), old[:4].ravel(), np.arange(PAST - REC, PAST)])
    tok = lambda p, s: np.concatenate([p.reshape(NP_, -1), s.reshape(NS, -1)])
    arr = dict(
        x=feat(tok(a["x_prompt"], a["x_sample"])),
        cst=constants(),
        gains=gains,
        win=np.stack([tiles(w_in, P, s) for s in starts]),
        wvs=w_in[:, a_end + 1024:].reshape(KD, P, 512).transpose(1, 0, 2),
        wqb=np.stack([tiles(a["w_qb"][0], HQ, HQ * h) for h in range(H)]),
        wk=w_kvb[:, :, 0].reshape(KC, P, 512).transpose(1, 0, 2),
        wv=w_kvb[:, :, 1].reshape(KC, P, 512).transpose(1, 0, 2),
        wkt=w_kvb[:, :, 0].transpose(2, 1, 0),
        wo=np.stack([tiles(a["w_o"][0], P, P * m) for m in range(KD)]),
        wgu=np.stack([tiles(w, P, P * m) for m in range(KF) for w in (gate, up)]),
        wdn=np.stack([tiles(down[z * 11 * P:(z + 1) * 11 * P], P, P * m) for m in range(KD) for z in range(2)]),
        wpl=np.stack([np.concatenate([tiles(a["w_ple_gate"][0], P, P * m), tiles(a["w_ple_proj"][0], P, P * m)], 1)
                      for m in range(KD)]),
        plt=feat(tok(a["p_prompt"], a["p_sample"])),
        pgt=lat.reshape(POOL, PAGE, KC, P).transpose(0, 3, 2, 1).reshape(POOL, P, KC * PAGE),
        pgk=a["cache_krope"][0].transpose(0, 2, 1),
        pgl=lat,
        ck=ck[:, order].transpose(0, 2, 3, 1),
        cv=a["cache_swa_v"][0].reshape(NB, PAST, 512),
        pt=a["page_table"].reshape(1, NB * NPG),
    )
    arr = {k: np.ascontiguousarray(v) for k, v in arr.items()}
    outs = dict(y=(KD, P, T), o_lat=(P, KC, T), o_kr=(ROPE, T), o_ks=(P, HP, T), o_vs=(NP_, 512),
                o_ck=(NB, HP, P, PAST), o_cv=(NB, PAST, 512))
    nc = bacc.Bacc("TRN2", target_bir_lowering=False, num_devices=1)
    args = [nc.dram_tensor(f"in_{k}", v.shape, mybir.dt.from_np(v.dtype), kind="ExternalInput").ap() for k, v in arr.items()]
    args += [nc.dram_tensor(f"out_{k}", s, F32, kind="ExternalOutput").ap() for k, s in outs.items()]
    build(nc, *args)
    r = run(nc, [{f"in_{k}": v for k, v in arr.items()}], core_ids=[0]).results[0]
    o = {k: np.asarray(r[f"out_{k}"]) for k in outs}

    def rows(x, width):
        x = x.reshape(width, T).T
        return x[:NP_], x[NP_:]

    yp, ys = rows(o["y"], D)
    lp, ls = rows(o["o_lat"].transpose(1, 0, 2), KVL)
    kp, ks = rows(o["o_kr"], ROPE)
    sp, ss = rows(o["o_ks"].transpose(1, 0, 2), 512)
    back = np.empty(PAST, np.int64)
    back[order] = np.arange(PAST)
    kold = o["o_ck"].reshape(NB, 512, PAST)[:, :, back[NQ:]].transpose(0, 2, 1)
    swk = np.concatenate([kold, ss.reshape(NB, NQ, 512)], 1)
    return (yp.reshape(1, NP_, D), ys.reshape(NB, NQ, D), lp.reshape(1, 1, NP_, KVL), kp.reshape(1, 1, NP_, ROPE),
            sp.reshape(1, 1, NP_, H, HD), o["o_vs"].reshape(1, 1, NP_, H, HD), ls.reshape(1, NB, NQ, KVL),
            ks.reshape(1, NB, NQ, ROPE), swk.reshape(1, NB, PAST, H, HD), o["o_cv"].reshape(1, NB, PAST, H, HD))
```

```python
from contextlib import ExitStack

import concourse.bass as bass
from concourse import mybir

F32 = mybir.dt.float32
I32 = mybir.dt.int32
ACT = mybir.ActivationFunctionType
ALU = mybir.AluOpType
AX = mybir.AxisListType
ADD_ALL = bass.bass_isa.ReduceOp.add
MAX_ALL = bass.bass_isa.ReduceOp.max

P = 128
D = 1024
KD = D // P
NP_ = 512
NB, NQ = 8, 4
NS = NB * NQ
T = NP_ + NS
HT = T // 2
H = 8
NOPE, ROPE, HQ = 64, 32, 96
QL, KVL = 768, 256
KQ, KC = QL // P, KVL // P
DFF = 2816
KF = DFF // P
HD = 64
HP = H // 2
PAST, PAGE = 2048, 128
NPG = PAST // PAGE
POOL = 160
PLE = 256
EPS = 1e-6
NEG = -1e30
SC_A = HQ ** -0.5
SC_B = HD ** -0.5
NIN = 17
U_CQ, U_LAT, U_KR, U_QS, U_KS = 0, 6, 8, 9, 13
RING = 4
SLOT = 11 * P
REC = 512
STR = (PAST - REC) // 16
NKW = 896 + NS
LOOP_LINKS = 9
NT_W = 9
PR = 8

C_ONE, C_B64, C_B96, C_RS, C_RQ, C_ID = (i * P for i in range(6))
C_MA = 6 * P
C_MB = C_MA + 512
C_CS = C_MB + 512
C_SS = C_CS + T
C_CQ = C_SS + T
C_SQ = C_CQ + T
C_MN = C_SQ + T
C_MW = C_MN + NB * 32
C_MX = C_MW + 896
NC_ = C_MX + NB * 32
G_ATT, G_FFN, G_PLE, B_PLE, G_QA, G_KVA, G_Q, G_K, G_QS, G_KS, G_OA, G_OB, G_EPS, NG = (
    0, 8, 16, 24, 32, 38, 40, 41, 42, 43, 44, 48, 52, 53)

W_IN, W_QB = 0, NIN
W_O = W_QB + H
W_GU = W_O + KD
W_DN = W_GU + 2 * KF
W_PL = W_DN + 2 * KD
W_END = W_PL + KD


def build(nc, x, cst, gains, win, wvs, wqb, wk, wv, wkt, wo, wgu, wdn, wpl, plt, pgt, pgk, pgl, ck, cv, pt,
          y, o_lat, o_kr, o_ks, o_vs, o_ck, o_cv):
    with ExitStack() as ctx:
        def sb(name, shape, dt=F32):
            return ctx.enter_context(nc.sbuf_tensor(name, shape, dt))

        def sem(name):
            return ctx.enter_context(nc.semaphore(name))

        hT = sb("hT", [P, KD, T])
        aT = sb("aT", [P, KD, T])
        big = sb("big", [P, (NIN + H) * T])
        uT = big[:, 0:NIN * T].rearrange("p (t n) -> p t n", n=T)
        QT = big[:, NIN * T:].rearrange("p (t n) -> p t n", n=T)
        hid = big[:, 0:KF * T].rearrange("p (t n) -> p t n", n=T)
        plT = big[:, KF * T:(KF + 2) * T].rearrange("p (t n) -> p t n", n=T)
        pgT = big[:, 0:PR * 256].rearrange("p (s n) -> p s n", s=PR)
        pgR = big[:, PR * 256:PR * 384].rearrange("p (s n) -> p s n", s=PR)
        cK = big[:, NIN * T:NIN * T + HP * 896].rearrange("p (c n) -> p c n", c=HP)
        kv1 = sb("kv1", [P, H * T])
        KT = kv1[:, :].rearrange("p (t n) -> p t n", n=T)
        wvS = kv1[:, 0:KD * 512].rearrange("p (k n) -> p k n", k=KD)
        pgL = kv1[:, 0:NPG * KVL].rearrange("p (t n) -> p t n", n=KVL)
        kv2 = sb("kv2", [P, 8 * 512])
        vA = kv2[:, 0:2048].rearrange("p (t n) -> p t n", n=512)
        vB = kv2[:, 2048:4096].rearrange("p (t n) -> p t n", n=512)
        wkT = kv2[0:NOPE, 0:2048].rearrange("p (h n) -> p h n", h=H)
        cVr = kv2[:, 0:2048].rearrange("p (j n) -> p j n", j=4)
        cVs = kv2[0:STR, 2048:4096].rearrange("p (r n) -> p r n", r=4)
        vNew = sb("vNew", [NS, 512])
        latNew = sb("latNew", [NS, KVL])
        ring = sb("ring", [P, RING, SLOT])
        C = sb("C", [P, NC_])
        G = sb("G", [P, NG])
        wK = sb("wK", [P, KC, 512])
        wV = sb("wV", [P, KC, 512])
        sq = sb("sq", [P, 2, T])
        R = sb("R", [P, 2, T])
        tmp = sb("tmp", [P, 2, T])
        att = sb("att", [P, 4, 512])
        pr = att
        sqK = att[:, 0:2, :]
        sRaw = att[:, 2:4, :].rearrange("p a (t c) -> p (a t) c", c=64)
        S = sq[:, :, :].rearrange("p a n -> p (a n)")[:, 0:544].rearrange("p (t c) -> p t c", c=32)
        E = sq[:, :, :].rearrange("p a n -> p (a n)")[:, 544:1088].rearrange("p (t c) -> p t c", c=32)
        Rf = R[:, :, :].rearrange("p a n -> p (a n)")
        prT = Rf[:, 0:1024].rearrange("p (a n) -> p a n", a=2)
        Ew = Rf[:, 0:288].rearrange("p (t c) -> p t c", c=32)
        qrAll = Rf[:, 576:832].rearrange("p (b c) -> p b c", b=NB)
        qwAll = Rf[:, 832:1088].rearrange("p (b c) -> p b c", b=NB)
        tf = tmp[:, :, :].rearrange("p a n -> p (a n)")
        qaAll = tf[:, 0:512].rearrange("p (b c) -> p b c", b=NB)
        oAbs = tf[:, 512:1024].rearrange("p (c h n) -> p c h n", c=KC, h=H)
        qa = sb("qa", [P, 64])
        qr = sb("qr", [P, 32])
        qw = sb("qw", [P, 160])
        Sw = sb("Sw", [NS, NKW])
        On = sb("On", [NS, KVL + 512])
        mNew = sb("mNew", [NS, 32])
        sm = sb("sm", [NS, 8])
        qg = sb("qg", [NOPE, H, NS])
        ssq = sb("ssq", [P, P])
        rkN = sb("rkN", [NS, H])
        sN = sb("sN", [NS, 32])
        mx = sb("mx", [P, 32])
        mxa = sb("mxa", [P, 32])
        es = sb("es", [P, 32])
        st = sb("st", [P, 16])
        ptab = sb("ptab", [1, NB * NPG], I32)

        ps = [ctx.enter_context(nc.psum_tensor(f"ps{i}", [P, 2, 512], F32)) for i in range(4)]

        s_c, s_x, s_g, s_wvs, s_wk, s_wkt, s_plt, s_pt = (sem(n) for n in (
            "const_in", "x_in", "gains_in", "wvs_in", "wkv_in", "wkt_in", "plt_in", "ptab_in"))
        w_in_ = [sem(f"w_in{i}") for i in range(RING)]
        w_used = sem("unit_done")
        n_sq, n_squ, n_rt, n_out, n_rot, n_nc, n_rope = (sem(n) for n in (
            "norm_sq", "norm_summed", "norm_root", "norm_out", "rot_mm", "rope_cos", "rope_out"))
        vs_mm, in_ev, qb_ev, k_mm, k_ev, v_mm, v_ev = (sem(n) for n in (
            "vs_mm", "in_ev", "qb_ev", "k_mm", "k_ev", "v_mm", "v_ev"))
        kr_b, tn_mm, tn_ev, kn_sq, kn_ss = (sem(n) for n in (
            "krope_spread", "latnew_mm", "latnew_ev", "knew_sq", "knew_ssq"))
        a_s, a_sm, a_e, a_p, a_t, a_tc, a_pv, a_o, a_nm = (sem(n) for n in (
            "att_scores", "att_max", "att_exp", "att_probs", "att_turned", "att_turned_sb", "att_pv", "att_out",
            "att_negmax"))
        dve = sem("dve_chain")
        p_set, p_qg, p_ab, p_all = (sem(n) for n in ("prep_zero", "prep_qg", "prep_absorb_mm", "prep_all"))
        q_st, k_raw, k_sq, k_ss, r_used, m_sc, m_cp, w_sc = (sem(n) for n in (
            "queries_staged", "kraw_mm", "kraw_sq", "kraw_ssq", "page_used", "mla_scores", "mla_scores_cp",
            "swa_scores"))
        k_rt, m_mx, m_ar, m_sub, m_e, m_es, m_pv, m_o = (sem(n) for n in (
            "key_root", "mla_max", "mla_allmax", "mla_shifted", "mla_exp", "mla_expsum", "mla_pv", "mla_out"))
        w_nm, w_e, w_t, w_tc, w_pv, w_on, w_tt, w_o, m_on, m_tt = (sem(n) for n in (
            "swa_negmax", "swa_exp", "swa_turned", "swa_turned_sb", "swa_pv", "swa_normed", "swa_out_turned", "swa_out",
            "mla_normed", "mla_out_turned"))
        pg_in = [sem(f"page_in{i}") for i in range(PR)]
        pl_in, ck_in, cv_in = sem("pages_in"), sem("ck_in"), sem("cv_in")
        passed, passed_v, passed_t = sem("pool_passed"), sem("dve_passed"), sem("pe_passed")
        oa_mm, oa_ev = sem("oa_mm"), sem("oa_ev")
        wo_ev, gu_act, pl_act, pl_mul = (sem(n) for n in ("wo_ev", "silu", "ple_gate", "ple_gated"))
        gu_ev, dn_ev, pl_ev = ([sem(f"{n}{j}") for j in range(2)] for n in ("hidden", "down_ev", "ple_ev"))
        out_c, out_s, out_y = sem("copies_out"), sem("states_out"), sem("y_out")

        def cm(off, rows=slice(0, P), n=P):
            return C[rows, off:off + n]

        FULL, LO, MID = slice(0, P), slice(0, HQ), slice(NOPE, HQ)
        groups = []

        def group(tiles, rows, ones, n, gain, w=T, rope=None, dst=None):
            groups.append(dict(src=tiles, dst=dst or tiles, rows=rows, ones=ones, n=n, gain=gain, w=w, rope=rope))
            return len(groups) - 1

        def hcol(buf, k):
            return buf[:, k, :]

        g_x = group([hT[:, k, :] for k in range(KD)], FULL, cm(C_ONE), D, G_ATT, dst=[aT[:, k, :] for k in range(KD)])
        g_cq = group([uT[:, k, :] for k in range(KQ)], FULL, cm(C_ONE), QL, G_QA)
        g_lat = group([uT[:, U_LAT + k, :] for k in range(KC)], FULL, cm(C_ONE), KVL, G_KVA)
        g_kr = group([uT[MID, U_KR, :]], MID, C[MID, C_B96 + NOPE:C_B96 + HQ], ROPE, G_K, rope=(C_RQ, C_CQ, C_SQ))
        g_qs = [group([uT[:, U_QS + i, :]], FULL, cm(C_B64), HD, G_QS, rope=(C_RS, C_CS, C_SS)) for i in range(HP)]
        g_ks = [group([uT[:, U_KS + i, :]], FULL, cm(C_B64), HD, G_KS, rope=(C_RS, C_CS, C_SS)) for i in range(HP)]
        g_qh = [group([QT[LO, h, :]], LO, C[LO, C_B96:C_B96 + HQ], None, G_Q, rope=(C_RQ, C_CQ, C_SQ)) for h in range(H)]
        LOW = slice(0, NOPE)
        g_kh = [group([KT[LOW, h, 0:NP_]], LOW, C[LOW, C_B96:C_B96 + NOPE], NOPE, G_K, w=NP_) for h in range(H)]
        g_oa = group([aT[:, k, :] for k in range(HP)], FULL, cm(C_ONE), H * HD, G_OA)
        g_ob = group([aT[:, HP + k, :] for k in range(HP)], FULL, cm(C_ONE), H * HD, G_OB)
        g_f = group([hT[:, k, :] for k in range(KD)], FULL, cm(C_ONE), D, G_FFN, dst=[aT[:, k, :] for k in range(KD)])
        g_p = group([hT[:, k, :] for k in range(KD)], FULL, cm(C_ONE), D, G_PLE, dst=[aT[:, k, :] for k in range(KD)])
        tiles_before = [sum(len(g["src"]) for g in groups[:i]) for i in range(len(groups) + 1)]
        ropes_before = [sum(g["rope"] is not None for g in groups[:i]) for i in range(len(groups) + 1)]

        def norm_squares(g):
            q = groups[g]
            rows, w = q["rows"], q["w"]
            for j, src in enumerate(q["src"]):
                k = tiles_before[g] + j
                if k >= 2:
                    nc.scalar.wait_ge(n_squ, k - 1)
                nc.scalar.activation(sq[rows, k % 2, 0:w], src, ACT.Square).then_inc(n_sq, 1)

        def norm_root(g):
            q = groups[g]
            rows, w = q["rows"], q["w"]
            nc.scalar.wait_ge(n_squ, tiles_before[g + 1])
            if g >= 2:
                nc.scalar.wait_ge(n_out, g - 1)
            scale = 1.0 / q["n"] if rows == FULL else 1.0
            nc.scalar.activation(R[rows, g % 2, 0:w].rearrange("p (a n) -> p a n", a=2),
                                 ps[2 + g % 2][rows, :, 0:w // 2], ACT.Sqrt, scale=scale,
                                 bias=G[rows, G_EPS:G_EPS + 1]).then_inc(n_rt, 1)

        def act_norms(gs):
            norm_squares(gs[0])
            for i, g in enumerate(gs):
                if i + 1 < len(gs):
                    norm_squares(gs[i + 1])
                norm_root(g)

        def pe_norm(g):
            q = groups[g]
            rows, hw = q["rows"], q["w"] // 2
            if g >= 2:
                nc.tensor.wait_ge(n_rt, g - 1)
            for j in range(len(q["src"])):
                k = tiles_before[g] + j
                nc.tensor.wait_ge(n_sq, k + 1)
                for a in range(2):
                    last = nc.tensor.matmul(ps[2 + g % 2][rows, a, 0:hw], q["ones"], sq[rows, k % 2, a * hw:(a + 1) * hw],
                                            start=(j == 0), stop=(j == len(q["src"]) - 1))
                last.then_inc(n_squ, 1)

        def pe_rot(g):
            q = groups[g]
            rows, w, i = q["rows"], q["w"], ropes_before[g]
            nc.tensor.wait_ge(n_out, g + 1)
            if i >= 1:
                nc.tensor.wait_ge(n_rope, i)
            for a in range(2):
                last = nc.tensor.matmul(ps[1][rows, a, 0:HT], C[rows, q["rope"][0] + rows.start:q["rope"][0] + rows.stop],
                                        q["dst"][0][:, a * HT:(a + 1) * HT], start=True, stop=True)
            last.then_inc(n_rot, 1)

        def pe_norms(gs):
            for i, g in enumerate(gs):
                pe_norm(g)
                if i and groups[gs[i - 1]]["rope"]:
                    pe_rot(gs[i - 1])
            if groups[gs[-1]]["rope"]:
                pe_rot(gs[-1])

        def pool_cos(g):
            q = groups[g]
            rows, i = q["rows"], ropes_before[g]
            nc.gpsimd.wait_ge(n_out, g + 1)
            if i >= 1:
                nc.gpsimd.wait_ge(n_rope, i)
            nc.gpsimd.tensor_tensor(tmp[rows, 0, :], q["dst"][0], C[rows, q["rope"][1]:q["rope"][1] + T],
                                    ALU.mult).then_inc(n_nc, 1)

        chain = dict(base=0, n=0)

        def link(ins):
            chain["n"] += 1
            ins.then_inc(dve, 1)
            nc.vector.wait_ge(dve, chain["base"] + chain["n"])

        def dve_scale(g):
            q = groups[g]
            rows, w = q["rows"], q["w"]
            nc.vector.wait_ge(n_rt, g + 1)
            link(nc.vector.reciprocal(R[rows, g % 2, 0:w], R[rows, g % 2, 0:w]))
            for j, (src, dst) in enumerate(zip(q["src"], q["dst"])):
                gc = q["gain"] + (j if len(q["src"]) > 1 else 0)
                last = nc.vector.scalar_tensor_tensor(out=dst, in0=src, scalar=G[rows, gc:gc + 1], in1=R[rows, g % 2, 0:w],
                                                      op0=ALU.mult, op1=ALU.mult)
            last.then_inc(n_out, 1)

        def dve_rope(g):
            q = groups[g]
            rows, i = q["rows"], ropes_before[g]
            nc.vector.wait_ge(n_rot, i + 1)
            link(nc.vector.tensor_tensor(tmp[rows, 1, :].rearrange("p (a n) -> p a n", a=2), ps[1][rows, :, 0:HT],
                                         C[rows, q["rope"][2]:q["rope"][2] + T].rearrange("p (a n) -> p a n", a=2),
                                         ALU.mult))
            nc.vector.wait_ge(n_nc, i + 1)
            nc.vector.tensor_tensor(q["dst"][0], tmp[rows, 0, :], tmp[rows, 1, :], ALU.add).then_inc(n_rope, 1)

        def dve_norms(gs):
            for i, g in enumerate(gs):
                dve_scale(g)
                if i and groups[gs[i - 1]]["rope"]:
                    dve_rope(gs[i - 1])
            if groups[gs[-1]]["rope"]:
                dve_rope(gs[-1])

        RUN1 = [g_cq, g_lat, g_kr]
        RUN2 = g_qs + g_ks
        RUN3 = g_qh + g_kh

        def pe_weight(u, i=None, per=0):
            n = 16 * (u // RING + 1)
            nc.tensor.wait_ge(w_in_[u % RING], n if i is None else n + i * (16 * per // RING))
            return ring[:, u % RING, :]

        def sp_weight(u, src):
            if u >= RING:
                nc.sync.wait_ge(w_used, u - RING + 1)
            nc.sync.dma_start(ring[:, u % RING, 0:src.shape[-1]], src).then_inc(w_in_[u % RING], 16)

        def sp_weight_loop(u0, n, src):
            with nc.sync.Fori(0, n // RING) as i:
                for j in range(RING):
                    nc.sync.wait_ge(w_used, i * RING + (u0 + j - RING + 1))
                    nc.sync.dma_start(ring[:, (u0 + j) % RING, 0:src.shape[-1]],
                                      src[bass.ds(i * RING + j, 1), :, :].rearrange("a p n -> p (a n)")
                                      ).then_inc(w_in_[(u0 + j) % RING], 16)

        units = [(h, i) for h in range(2 * H) for i in range(4)]

        def heads(h):
            if h < H:
                return QT[LO, h, :], KT[LO, h, :], vA
            r = slice((h % 2) * HD, (h % 2) * HD + HD)
            c = (h - H) // 2
            return uT[r, U_QS + c, :], uT[r, U_KS + c, :], vB

        block = ctx.enter_context(nc.Block())

        @block.sync
        def _(sp):
            sp.dma_start(hT[:, :, :], x).then_inc(s_x, 16)
            sp.dma_start(G[:, :], gains).then_inc(s_g, 16)
            sp.dma_start(C[:, :], cst).then_inc(s_c, 16)
            for u in range(RING):
                sp_weight(W_IN + u, win[u])
            sp.dma_start(wvS, wvs).then_inc(s_wvs, 16)
            sp.dma_start(wK[:, :, :], wk).then_inc(s_wk, 16)
            sp.dma_start(wV[:, :, :], wv).then_inc(s_wk, 16)
            sp.dma_start(ptab[:, :], pt).then_inc(s_pt, 16)
            for u in range(RING, NIN):
                sp_weight(W_IN + u, win[u])
            for u in range(H):
                sp_weight(W_QB + u, wqb[u])
            for u in range(RING):
                sp_weight(W_O + u, wo[u])
            sp.wait_ge(a_o, H)
            sp.dma_start(wkT, wkt).then_inc(s_wkt, 16)
            sp.wait_ge(s_pt, 16)
            with sp.Fori(0, NB) as b:
                page = []

                def load_page_T(t):
                    src = bass.ds(page[t], 1)
                    sp.dma_start(pgT[:, t % PR, :], pgt[src, :, :].rearrange("a p n -> p (a n)")).then_inc(pg_in[t % PR], 16)
                    sp.dma_start(pgR[MID, t % PR, :], pgk[src, :, :].rearrange("a p n -> p (a n)")).then_inc(pg_in[t % PR], 16)

                sp.wait_ge(w_sc, b)
                sp.wait_ge(out_s, 80)
                sp.wait_ge(p_all, 1)
                sp.dma_start(cK, ck[bass.ds(b, 1), :, :, PAST - 896:PAST].rearrange("a c p n -> p (a c) n")).then_inc(ck_in, 16)
                for t in range(NPG):
                    page.append(sp.value_load(ptab[0:1, bass.ds(b * NPG + t, 1)], min_val=0, max_val=POOL - 1))
                sp.wait_ge(m_sc, b)
                for t in range(PR):
                    load_page_T(t)
                sp.wait_ge(w_pv, b)
                sp.dma_start(cVr, cv[bass.ds(b, 1), PAST - REC:PAST, :].rearrange("a (j p) n -> p (a j) n", p=P)).then_inc(cv_in, 16)
                sp.dma_start(cVs, cv[bass.ds(b, 1), 0:PAST - REC, :].rearrange("a (g r) n -> g (a r) n", r=16)[:, 0:4, :]).then_inc(cv_in, 16)
                sp.wait_ge(m_pv, b)
                for t in range(NPG):
                    sp.dma_start(pgL[:, t, :], pgl[bass.ds(page[t], 1), :, :].rearrange("a p n -> p (a n)")).then_inc(pl_in, 16)
                for t in range(PR, NPG):
                    sp.wait_ge(r_used, b * NPG + (t - PR + 1))
                    load_page_T(t)
            for u in range(RING, KD):
                sp_weight(W_O + u, wo[u])
            sp.wait_ge(w_pv, NB)
            sp.dma_start(plT, plt).then_inc(s_plt, 16)
            sp_weight_loop(W_GU, 2 * KF, wgu)
            sp_weight_loop(W_DN, 2 * KD, wdn)
            sp_weight_loop(W_PL, KD, wpl)
            for m in range(KD):
                sp.wait_ge(pl_ev[m % 2], m // 2 + 1)
                sp.dma_start(y[m], hT[:, m, :]).then_inc(out_y, 16)
            sp.wait_ge(out_y, 16 * KD)

        @block.gpsimd
        def _(pool):
            HALF = (PAST - NQ) // 2

            def copy_k(b, z):
                c = slice(2 * z, 2 * z + 2)
                pool.dma_start(o_ck[b, c].rearrange("c p n -> (c p n)").rearrange("(a n) -> a n", a=32),
                               ck[b, c].rearrange("c p n -> (c p n)").rearrange("(a n) -> a n", a=32)).then_inc(out_c, 16)

            def copy_v(b, z):
                pool.dma_start(o_cv[b, z * HALF:(z + 1) * HALF, :],
                               cv[b, NQ + z * HALF:NQ + (z + 1) * HALF, :]).then_inc(out_c, 16)

            for k in range(8):
                pool.wait_ge(w_used, 2 * k + 1)
                copy_k(k // 2, k % 2)
            pool.wait_ge(s_c, 16)
            pool_cos(g_kr)
            for g in RUN2:
                pool_cos(g)
            for g in g_qh:
                pool_cos(g)
            pool.wait_ge(n_rope, 1 + len(RUN2))
            pool.dma_start(o_lat, uT[:, U_LAT:U_LAT + KC, :]).then_inc(out_s, 16)
            pool.dma_start(o_kr, uT[MID, U_KR, :]).then_inc(out_s, 16)
            pool.dma_start(o_ks, uT[:, U_KS:U_KS + HP, :]).then_inc(out_s, 16)
            pool.wait_ge(in_ev, NIN + 5)
            pool.dma_start(o_vs.rearrange("(t p) n -> p t n", p=P), vB).then_inc(out_s, 16)
            pool.dma_start(o_cv[:, PAST - NQ:PAST, :].rearrange("b q n -> b (q n)"),
                           vNew[:, :]).then_inc(out_s, 16)
            pool.wait_ge(out_s, 80)
            for k in range(8):
                pool.wait_ge(a_s, 8 * k + 1)
                copy_v(k // 2, k % 2)
            pool.wait_ge(p_all, 1)
            with pool.Fori(0, NB) as b:
                pool.wait_ge(m_sc, b)
                pool.tensor_copy(qa[:, :], qaAll[:, bass.ds(b, 1), :].rearrange("p a n -> p (a n)")).then_inc(q_st, 1)
                pool.wait_ge(q_st, b * 4 + 1)
                pool.tensor_copy(qr[MID, :], qrAll[MID, bass.ds(b, 1), :].rearrange("p a n -> p (a n)")).then_inc(q_st, 1)
                pool.wait_ge(q_st, b * 4 + 2)
                pool.tensor_copy(qw[:, 0:160].rearrange("p (c n) -> p c n", n=40)[:, :, 0:8],
                                 qwAll[:, bass.ds(b, 1), :].rearrange("p a (c n) -> p (a c) n", c=HP)).then_inc(q_st, 1)
                pool.wait_ge(q_st, b * 4 + 3)
                pool.tensor_copy(mNew[:, :], C[0:NS, bass.ds(b * 32 + C_MX, 32)]).then_inc(q_st, 1)
                pool.wait_ge(q_st, b * 4 + 4)
                pool.wait_ge(m_mx, b + 1)
                pool.sem_inc(passed, 1)
                pool.partition_all_reduce(mxa[:, :], mx[:, :], P, MAX_ALL).then_inc(m_ar, 1)
            for b in range(4, NB):
                for k in range(4):
                    pool.wait_ge(w_used, W_GU + 16 * (b - 4) + 4 * k + 1)
                    (copy_v if k % 2 else copy_k)(b, k // 2)
            pool.wait_ge(out_c, 16 * 4 * NB)

        @block.scalar
        def _(act):
            act.wait_ge(s_x, 16)
            act.wait_ge(s_g, 16)
            act.wait_ge(s_c, 16)
            act_norms([g_x])

            def in_copy(m):
                if m < NIN:
                    act.wait_ge(w_used, W_IN + m + 1)
                else:
                    act.wait_ge(vs_mm, m - NIN + 1)
                if m < NIN:
                    rows = MID if m == U_KR else FULL
                    act.activation(uT[rows, m, :].rearrange("p (a n) -> p a n", a=2), ps[m % 2][rows, :, 0:HT],
                                   ACT.Copy).then_inc(in_ev, 1)
                elif m < NIN + 4:
                    act.activation(vB[:, m - NIN, :], ps[m % 2][:, 0, :], ACT.Copy).then_inc(in_ev, 1)
                else:
                    act.activation(vNew[:, :], ps[m % 2][0:NS, 0, :], ACT.Copy).then_inc(in_ev, 1)

            for m in range(U_QS):
                in_copy(m)
            act.wait_ge(in_ev, U_QS)
            act_norms(RUN1)
            for m in range(U_QS, NIN + 5):
                in_copy(m)
            act.wait_ge(in_ev, NIN + 5)
            act_norms(RUN2)
            for h in range(H):
                act.wait_ge(w_used, W_QB + h + 1)
                act.activation(QT[LO, h, :].rearrange("p (a n) -> p a n", a=2), ps[(NIN + 5 + h) % 2 * 3][LO, :, 0:HT],
                               ACT.Copy).then_inc(qb_ev, 1)
            for h in range(H):
                act.wait_ge(k_mm, h + 1)
                act.activation(KT[LOW, h, 0:NP_], ps[0][LOW, h % 2, :], ACT.Copy).then_inc(k_ev, 1)
            for t in range(4):
                act.wait_ge(v_mm, t + 1)
                act.activation(vA[:, t, :], ps[0][:, t % 2, :], ACT.Copy).then_inc(v_ev, 1)
            act.wait_ge(v_mm, 5)
            act.wait_ge(n_rope, ropes_before[RUN2[-1] + 1])
            act.activation(tmp[0:NS, 0, 0:512], ps[0][0:NS, 0, :], ACT.Square).then_inc(kn_sq, 1)
            act.wait_ge(tn_mm, 1)
            act.activation(latNew[:, :], ps[0][0:NS, 1, 0:KVL], ACT.Copy).then_inc(tn_ev, 1)
            act.wait_ge(k_ev, H)
            act.wait_ge(qb_ev, H)
            act_norms(RUN3)
            act.wait_ge(kn_ss, 1)
            act.activation(rkN[:, :], rkN[:, :], ACT.Sqrt, scale=1.0 / NOPE, bias=G[0:NS, G_EPS:G_EPS + 1]).then_inc(k_rt, 1)

            for n in range(len(units) + 4):
                if n < len(units):
                    w = (units[n][1] + 1) * P
                    k = n % 4
                    act.wait_ge(a_nm, n + 1)
                    act.activation(pr[:, k, 0:w], pr[:, k, 0:w], ACT.Exp, bias=st[:, k:k + 1],
                                   accum_out=st[:, 4 + k:5 + k]).then_inc(a_e, 1)
                if n >= 4:
                    m = n - 4
                    w = (units[m][1] + 1) * P
                    act.wait_ge(a_t, m + 1)
                    if m >= 2:
                        act.wait_ge(a_pv, m - 1)
                    act.activation(prT[:, m % 2, 0:w], ps[1][:, m % 2, 0:w], ACT.Copy).then_inc(a_tc, 1)

            with act.Fori(0, NB) as b:
                act.wait_ge(w_nm, b + 1)
                act.activation(Sw[:, :], Sw[:, :], ACT.Exp, bias=sm[:, 5:6], accum_out=sm[:, 3:4]).then_inc(w_e, 1)
                for t in range(NPG):
                    act.wait_ge(k_raw, b * NPG + (t + 1))
                    if t >= 2:
                        act.wait_ge(k_ss, b * NPG + (t - 1))
                    else:
                        act.wait_ge(k_ss, b * NPG)
                    act.activation(sqK[:, t % 2, :], ps[0][:, t % 2, :], ACT.Square).then_inc(k_sq, 1)
                act.wait_ge(w_t, b + 1)
                act.activation(Rf[:, 0:256], ps[2][:, 0, 0:256], ACT.Copy)
                act.activation(Rf[0:NS, 256:288], ps[2][0:NS, 0, 256:288], ACT.Copy).then_inc(w_tc, 1)
                act.wait_ge(k_ss, b * NPG + NPG)
                act.activation(ssq[:, :], ssq[:, :], ACT.Sqrt, scale=1.0 / NOPE, bias=G[:, G_EPS:G_EPS + 1]).then_inc(k_rt, 1)
                act.wait_ge(m_sub, b + 1)
                act.activation(E, S, ACT.Exp, scale=SC_A).then_inc(m_e, 1)
            act.wait_ge(oa_mm, 1)
            act.activation(aT[:, 0:HP, NP_:T], ps[0][:, 0, 0:HP * NS].rearrange("p (c n) -> p c n", c=HP), ACT.Copy).then_inc(oa_ev, 1)
            act.wait_ge(oa_ev, 1)
            act.wait_ge(w_o, NB)
            act_norms([g_oa, g_ob])
            act.wait_ge(wo_ev, KD)
            act_norms([g_f])
            with act.Fori(0, KF // 2) as i:
                for j in range(2):
                    act.wait_ge(w_used, i * 4 + (W_GU + 2 * j + 2))
                    act.wait_ge(gu_ev[j], i)
                    act.activation(tmp[:, j, :].rearrange("p (a n) -> p a n", a=2), ps[2 * j][:, :, 0:HT],
                                   ACT.Silu).then_inc(gu_act, 1)
            for j in range(2):
                act.wait_ge(dn_ev[j], KD // 2)
            act_norms([g_p])
            with act.Fori(0, KD // 4) as i:
                for j in range(4):
                    act.wait_ge(w_used, i * 4 + (W_PL + j + 1))
                    act.wait_ge(pl_ev[j % 2], i * 2 + j // 2)
                    act.activation(tmp[:, j % 2, :].rearrange("p (a n) -> p a n", a=2), ps[2 * (j % 2)][:, :, 0:HT],
                                   ACT.Sigmoid, bias=G[:, bass.ds(i * 4 + (B_PLE + j), 1)]).then_inc(pl_act, 1)

        @block.tensor
        def _(pe):
            mm = nc.tensor.matmul
            pe.wait_ge(s_c, 16)
            pe_norms([g_x])
            pe.wait_ge(n_out, 1)

            def in_tile(m):
                if m >= 2:
                    pe.wait_ge(in_ev, m - 1)
                if m < NIN:
                    w = pe_weight(W_IN + m)
                    cols, rows = (HQ, LO) if m == U_KR else (P, FULL)
                    for k in range(KD):
                        for a in range(2):
                            last = mm(ps[m % 2][rows, a, 0:HT], w[:, k * P:k * P + cols], aT[:, k, a * HT:(a + 1) * HT],
                                      start=(k == 0), stop=(k == KD - 1))
                    last.then_inc(w_used, 1)
                else:
                    t = m - NIN
                    n = P if t < 4 else NS
                    if t == 0:
                        pe.wait_ge(s_wvs, 16)
                    for k in range(KD):
                        last = mm(ps[m % 2][0:n, 0, :], aT[:, k, t * P:t * P + n], wvS[:, k, :], start=(k == 0), stop=(k == KD - 1))
                    last.then_inc(vs_mm, 1)

            for m in range(U_QS):
                in_tile(m)
            for g in RUN1:
                pe_norm(g)
            for m in range(U_QS, NIN + 5):
                in_tile(m)
            pe.wait_ge(in_ev, NIN + 5)
            pe_rot(g_kr)
            pe_norms(RUN2)
            for h in range(H):
                bank = ps[(NIN + 5 + h) % 2 * 3]
                if h >= 2:
                    pe.wait_ge(qb_ev, h - 1)
                elif h == 1:
                    pe.wait_ge(n_rt, RUN2[-1] + 1)
                w = pe_weight(W_QB + h)
                for k in range(KQ):
                    for a in range(2):
                        last = mm(bank[LO, a, 0:HT], w[:, k * HQ:(k + 1) * HQ], uT[:, U_CQ + k, a * HT:(a + 1) * HT],
                                  start=(k == 0), stop=(k == KQ - 1))
                last.then_inc(w_used, 1)
            pe.wait_ge(s_wk, 32)
            pe.wait_ge(qb_ev, H)
            for h in range(H):
                if h >= 2:
                    pe.wait_ge(k_ev, h - 1)
                for k in range(KC):
                    last = mm(ps[0][LOW, h % 2, :], wK[:, k, h * NOPE:(h + 1) * NOPE], uT[:, U_LAT + k, 0:NP_],
                              start=(k == 0), stop=(k == KC - 1))
                last.then_inc(k_mm, 1)
            for t in range(5):
                pe.wait_ge(k_ev, H) if t < 2 else pe.wait_ge(v_ev, t - 1)
                n = P if t < 4 else NS
                for k in range(KC):
                    last = mm(ps[0][0:n, t % 2, :], uT[:, U_LAT + k, t * P:t * P + n], (wV if t < 4 else wK)[:, k, :],
                              start=(k == 0), stop=(k == KC - 1))
                last.then_inc(v_mm, 1)
            pe.wait_ge(v_ev, 4)
            for k in range(KC):
                last = pe.transpose(ps[0][0:NS, 1, k * P:(k + 1) * P], uT[:, U_LAT + k, NP_:T], cm(C_ID))
            last.then_inc(tn_mm, 1)
            pe_norms(RUN3)

            pe.wait_ge(kr_b, 1)
            pe.wait_ge(n_rope, ropes_before[-1])
            pe.wait_ge(n_out, g_kh[-1] + 1)
            pe.wait_ge(tn_ev, 1)
            pe.wait_ge(kn_sq, 1)
            for n in range(len(units) + 5):
                if n < len(units):
                    h, i = units[n]
                    q, k, _v = heads(h)
                    if n >= 2:
                        pe.wait_ge(a_sm, n - 1)
                    mm(ps[0][:, n % 2, 0:(i + 1) * P], q[:, i * P:(i + 1) * P], k[:, 0:(i + 1) * P],
                       start=True, stop=True).then_inc(a_s, 1)
                if n >= 3 and n - 3 < len(units):
                    m = n - 3
                    h, i = units[m]
                    pe.wait_ge(a_p, m + 1)
                    if m >= 2:
                        pe.wait_ge(a_tc, m - 1)
                    for j in range(i + 1):
                        last = pe.transpose(ps[1][:, m % 2, j * P:(j + 1) * P], pr[:, m % 4, j * P:(j + 1) * P], cm(C_ID))
                    last.then_inc(a_t, 1)
                if n >= 5:
                    m = n - 5
                    h, i = units[m]
                    _q, _k, v = heads(h)
                    pe.wait_ge(a_tc, m + 1)
                    if i == 0 and h % 2 == 0 and h >= 4:
                        pe.wait_ge(a_o, h // 2 - 1)
                    r = slice((h % 2) * HD, (h % 2) * HD + HD)
                    for j in range(i + 1):
                        last = mm(ps[2][r, (h // 2) % 2, i * P:(i + 1) * P], v[:, j, (h % H) * HD:(h % H + 1) * HD],
                                  prT[:, m % 2, j * P:(j + 1) * P], start=(j == 0), stop=(j == i))
                    last.then_inc(a_pv, 1)

            pe.wait_ge(s_wkt, 16)
            pe.wait_ge(p_qg, 1)
            for c in range(KC):
                for h in range(H):
                    o = (c * H + h) * NS
                    last = mm(ps[3][:, 0, o:o + NS], wkT[:, h, c * P:(c + 1) * P], qg[:, h, :], start=True, stop=True)
            last.then_inc(p_ab, 1)
            pe.wait_ge(a_o, H)
            pe.wait_ge(p_all, 1)

            with pe.Fori(0, NB) as b:
                pe.wait_ge(q_st, b * 4 + 3)
                pe.wait_ge(m_o, b)
                pe.wait_ge(ck_in, b * 16 + 16)
                for bank, lo, n in ((0, 384, 512), (1, 0, 384), (1, None, NS)):
                    o = 384 if lo is None else 0
                    for c in range(HP):
                        rhs = uT[:, U_KS + c, NP_:T] if lo is None else cK[:, c, lo:lo + n]
                        last = mm(ps[2][0:NS, bank, o:o + n], qw[:, c * 32:(c + 1) * 32], rhs, start=(c == 0), stop=(c == HP - 1))
                last.then_inc(w_sc, 1)
                for t in range(NPG + 1):
                    new = t == NPG
                    grp = t // 4
                    n = NS if new else P
                    if not new:
                        pe.wait_ge(pg_in[t % PR], b * 64 + (32 if t < PR else 64))
                        if t < 2:
                            pe.wait_ge(k_sq, b * NPG)
                        else:
                            pe.wait_ge(k_sq, b * NPG + (t - 1))
                        for c in range(KC):
                            last = mm(ps[0][:, t % 2, :], pgT[:, t % PR, c * P:(c + 1) * P], wK[:, c, :],
                                      start=(c == 0), stop=(c == KC - 1))
                        last.then_inc(k_raw, 1)
                    if t % 4 == 0:
                        pe.wait_ge(m_cp, b * 5 + max(grp - 1, 0))
                    o = (t % 4) * 64
                    bank = ps[1][0:n, grp % 2, :]
                    for c in range(KC):
                        lhs = uT[:, U_LAT + c, NP_:T] if new else pgT[:, t % PR, c * P:(c + 1) * P]
                        mm(bank[:, o:o + 32], lhs, qa[:, c * 32:(c + 1) * 32], start=(c == 0), stop=(c == KC - 1))
                    lhs = uT[MID, U_KR, NP_:T] if new else pgR[MID, t % PR, :]
                    last = mm(bank[:, o + 32:o + 64], lhs, qr[MID, :], start=True, stop=True)
                    if not new:
                        last.then_inc(r_used, 1)
                    else:
                        last.then_inc(m_sc, 1)
                pe.wait_ge(w_e, b + 1)
                pe.sem_inc(passed_t, 1)
                for t in range(NT_W):
                    lo = t * STR if t < 4 else 384 + (t - 4) * P
                    n = P if t < 8 else NS
                    last = pe.transpose(ps[2][0:n, 0, t * 32:(t + 1) * 32], Sw[:, lo:lo + n], C[0:NS, C_ID:C_ID + NS])
                last.then_inc(w_t, 1)
                pe.wait_ge(w_tc, b + 1)
                pe.wait_ge(cv_in, b * 32 + 32)
                for t in range(NT_W):
                    if t < 4:
                        lhs, rhs = Ew[0:STR, t, :], cVs[:, t, :]
                    elif t < 8:
                        lhs, rhs = Ew[:, t, :], cVr[:, t - 4, :]
                    else:
                        lhs, rhs = Ew[0:NS, t, :], vNew[:, :]
                    last = mm(ps[3][0:NS, 1, :], lhs, rhs, start=(t == 0), stop=(t == NT_W - 1))
                last.then_inc(w_pv, 1)
                pe.wait_ge(pl_in, b * (16 * NPG) + 16 * NPG)
                pe.wait_ge(m_es, b + 1)
                for t in range(NPG + 1):
                    lhs, rhs = (E[:, t, :], pgL[:, t, :]) if t < NPG else (E[0:NS, t, :], latNew[:, :])
                    mm(ps[3][0:NS, 0, 0:KVL], lhs, rhs, start=(t == 0), stop=(t == NPG))
                mm(ps[3][0:NS, 0, KVL:KVL + 1], es[:, :], C[:, C_ONE:C_ONE + 1], start=True, stop=True).then_inc(m_pv, 1)
                pe.wait_ge(m_cp, b * 5 + 4)
                pe.wait_ge(w_on, b + 1)
                pe.sem_inc(passed_t, 1)
                for c in range(HP):
                    last = pe.transpose(ps[1][:, 1, c * 32:(c + 1) * 32], On[:, KVL + c * P:KVL + (c + 1) * P], C[0:NS, C_ID:C_ID + NS])
                last.then_inc(w_tt, 1)
                pe.wait_ge(m_on, b + 1)
                pe.sem_inc(passed_t, 1)
                for c in range(KC):
                    last = pe.transpose(ps[2][:, 1, c * 32:(c + 1) * 32], On[:, c * P:(c + 1) * P], C[0:NS, C_ID:C_ID + NS])
                last.then_inc(m_tt, 1)

            pe.wait_ge(m_o, NB)
            for h in range(H):
                r = slice((h % 2) * HD, (h % 2) * HD + HD)
                for c in range(KC):
                    last = mm(ps[0][r, 0, (h // 2) * NS:(h // 2 + 1) * NS], wV[:, c, h * HD:(h + 1) * HD], oAbs[:, c, h, :],
                              start=(c == 0), stop=(c == KC - 1))
            last.then_inc(oa_mm, 1)
            pe_norms([g_oa, g_ob])
            pe.wait_ge(n_out, g_ob + 1)

            for m in range(KD):
                w = pe_weight(W_O + m)
                if m >= 2:
                    pe.wait_ge(wo_ev, m - 1)
                for k in range(KD):
                    for a in range(2):
                        last = mm(ps[m % 2][:, a, 0:HT], w[:, k * P:(k + 1) * P], aT[:, k, a * HT:(a + 1) * HT],
                                  start=(k == 0), stop=(k == KD - 1))
                last.then_inc(w_used, 1)
            pe_norms([g_f])
            pe.wait_ge(n_out, g_f + 1)
            with pe.Fori(0, KF // 2) as i:
                for j in range(2):
                    pe.wait_ge(gu_ev[j], i)
                    for z in range(2):
                        w = pe_weight(W_GU + 2 * j + z, i, 4)
                        for k in range(KD):
                            for a in range(2):
                                last = mm(ps[2 * j + z][:, a, 0:HT], w[:, k * P:(k + 1) * P], aT[:, k, a * HT:(a + 1) * HT],
                                          start=(k == 0), stop=(k == KD - 1))
                        last.then_inc(w_used, 1)
            for j in range(2):
                pe.wait_ge(gu_ev[j], KF // 2)
            with pe.Fori(0, KD // 2) as i:
                for j in range(2):
                    pe.wait_ge(dn_ev[j], i)
                    for z in range(2):
                        w = pe_weight(W_DN + 2 * j + z, i, 4)
                        for k in range(11):
                            kk = 11 * z + k
                            for a in range(2):
                                last = mm(ps[j][:, a, 0:HT], w[:, k * P:(k + 1) * P], hid[:, kk, a * HT:(a + 1) * HT],
                                          start=(kk == 0), stop=(kk == KF - 1))
                        last.then_inc(w_used, 1)
            pe_norms([g_p])
            pe.wait_ge(n_out, g_p + 1)
            pe.wait_ge(s_plt, 16)
            with pe.Fori(0, KD // 4) as i:
                for j in range(4):
                    w = pe_weight(W_PL + j, i, 4)
                    pe.wait_ge(pl_ev[j % 2], i * 2 + j // 2)
                    for k in range(KD):
                        for a in range(2):
                            mm(ps[2 * (j % 2)][:, a, 0:HT], w[:, k * P:(k + 1) * P], aT[:, k, a * HT:(a + 1) * HT],
                               start=(k == 0), stop=(k == KD - 1))
                    for k in range(2):
                        for a in range(2):
                            last = mm(ps[2 * (j % 2) + 1][:, a, 0:HT], w[:, (KD + k) * P:(KD + k + 1) * P],
                                      plT[:, k, a * HT:(a + 1) * HT], start=(k == 0), stop=(k == 1))
                    last.then_inc(w_used, 1)

        @block.vector
        def _(v):
            v.wait_ge(s_x, 16)
            v.wait_ge(s_g, 16)
            v.wait_ge(s_c, 16)
            dve_norms([g_x])
            v.wait_ge(in_ev, U_QS)
            for g in RUN1[:-1]:
                dve_scale(g)
            dve_scale(g_kr)
            v.wait_ge(in_ev, NIN + 5)
            dve_rope(g_kr)
            dve_norms(RUN2)
            v.wait_ge(n_rope, 1)
            v.wait_ge(s_wvs, 16)
            v.wait_ge(vs_mm, 5)
            v.tensor_copy(KT[MID, :, 0:NP_], uT[MID, U_KR:U_KR + 1, 0:NP_].broadcast_to([ROPE, H, NP_])).then_inc(kr_b, 1)
            v.wait_ge(kn_sq, 1)
            v.tensor_reduce(rkN[:, :], tmp[0:NS, 0, 0:512].rearrange("p (h d) -> p h d", h=H), AX.X, ALU.add).then_inc(kn_ss, 1)
            v.wait_ge(qb_ev, H)
            v.wait_ge(k_ev, H)
            dve_norms(RUN3)
            v.wait_ge(k_rt, 1)
            link(v.reciprocal(rkN[:, :], rkN[:, :]))
            for n in range(len(units) + 5):
                if n < len(units):
                    h, i = units[n]
                    w = (i + 1) * P
                    k = n % 4
                    mask = (C_MA if h < H else C_MB) + (3 - i) * P
                    v.wait_ge(a_s, n + 1)
                    if n >= 4:
                        v.wait_ge(a_t, n - 3)
                    v.tensor_tensor_reduce(pr[:, k, 0:w], ps[0][:, n % 2, 0:w], C[:, mask:mask + w],
                                           SC_A if h < H else SC_B, NEG * 4, ALU.add, ALU.max,
                                           st[:, 8 + k:9 + k]).then_inc(a_sm, 1)
                    v.wait_ge(a_sm, n + 1)
                    v.tensor_scalar(st[:, k:k + 1], st[:, 8 + k:9 + k], -1.0, None, ALU.mult).then_inc(a_nm, 1)
                if n >= 2 and n - 2 < len(units):
                    m = n - 2
                    k = m % 4
                    w = (units[m][1] + 1) * P
                    v.wait_ge(a_e, m + 1)
                    link(v.reciprocal(st[:, 12 + k:13 + k], st[:, 4 + k:5 + k]))
                    v.tensor_scalar(pr[:, k, 0:w], pr[:, k, 0:w], st[:, 12 + k:13 + k], None, ALU.mult).then_inc(a_p, 1)
                if n >= 5:
                    h, i = units[n - 5]
                    if i == 3 and h % 2 == 1:
                        c = h // 2
                        v.wait_ge(a_pv, n - 4)
                        v.tensor_copy(aT[:, c, 0:NP_], ps[2][:, c % 2, :]).then_inc(a_o, 1)
            v.wait_ge(n_rope, ropes_before[-1])
            v.tensor_scalar(qg[:, :, :], QT[LOW, :, NP_:T], G[LOW, G_K:G_K + 1], None, ALU.mult).then_inc(p_qg, 1)
            link(v.memset(S, NEG))
            link(v.memset(qw[:, :], 0.0))
            link(v.memset(qwAll, 0.0))
            link(v.tensor_copy(qrAll[MID, :, :].rearrange("p b (h q) -> p h b q", h=H),
                               QT[MID, :, NP_:T].rearrange("p h (b q) -> p h b q", q=NQ)))
            for z in range(2):
                r = slice(z * HD, (z + 1) * HD)
                link(v.tensor_copy(qwAll[r, :, :].rearrange("p b (c z q) -> p c z b q", c=HP, z=2)[:, :, z],
                                   uT[r, U_QS:U_QS + HP, NP_:T].rearrange("p c (b q) -> p c b q", q=NQ)))
            v.wait_ge(p_ab, 1)
            v.tensor_copy(qaAll.rearrange("p b (c q) -> p c b q", q=NQ),
                          ps[3][:, 0, :].rearrange("p (c b q) -> p c b q", b=NB, q=NQ)).then_inc(p_all, 1)

            before = chain["n"]
            with v.Fori(0, NB) as b:
                chain["base"], chain["n"] = b * LOOP_LINKS + before, 0
                v.wait_ge(w_sc, b + 1)
                v.wait_ge(q_st, b * 4 + 4)
                v.sem_inc(passed_v, 1)
                for j, (out, src, mask) in enumerate((
                        (Sw[:, 384:896], ps[2][0:NS, 0, :], C[0:NS, C_MW + 384:C_MW + 896]),
                        (Sw[:, 0:384], ps[2][0:NS, 1, 0:384], C[0:NS, C_MW:C_MW + 384]),
                        (Sw[:, 896:NKW], ps[2][0:NS, 1, 384:416], mNew[:, :]))):
                    last = v.tensor_tensor_reduce(out, src, mask, SC_B, NEG * 4, ALU.add, ALU.max, sm[:, j:j + 1])
                link(last)
                link(v.tensor_reduce(sm[:, 7:8], sm[:, 0:3], AX.X, ALU.max))
                v.tensor_scalar(sm[:, 5:6], sm[:, 7:8], -1.0, None, ALU.mult).then_inc(w_nm, 1)
                for t in range(NPG):
                    v.wait_ge(k_sq, b * NPG + (t + 1))
                    v.tensor_reduce(ssq[:, t * H:(t + 1) * H], sqK[:, t % 2, :].rearrange("p (h d) -> p h d", h=H), AX.X,
                                    ALU.add).then_inc(k_ss, 1)
                    if t % 4 == 3:
                        g = t // 4
                        v.wait_ge(r_used, b * NPG + (t + 1))
                        v.tensor_copy(sRaw[:, 4 * g:4 * g + 4, :], ps[1][:, g % 2, 0:256].rearrange("p (t c) -> p t c", c=64)).then_inc(m_cp, 1)
                v.wait_ge(m_sc, b + 1)
                link(v.tensor_tensor(sN[:, :].rearrange("p (h q) -> p h q", q=NQ),
                                     ps[1][0:NS, 0, 0:32].rearrange("p (h q) -> p h q", q=NQ),
                                     rkN[:, :].unsqueeze(2).broadcast_to([NS, H, NQ]), ALU.mult))
                link(v.tensor_tensor(sN[:, :], ps[1][0:NS, 0, 32:64], sN[:, :], ALU.add))
                v.tensor_tensor(S[0:NS, NPG, :], sN[:, :], C[0:NS, bass.ds(b * 32 + C_MN, 32)], ALU.add).then_inc(m_cp, 1)
                v.wait_ge(k_rt, b + 2)
                link(v.reciprocal(ssq[:, :], ssq[:, :]))
                v.wait_ge(m_cp, b * 5 + 5)
                link(v.tensor_tensor(S[:, 0:NPG, :].rearrange("p t (h q) -> p t h q", q=NQ),
                                     sRaw[:, :, 0:32].rearrange("p t (h q) -> p t h q", q=NQ),
                                     ssq[:, :].rearrange("p (t h) -> p t h", h=H).unsqueeze(3).broadcast_to([P, NPG, H, NQ]), ALU.mult))
                link(v.tensor_tensor(S[:, 0:NPG, :], S[:, 0:NPG, :], sRaw[:, :, 32:64], ALU.add))
                v.tensor_reduce(mx[:, :], S.rearrange("p t c -> p c t"), AX.X, ALU.max).then_inc(m_mx, 1)
                v.wait_ge(w_e, b + 1)
                link(v.reciprocal(sm[:, 4:5], sm[:, 3:4]))
                v.wait_ge(m_ar, b + 1)
                v.tensor_tensor(S, S, mxa[:, :].unsqueeze(1).broadcast_to([P, NPG + 1, 32]), ALU.subtract).then_inc(m_sub, 1)
                v.wait_ge(m_e, b + 1)
                v.tensor_reduce(es[:, :], E.rearrange("p t c -> p c t"), AX.X, ALU.add).then_inc(m_es, 1)
                v.wait_ge(w_pv, b + 1)
                v.tensor_scalar(On[:, KVL:], ps[3][0:NS, 1, :], sm[:, 4:5], None, ALU.mult).then_inc(w_on, 1)
                v.wait_ge(m_pv, b + 1)
                link(v.reciprocal(sm[:, 6:7], ps[3][0:NS, 0, KVL:KVL + 1]))
                v.tensor_scalar(On[:, 0:KVL], ps[3][0:NS, 0, 0:KVL], sm[:, 6:7], None, ALU.mult).then_inc(m_on, 1)
                v.wait_ge(w_tt, b + 1)
                for z in range(2):
                    r = slice(z * HD, (z + 1) * HD)
                    o = ps[1][r, 1, 0:160].rearrange("p (c n) -> p c n", n=40)[:, :, 4 * z:4 * z + NQ]
                    last = v.tensor_copy(aT[r, HP:KD, bass.ds(b * NQ + NP_, NQ)], o)
                last.then_inc(w_o, 1)
                v.wait_ge(m_tt, b + 1)
                v.tensor_copy(oAbs[:, :, :, bass.ds(b * NQ, NQ)].rearrange("p c h q -> p (c h) q"),
                              ps[2][:, 1, 0:64].rearrange("p (x q) -> p x q", q=NQ)).then_inc(m_o, 1)
                assert chain["n"] == LOOP_LINKS, chain
            chain["base"], chain["n"] = before + NB * LOOP_LINKS, 0
            v.wait_ge(oa_ev, 1)
            dve_norms([g_oa, g_ob])
            for m in range(KD):
                v.wait_ge(w_used, W_O + m + 1)
                v.tensor_tensor(hT[:, m, :].rearrange("p (a n) -> p a n", a=2), ps[m % 2][:, :, 0:HT],
                                hT[:, m, :].rearrange("p (a n) -> p a n", a=2), ALU.add).then_inc(wo_ev, 1)
            v.wait_ge(wo_ev, KD)
            dve_norms([g_f])
            v.wait_ge(out_s, 80)
            with v.Fori(0, KF // 2) as i:
                for j in range(2):
                    v.wait_ge(gu_act, i * 2 + (j + 1))
                    v.tensor_tensor(hid[:, bass.ds(i * 2 + j, 1), :].rearrange("p t (a n) -> p (t a) n", a=2),
                                    ps[2 * j + 1][:, :, 0:HT], tmp[:, j, :].rearrange("p (a n) -> p a n", a=2),
                                    ALU.mult).then_inc(gu_ev[j], 1)
            with v.Fori(0, KD // 2) as i:
                for j in range(2):
                    v.wait_ge(w_used, i * 4 + (W_DN + 2 * j + 2))
                    h2 = hT[:, bass.ds(i * 2 + j, 1), :].rearrange("p t (a n) -> p (t a) n", a=2)
                    v.tensor_tensor(h2, ps[j][:, :, 0:HT], h2, ALU.add).then_inc(dn_ev[j], 1)
            for j in range(2):
                v.wait_ge(dn_ev[j], KD // 2)
            dve_norms([g_p])
            with v.Fori(0, KD // 4) as i:
                for j in range(4):
                    v.wait_ge(pl_act, i * 4 + (j + 1))
                    t2 = tmp[:, j % 2, :].rearrange("p (a n) -> p a n", a=2)
                    v.tensor_tensor(t2, ps[2 * (j % 2) + 1][:, :, 0:HT], t2, ALU.mult).then_inc(pl_mul, 1)
                    v.wait_ge(pl_mul, i * 4 + (j + 1))
                    h2 = hT[:, bass.ds(i * 4 + j, 1), :].rearrange("p t (a n) -> p (t a) n", a=2)
                    v.tensor_tensor(h2, t2, h2, ALU.add).then_inc(pl_ev[j % 2], 1)


def constants():
    import numpy as np
    c = np.zeros((P, NC_), np.float32)
    i = np.arange(P)
    c[:, C_ONE:C_ONE + P] = 1
    c[:, C_B64:C_B64 + P] = i[:, None] // 64 == i[None] // 64
    b96 = c[:, C_B96:C_B96 + P]
    b96[:64, :64] = 1 / 64
    b96[64:96, 64:96] = 1 / 32
    c[:, C_ID:C_ID + P] = np.eye(P)
    pos = np.concatenate([np.arange(NP_), np.tile(PAST + np.arange(NQ), NB)]).astype(np.float32)

    def rope(rot, cs, sn, starts, half, theta):
        inv = np.float32(theta) ** (-np.arange(half, dtype=np.float32) / np.float32(half))
        ang = pos[None] * inv[:, None]
        c[:, cs:cs + T] = 1
        for s0 in starts:
            for j in range(half):
                a, b = s0 + j, s0 + half + j
                c[b, rot + a] = -1
                c[a, rot + b] = 1
                c[a, cs:cs + T] = c[b, cs:cs + T] = np.cos(ang[j])
                c[a, sn:sn + T] = c[b, sn:sn + T] = np.sin(ang[j])

    rope(C_RS, C_CS, C_SS, (0, 64), 8, 500000.0)
    rope(C_RQ, C_CQ, C_SQ, (64,), 16, 10000.0)

    def multiplicity(dist):
        n = sum((dist >= 0) & (dist <= w) & (dist % d == 0) for w, d in ((128, 1), (512, 4), (2048, 16)))
        return np.where(n > 0, np.log(np.maximum(n, 1)) / SC_B, NEG)

    for blk in range(4):
        dist = (3 - blk) * P + i[:, None] - i[None]
        c[:, C_MA + blk * P:C_MA + (blk + 1) * P] = np.where(dist >= 0, 0, NEG)
        c[:, C_MB + blk * P:C_MB + (blk + 1) * P] = multiplicity(dist)
    q = np.arange(NQ)
    older = 16 * np.arange(STR)[None] + np.arange(4)[:, None]
    key = np.concatenate([older.ravel(), np.arange(PAST - REC, PAST)])
    c[:NS, C_MW:C_MW + 896] = np.tile(multiplicity(PAST + q[:, None] - key[None]), (H, 1))
    for b in range(NB):
        same_t = (np.arange(NS)[None] // NQ == b)
        dist_t = q[:, None] - np.arange(NS)[None] % NQ
        same = (np.arange(NS)[:, None] // NQ == b)
        dist = q[None] - np.arange(NS)[:, None] % NQ
        c[:, C_MN + b * 32:C_MN + (b + 1) * 32] = NEG
        c[:NS, C_MN + b * 32:C_MN + (b + 1) * 32] = np.tile(np.where(same & (dist >= 0), 0, NEG), (1, H))
        c[:NS, C_MX + b * 32:C_MX + (b + 1) * 32] = np.tile(np.where(same_t, multiplicity(dist_t), NEG), (H, 1))
    return c


def kernel(**inputs):
    import numpy as np
    import concourse.bacc as bacc
    from concourse.bass_utils import run_bass_kernel_spmd as run

    a = {k: np.asarray(v) for k, v in inputs.items()}

    def tiles(w, width, start=0):
        k = w.shape[0] // P
        return w[:, start:start + width].reshape(k, P, width).transpose(1, 0, 2).reshape(P, k * width)

    def feat(x):
        return x.T.reshape(-1, P, x.shape[0]).transpose(1, 0, 2)

    w_in, w_kvb = a["w_in"][0], a["w_kvb"][0].reshape(KVL, H, 2, NOPE)
    a_end = QL + KVL + ROPE
    starts = [P * m for m in range(8)] + [a_end - HQ] + [a_end + P * m for m in range(8)]
    gate, up = a["w_gate"][0], a["w_up"][0]
    down = a["w_down"][0]
    gains = np.zeros((P, NG), np.float32)
    for name, col in (("g_attn", G_ATT), ("g_ffn", G_FFN), ("g_ple", G_PLE), ("b_ple_gate", B_PLE), ("g_qa", G_QA),
                      ("g_kva", G_KVA), ("g_oa", G_OA), ("g_ob", G_OB)):
        g = a[name][0].reshape(-1, P).T
        gains[:, col:col + g.shape[1]] = g
    gains[:NOPE, G_Q], gains[NOPE:HQ, G_Q] = a["g_qn"][0], a["g_qr"][0]
    gains[:NOPE, G_K], gains[NOPE:HQ, G_K] = a["g_kn"][0], a["g_kr"][0]
    for name, col in (("g_qs", G_QS), ("g_ks", G_KS)):
        gains[:HD, col] = gains[HD:, col] = a[name][0]
    gains[:, G_EPS] = EPS

    lat = a["cache_latent"][0]
    ck = a["cache_swa_k"][0].reshape(NB, PAST, HP, P)
    old = np.arange(PAST - REC).reshape(STR, 16).T
    order = np.concatenate([old[4:].ravel(), old[:4].ravel(), np.arange(PAST - REC, PAST)])
    tok = lambda p, s: np.concatenate([p.reshape(NP_, -1), s.reshape(NS, -1)])
    arr = dict(
        x=feat(tok(a["x_prompt"], a["x_sample"])),
        cst=constants(),
        gains=gains,
        win=np.stack([tiles(w_in, P, s) for s in starts]),
        wvs=w_in[:, a_end + 1024:].reshape(KD, P, 512).transpose(1, 0, 2),
        wqb=np.stack([tiles(a["w_qb"][0], HQ, HQ * h) for h in range(H)]),
        wk=w_kvb[:, :, 0].reshape(KC, P, 512).transpose(1, 0, 2),
        wv=w_kvb[:, :, 1].reshape(KC, P, 512).transpose(1, 0, 2),
        wkt=w_kvb[:, :, 0].transpose(2, 1, 0),
        wo=np.stack([tiles(a["w_o"][0], P, P * m) for m in range(KD)]),
        wgu=np.stack([tiles(w, P, P * m) for m in range(KF) for w in (gate, up)]),
        wdn=np.stack([tiles(down[z * 11 * P:(z + 1) * 11 * P], P, P * m) for m in range(KD) for z in range(2)]),
        wpl=np.stack([np.concatenate([tiles(a["w_ple_gate"][0], P, P * m), tiles(a["w_ple_proj"][0], P, P * m)], 1)
                      for m in range(KD)]),
        plt=feat(tok(a["p_prompt"], a["p_sample"])),
        pgt=lat.reshape(POOL, PAGE, KC, P).transpose(0, 3, 2, 1).reshape(POOL, P, KC * PAGE),
        pgk=a["cache_krope"][0].transpose(0, 2, 1),
        pgl=lat,
        ck=ck[:, order].transpose(0, 2, 3, 1),
        cv=a["cache_swa_v"][0].reshape(NB, PAST, 512),
        pt=a["page_table"].reshape(1, NB * NPG),
    )
    arr = {k: np.ascontiguousarray(v) for k, v in arr.items()}
    outs = dict(y=(KD, P, T), o_lat=(P, KC, T), o_kr=(ROPE, T), o_ks=(P, HP, T), o_vs=(NP_, 512),
                o_ck=(NB, HP, P, PAST), o_cv=(NB, PAST, 512))
    nc = bacc.Bacc("TRN2", target_bir_lowering=False, num_devices=1)
    args = [nc.dram_tensor(f"in_{k}", v.shape, mybir.dt.from_np(v.dtype), kind="ExternalInput").ap() for k, v in arr.items()]
    args += [nc.dram_tensor(f"out_{k}", s, F32, kind="ExternalOutput").ap() for k, s in outs.items()]
    build(nc, *args)
    r = run(nc, [{f"in_{k}": v for k, v in arr.items()}], core_ids=[0]).results[0]
    o = {k: np.asarray(r[f"out_{k}"]) for k in outs}

    def rows(x, width):
        x = x.reshape(width, T).T
        return x[:NP_], x[NP_:]

    yp, ys = rows(o["y"], D)
    lp, ls = rows(o["o_lat"].transpose(1, 0, 2), KVL)
    kp, ks = rows(o["o_kr"], ROPE)
    sp, ss = rows(o["o_ks"].transpose(1, 0, 2), 512)
    back = np.empty(PAST, np.int64)
    back[order] = np.arange(PAST)
    kold = o["o_ck"].reshape(NB, 512, PAST)[:, :, back[NQ:]].transpose(0, 2, 1)
    swk = np.concatenate([kold, ss.reshape(NB, NQ, 512)], 1)
    return (yp.reshape(1, NP_, D), ys.reshape(NB, NQ, D), lp.reshape(1, 1, NP_, KVL), kp.reshape(1, 1, NP_, ROPE),
            sp.reshape(1, 1, NP_, H, HD), o["o_vs"].reshape(1, 1, NP_, H, HD), ls.reshape(1, NB, NQ, KVL),
            ks.reshape(1, NB, NQ, ROPE), swk.reshape(1, NB, PAST, H, HD), o["o_cv"].reshape(1, NB, PAST, H, HD))
```

```python
from contextlib import ExitStack

import concourse.bass as bass
from concourse import mybir

F32 = mybir.dt.float32
F32R = mybir.dt.float32r
I32 = mybir.dt.int32
ACT = mybir.ActivationFunctionType
ALU = mybir.AluOpType
AX = mybir.AxisListType
MAX_ALL = bass.bass_isa.ReduceOp.max

P = 128
D = 1024
KD = D // P
NP_ = 512
NB, NQ = 8, 4
NS = NB * NQ
T = NP_ + NS
HT = T // 2
H = 8
NOPE, ROPE, HQ = 64, 32, 96
QL, KVL = 768, 256
KQ, KC = QL // P, KVL // P
DFF = 2816
KF = DFF // P
HD = 64
HP = H // 2
PAST, PAGE = 2048, 128
NPG = PAST // PAGE
POOL = 160
EPS = 1e-6
NEG = -1e30
SC_A = HQ ** -0.5
SC_B = HD ** -0.5
NIN = 21
NU = 17
U_LAT, U_KR, U_QS, U_KS = 6, 8, 9, 13
HALVES = (12, 10)
SLOT = HALVES[0] * P
REC = 512
STR = (PAST - REC) // 16
NKW = 896 + NS
EXP_AT, TURN_AT = 2, 12
FIRST = 1
LOOP_LINKS = 9
NT_W = 9
PR = 8

C_ONE, C_RS, C_RQ, C_ID, C_Z = (i * P for i in range(5))
C_MA = 5 * P
Z_64, Z_96, Z_CQ, Z_LAT = (C_Z + 32 * i for i in range(4))
C_MB = C_MA + 512
C_CS = C_MB + 512
C_SS = C_CS + T
C_CQ = C_SS + T
C_SQ = C_CQ + T
C_MN = C_SQ + T
C_MW = C_MN + NB * 32
C_MX = C_MW + 896
NC_ = C_MX + NB * 32
C_W, W_ROW = C_MW, 32
G_ATT, G_FFN, G_PLE, B_PLE, G_QA, G_KVA, G_Q, G_K, G_QS, G_KS, G_OA, G_OB, G_EPS, NG = (
    0, 8, 16, 24, 32, 38, 40, 41, 42, 43, 44, 48, 52, 53)

W_IN, W_QB = 0, NIN
W_O = W_QB + H
W_GU = W_O + KD
W_DN = W_GU + 2 * HALVES[0]
W_GU2 = W_DN + KD
W_DN2 = W_GU2 + 2 * HALVES[1]
W_PL = W_DN2 + KD


def build(nc, x, cst, gains, win, wqb, wk, wv, wkt, wo, wgu, wdn, wdn2, wpl, plt, pgt, pgk, pgl, ck, cv, pt,
          y, o_lat, o_kr, o_ks, o_vs, o_ck, o_cv):
    with ExitStack() as ctx:
        place = [-(-nc.sbuf_base // 32) * 32]

        def at(name, shape, off, dt=F32):
            return nc.alloc_sbuf_tensor_at(name, shape, dt, offset=off)

        def room(cols):
            off = place[0]
            place[0] = off + -(-cols * 4 // 32) * 32
            assert place[0] <= nc.sbuf_usable_end, place[0]
            return off

        def sb(name, shape, dt=F32):
            n = 1
            for x in shape[1:]:
                n *= x
            return at(name, shape, room(n), dt)

        def sem(name):
            return ctx.enter_context(nc.semaphore(name))

        hT = sb("hT", [P, KD, T])
        o_a, o_b, o_big = room(KD * T), room(KD * T), room(25 * T)
        aT = at("aT", [P, KD, T], o_a)
        aHi = at("aHi", [P, KD, T], o_a, F32R)
        aLo = at("aLo", [P, KD, T], o_b, F32R)
        big = at("big", [P, 25 * T], o_big)
        uT = big[:, 0:NU * T].rearrange("p (t n) -> p t n", n=T)
        QT = big[:, NU * T:].rearrange("p (t n) -> p t n", n=T)
        hidHi = at("hidHi", [P, HALVES[0], T], o_big, F32R)
        hidLo = at("hidLo", [P, HALVES[0], T], o_big + HALVES[0] * T * 4, F32R)
        plHi = at("plHi", [P, 2, T], o_big, F32R)
        plLo = at("plLo", [P, 2, T], o_big + 2 * T * 4, F32R)
        pgT = big[:, 0:PR * 256].rearrange("p (s n) -> p s n", s=PR)
        pgR = big[:, PR * 256:PR * 384].rearrange("p (s n) -> p s n", s=PR)
        cK = big[:, NU * T:NU * T + HP * 896].rearrange("p (c n) -> p c n", c=HP)
        kv1 = at("kv1", [P, H * T], o_b)
        KT = kv1[:, :].rearrange("p (t n) -> p t n", n=T)
        pgL = kv1[:, 0:NPG * KVL].rearrange("p (t n) -> p t n", n=KVL)
        kv2 = sb("kv2", [P, 8 * 512])
        vA = kv2[:, 0:2048].rearrange("p (t n) -> p t n", n=512)
        vB = kv2[:, 2048:4096].rearrange("p (t n) -> p t n", n=512)
        wkT = kv2[0:NOPE, 0:2048].rearrange("p (h n) -> p h n", h=H)
        cVr = kv2[:, 0:2048].rearrange("p (j n) -> p j n", j=4)
        cVs = kv2[0:STR, 2048:4096].rearrange("p (r n) -> p r n", r=4)
        plT = kv2[:, 0:2 * T].rearrange("p (t n) -> p t n", n=T)
        vNew = sb("vNew", [NS, 512])
        latNew = sb("latNew", [NS, KVL])
        ring = sb("ring", [P, 2, SLOT])
        o_split = room(4 * SLOT)
        wHi = at("wHi", [P, 2, SLOT], o_split, F32R)
        wLo = at("wLo", [P, 2, SLOT], o_split + 2 * SLOT * 4, F32R)
        C = sb("C", [P, NC_])
        G = sb("G", [P, NG])
        wK = sb("wK", [P, KC, 512])
        wV = sb("wV", [P, KC, 512])
        sq = sb("sq", [P, 2, T])
        R = sb("R", [P, 2, T])
        tmp = sb("tmp", [P, 2, T])
        att = at("att", [P, 4, 512], o_split)
        wkHi, wkLo = (at(n, [P, KC, 512], o_split + (2048 + 1024 * i) * 4, F32R) for i, n in enumerate(("wkHi", "wkLo")))
        pgHi, pgLo = (at(n, [P, 2, KVL], o_split + (4096 + 512 * i) * 4, F32R) for i, n in enumerate(("pgHi", "pgLo")))
        pr = att
        sqK = att[:, 0:2, :]
        sRaw = att[:, 2:4, :].rearrange("p a (t c) -> p (a t) c", c=64)
        S = sq[:, :, :].rearrange("p a n -> p (a n)")[:, 0:544].rearrange("p (t c) -> p t c", c=32)
        E = sq[:, :, :].rearrange("p a n -> p (a n)")[:, 544:1088].rearrange("p (t c) -> p t c", c=32)
        Rf = R[:, :, :].rearrange("p a n -> p (a n)")
        prT = at("prT", [P, 2, 512], o_split + 5120 * 4)
        Ew = Rf[:, 0:288].rearrange("p (t c) -> p t c", c=32)
        qrAll = Rf[:, 576:832].rearrange("p (b c) -> p b c", b=NB)
        qwAll = Rf[:, 832:1088].rearrange("p (b c) -> p b c", b=NB)
        tf = tmp[:, :, :].rearrange("p a n -> p (a n)")
        qaAll = tf[:, 0:512].rearrange("p (b c) -> p b c", b=NB)
        oAbs = tf[:, 512:1024].rearrange("p (c h n) -> p c h n", c=KC, h=H)
        qa = sb("qa", [P, 64])
        qr = sb("qr", [P, 32])
        qw = sb("qw", [P, 160])
        Sw = C[0:NS, C_CS:C_CS + NKW]
        On = C[0:NS, C_CQ:C_CQ + KVL + 512]
        mNew = sb("mNew", [NS, 32])
        sm = sb("sm", [NS, 8])
        qg = sb("qg", [NOPE, H, NS])
        ssq = sb("ssq", [P, P])
        rkN = sb("rkN", [NS, H])
        sN = sb("sN", [NS, 32])
        mx = sb("mx", [P, 32])
        mxa = sb("mxa", [P, 32])
        es = sb("es", [P, 32])
        warm = sb("warm", [P, 1])
        st = sb("st", [P, 16])
        ptab = sb("ptab", [1, NB * NPG], I32)

        ps = [ctx.enter_context(nc.psum_tensor(f"ps{i}", [P, 2, 512], F32)) for i in range(4)]

        s_x = [sem(f"x_in{k}") for k in range(KD // 2)]
        s_c, s_c2, s_g, s_wk, s_wkt, s_plt, s_pt = (sem(n) for n in (
            "const_in", "tables_in", "gains_in", "wkv_in", "wkt_in", "plt_in", "ptab_in"))
        w_in_ = [sem(f"w_in{i}") for i in range(2)]
        w_hi, w_lo = sem("w_hi"), sem("w_lo")
        n_tmp, n_hi, n_lo = sem("norm_tmp"), sem("norm_hi"), sem("norm_lo")
        h_tmp, h_hi, h_lo, pl_hi, pl_lo = (sem(n) for n in ("hid_tmp", "hid_hi", "hid_lo", "plt_hi", "plt_lo"))
        cq_hi, cq_lo = sem("cq_hi"), sem("cq_lo")
        wk_hi, wk_lo, p_hi, p_lo = (sem(n) for n in ("wk_hi", "wk_lo", "page_hi", "page_lo"))
        w_used = sem("unit_done")
        n_acc, n_clr = sem("squares_added"), sem("squares_cleared")
        n_rc, n_bc = sem("norm_reciprocal"), sem("norm_spread")
        n_sq, n_squ, n_rt, n_out, n_rot, n_nc, n_rope = (sem(n) for n in (
            "norm_sq", "norm_summed", "norm_root", "norm_out", "rot_mm", "rope_cos", "rope_out"))
        vs_mm, vs_ev, in_ev, qb_ev, k_mm, k_ev, v_mm, v_ev = (sem(n) for n in (
            "vs_mm", "vs_ev", "in_ev", "qb_ev", "k_mm", "k_ev", "v_mm", "v_ev"))
        kr_b, tn_mm, tn_ev, kn_sq, kn_ss = (sem(n) for n in (
            "krope_spread", "latnew_mm", "latnew_ev", "knew_sq", "knew_ssq"))
        a_s, a_sm, a_e, a_p, a_t, a_tc, a_pv, a_o, a_nm = (sem(n) for n in (
            "att_scores", "att_max", "att_exp", "att_probs", "att_turned", "att_turned_sb", "att_pv", "att_out",
            "att_negmax"))
        dve = sem("dve_chain")
        p_read = sem("prep_read")
        p_qg, p_ab, p_all = (sem(n) for n in ("prep_qg", "prep_absorb_mm", "prep_all"))
        q_st, k_raw, k_sq, k_ss, r_used, m_sc, m_cp, w_sc = (sem(n) for n in (
            "queries_staged", "kraw_mm", "kraw_sq", "kraw_ssq", "page_used", "mla_scores", "mla_scores_cp",
            "swa_scores"))
        k_rt, m_mx, m_ar, m_sub, m_e, m_es, m_pv, m_o = (sem(n) for n in (
            "key_root", "mla_max", "mla_allmax", "mla_shifted", "mla_exp", "mla_expsum", "mla_pv", "mla_out"))
        w_nm, w_e, w_t, w_tc, w_pv, w_on, w_tt, w_o, m_on, m_tt = (sem(n) for n in (
            "swa_negmax", "swa_exp", "swa_turned", "swa_turned_sb", "swa_pv", "swa_normed", "swa_out_turned", "swa_out",
            "mla_normed", "mla_out_turned"))
        pg_in = [sem(f"page_in{i}") for i in range(PR)]
        pl_in, ck_in, cv_in = sem("pages_in"), sem("ck_in"), sem("cv_in")
        passed, passed_v, passed_t = sem("pool_passed"), sem("dve_passed"), sem("pe_passed")
        oa_mm, oa_ev = sem("oa_mm"), sem("oa_ev")
        wo_ev, gu_act, pl_act, pl_mul = (sem(n) for n in ("wo_ev", "silu", "ple_gate", "ple_gated"))
        gu_ev, dn_ev, pl_ev = ([sem(f"{n}{j}") for j in range(2)] for n in ("gateup_ev", "down_ev", "ple_ev"))
        out_c, out_s, out_y = sem("copies_out"), sem("states_out"), sem("y_out")

        def cm(off, rows=slice(0, P), n=P):
            return C[rows, off:off + n]

        FULL, LO, MID = slice(0, P), slice(0, HQ), slice(NOPE, HQ)
        groups = []

        def group(tiles, rows, gain, n=None, z=None, w=T, rope=None, split=None, acc=False):
            groups.append(dict(src=tiles, dst=tiles, rows=rows, n=n, gain=gain, z=z, w=w, rope=rope, split=split, acc=acc))
            return len(groups) - 1

        a_split = (aHi, aLo)
        g_x = group([hT[:, k, :] for k in range(KD)], FULL, G_ATT, D, split=a_split)
        g_cq = group([uT[:, k, :] for k in range(KQ)], FULL, G_QA, z=Z_CQ)
        g_lat = group([uT[:, U_LAT + k, :] for k in range(KC)], FULL, G_KVA, z=Z_LAT)
        g_kr = group([uT[MID, U_KR, :]], MID, G_K, z=Z_96, rope=(C_RQ, C_CQ, C_SQ))
        g_qs = [group([uT[:, U_QS + i, :]], FULL, G_QS, z=Z_64, rope=(C_RS, C_CS, C_SS)) for i in range(HP)]
        g_ks = [group([uT[:, U_KS + i, :]], FULL, G_KS, z=Z_64, rope=(C_RS, C_CS, C_SS)) for i in range(HP)]
        g_qh = [group([QT[LO, h, :]], LO, G_Q, z=Z_96, rope=(C_RQ, C_CQ, C_SQ)) for h in range(H)]
        LOW = slice(0, NOPE)
        g_kh = [group([KT[LOW, h, 0:NP_]], LOW, G_K, z=Z_96, w=NP_) for h in range(H)]
        g_oa = group([aT[:, k, :] for k in range(HP)], FULL, G_OA, H * HD, split=a_split)
        g_ob = group([aT[:, HP + k, :] for k in range(HP)], FULL, G_OB, H * HD, split=(aHi[:, HP:KD, :], aLo[:, HP:KD, :]))
        g_f = group([hT[:, k, :] for k in range(KD)], FULL, G_FFN, D, split=a_split, acc=True)
        g_p = group([hT[:, k, :] for k in range(KD)], FULL, G_PLE, D, split=a_split, acc=True)
        packs = [[g_x], [g_cq, g_lat, g_kr], g_qs + g_ks, g_qh, g_kh, [g_oa], [g_ob], [g_f], [g_p]]
        P_X, P_IN, P_S, P_QH, P_KH, P_OA, P_OB, P_F, P_P = range(len(packs))
        pack_of = {g: (p, t) for p, gs in enumerate(packs) for t, g in enumerate(gs)}
        tiles_before = [sum(len(g["src"]) for g in groups[:i]) for i in range(len(groups) + 1)]
        ropes_before = [sum(g["rope"] is not None for g in groups[:i]) for i in range(len(groups) + 1)]
        sums_before = [sum(1 if g["acc"] else len(g["src"]) for g in groups[:i]) for i in range(len(groups) + 1)]
        accs_before = [sum(len(g["src"]) for g in groups[:i] if g["acc"]) for i in range(len(groups) + 1)]
        splits_before = [sum(len(g["src"]) for g in groups[:i] if g["split"]) for i in range(len(groups) + 1)]
        spreads_before = [sum(g["z"] is not None for g in groups[:i]) for i in range(len(groups) + 1)]

        def spread_pair(g):
            p, t = pack_of[g]
            return ps[3 - t % 2] if p == P_KH else ps[3]

        def sum_rows(p):
            return slice(0, P) if groups[packs[p][0]]["z"] is None else slice(W_ROW, W_ROW + 2 * len(packs[p]))

        def norm_squares(g):
            q = groups[g]
            rows, w = q["rows"], q["w"]
            for j, src in enumerate(q["src"]):
                k = sums_before[g] + j
                if g == g_x and j % 2 == 0:
                    nc.scalar.wait_ge(s_x[j // 2], 16)
                if k >= 2:
                    nc.scalar.wait_ge(n_squ, k - 1)
                nc.scalar.activation(sq[rows, k % 2, 0:w], src, ACT.Square).then_inc(n_sq, 1)

        def acc_square(g, j, m=0):
            if isinstance(m, int) and m + j < 2:
                nc.scalar.wait_ge(n_squ, sums_before[g])
            else:
                nc.scalar.wait_ge(n_acc, m + (accs_before[g] + j - 1))
            src = hT[:, bass.ds(m + j, 1), :].rearrange("p t n -> p (t n)")
            nc.scalar.activation(sq[:, j % 2, :], src, ACT.Square).then_inc(n_sq, 1)

        def acc_clear(g):
            nc.vector.memset(R[:, 1 - pack_of[g][0] % 2, :], 0.0).then_inc(n_clr, 1)

        def dve_accumulate(g, j, m=0):
            acc = R[:, 1 - pack_of[g][0] % 2, :]
            nc.vector.wait_ge(n_clr, [x for x in range(len(groups)) if groups[x]["acc"]].index(g) + 1)
            nc.vector.wait_ge(n_acc, m + (accs_before[g] + j))
            nc.vector.wait_ge(n_sq, m + (tiles_before[g] + j + 1))
            nc.vector.tensor_tensor(acc, sq[:, j % 2, :], acc, ALU.add).then_inc(n_acc, 1)

        def norm_root(p):
            g, w, rows = packs[p][-1], groups[packs[p][-1]]["w"], sum_rows(p)
            nc.scalar.wait_ge(n_squ, sums_before[g + 1])
            if p >= 2:
                nc.scalar.wait_ge(n_out, packs[p - 1][0])
            scale = 1.0 / groups[g]["n"] if groups[g]["n"] else 1.0
            nc.scalar.activation(R[rows, p % 2, 0:w].rearrange("p (a n) -> p a n", a=2),
                                 ps[2][rows, :, 0:w // 2], ACT.Sqrt, scale=scale,
                                 bias=G[rows, G_EPS:G_EPS + 1]).then_inc(n_rt, 1)

        def act_hi(g):
            q = groups[g]
            for j in range(len(q["src"])):
                k = splits_before[g] + j
                nc.scalar.wait_ge(n_tmp, k + 1)
                nc.scalar.activation(q["split"][0][:, j, :], tmp[:, k % 2, :], ACT.Copy).then_inc(n_hi, 1)

        def sqrt_table():
            nc.scalar.activation(warm[:, :], G[:, G_EPS:G_EPS + 1], ACT.Sqrt)

        def act_norm_split(p, between=None):
            if not groups[packs[p][0]]["acc"]:
                norm_squares(packs[p][0])
            norm_root(p)
            if between:
                between()
            act_hi(packs[p][0])

        def dve_lo(g, j):
            q = groups[g]
            k = splits_before[g] + j
            nc.vector.wait_ge(n_hi, k + 1)
            nc.vector.tensor_tensor(q["split"][1][:, j, :], tmp[:, k % 2, :], q["split"][0][:, j, :].bitcast(F32),
                                    ALU.subtract).then_inc(n_lo, 1)

        def act_weight(u, width, i=0):
            nc.scalar.wait_ge(w_in_[u % 2], i * 8 + 16 * (u // 2 + 1))
            if u >= 2:
                nc.scalar.wait_ge(w_used, i + (u - 1))
            nc.scalar.activation(wHi[:, u % 2, 0:width], ring[:, u % 2, 0:width], ACT.Copy).then_inc(w_hi, 1)

        def dve_weight(u, width, i=0):
            nc.vector.wait_ge(w_hi, i + (u + 1))
            nc.vector.tensor_tensor(wLo[:, u % 2, 0:width], ring[:, u % 2, 0:width], wHi[:, u % 2, 0:width].bitcast(F32),
                                    ALU.subtract).then_inc(w_lo, 1)

        def pe_norm(g):
            q, (p, t) = groups[g], pack_of[g]
            rows, hw, out = q["rows"], q["w"] // 2, sum_rows(p)
            if t == 0 and p >= 1:
                nc.tensor.wait_ge(n_rt, p)
            ones = C[rows, C_ONE:C_ONE + P] if q["z"] is None else C[rows, q["z"] + 15 - 2 * t:q["z"] + 15 - 2 * t + out.stop - out.start]
            if q["acc"]:
                nc.tensor.wait_ge(n_acc, accs_before[g + 1])
                for a in range(2):
                    last = nc.tensor.matmul(ps[2][out, a, 0:hw], ones, R[:, 1 - p % 2, a * hw:(a + 1) * hw],
                                            start=True, stop=True)
                last.then_inc(n_squ, 1)
                return
            for j in range(len(q["src"])):
                k = tiles_before[g] + j
                nc.tensor.wait_ge(n_sq, k + 1)
                for a in range(2):
                    last = nc.tensor.matmul(ps[2][out, a, 0:hw], ones, sq[rows, k % 2, a * hw:(a + 1) * hw],
                                            start=(j == 0 and t == 0), stop=(j == len(q["src"]) - 1 and g == packs[p][-1]))
                last.then_inc(n_squ, 1)

        def pe_spread(g):
            q, (p, t) = groups[g], pack_of[g]
            rows, hw, src = q["rows"], q["w"] // 2, sum_rows(p)
            nc.tensor.wait_ge(n_rc, p + 1)
            nc.tensor.wait_ge(n_out, g - (p == P_KH and t > 0))
            for a in range(2):
                last = nc.tensor.matmul(spread_pair(g)[rows, a, 0:hw], C[src, C_W + t * P + rows.start:C_W + t * P + rows.stop],
                                        R[src, p % 2, a * hw:(a + 1) * hw], start=True, stop=True)
            last.then_inc(n_bc, 1)

        def pe_rot(g):
            q = groups[g]
            rows, w, i = q["rows"], q["w"], ropes_before[g]
            nc.tensor.wait_ge(n_out, g + 1)
            if i >= 1:
                nc.tensor.wait_ge(n_rope, i)
            for a in range(2):
                last = nc.tensor.matmul(ps[1][rows, a, 0:HT], C[rows, q["rope"][0] + rows.start:q["rope"][0] + rows.stop],
                                        q["dst"][0][:, a * HT:(a + 1) * HT], start=True, stop=True)
            last.then_inc(n_rot, 1)

        def pool_cos(g):
            q = groups[g]
            rows, i = q["rows"], ropes_before[g]
            nc.gpsimd.wait_ge(n_out, g + 1)
            if i >= 1:
                nc.gpsimd.wait_ge(n_rope, i)
            nc.gpsimd.tensor_tensor(tmp[rows, 0, :], q["dst"][0], C[rows, q["rope"][1]:q["rope"][1] + T],
                                    ALU.mult).then_inc(n_nc, 1)

        chain = dict(base=0, n=0)

        def link(ins):
            chain["n"] += 1
            ins.then_inc(dve, 1)
            nc.vector.wait_ge(dve, chain["base"] + chain["n"])

        def dve_recip(p):
            rows, w = sum_rows(p), groups[packs[p][0]]["w"]
            nc.vector.wait_ge(n_rt, p + 1)
            nc.vector.reciprocal(R[rows, p % 2, 0:w], R[rows, p % 2, 0:w]).then_inc(n_rc, 1)

        def dve_scale(g, between=None):
            q, p = groups[g], pack_of[g][0]
            rows, w = q["rows"], q["w"]
            halves = lambda x: x.rearrange("p (a n) -> p a n", a=2)
            if q["z"] is None:
                nc.vector.wait_ge(n_rc, p + 1)
            else:
                nc.vector.wait_ge(n_bc, spreads_before[g] + 1)
            for j, (src, dst) in enumerate(zip(q["src"], q["dst"])):
                gc = q["gain"] + (j if len(q["src"]) > 1 else 0)
                if q["split"]:
                    k = splits_before[g] + j
                    if k >= 2:
                        nc.vector.wait_ge(n_lo, k - 1)
                    nc.vector.scalar_tensor_tensor(out=tmp[:, k % 2, :], in0=src, scalar=G[rows, gc:gc + 1], in1=R[rows, p % 2, 0:w],
                                                   op0=ALU.mult, op1=ALU.mult).then_inc(n_tmp, 1)
                    if between and j in between:
                        between[j]()
                    if j >= 1:
                        dve_lo(g, j - 1)
                    continue
                last = nc.vector.scalar_tensor_tensor(out=halves(dst), in0=halves(src), scalar=G[rows, gc:gc + 1], in1=spread_pair(g)[rows, :, 0:w // 2],
                                                      op0=ALU.mult, op1=ALU.mult)
            if q["split"]:
                dve_lo(g, len(q["src"]) - 1)
                nc.vector.wait_ge(n_lo, splits_before[g + 1])
                nc.vector.sem_inc(n_out, 1)
            else:
                last.then_inc(n_out, 1)

        def dve_rope(g):
            q = groups[g]
            rows, i = q["rows"], ropes_before[g]
            nc.vector.wait_ge(n_rot, i + 1)
            link(nc.vector.tensor_tensor(tmp[rows, 1, :].rearrange("p (a n) -> p a n", a=2), ps[1][rows, :, 0:HT],
                                         C[rows, q["rope"][2]:q["rope"][2] + T].rearrange("p (a n) -> p a n", a=2),
                                         ALU.mult))
            nc.vector.wait_ge(n_nc, i + 1)
            nc.vector.tensor_tensor(q["dst"][0], tmp[rows, 0, :], tmp[rows, 1, :], ALU.add).then_inc(n_rope, 1)

        def dve_norm_split(p, between=None):
            dve_recip(p)
            dve_scale(packs[p][0], between)

        def mm3(u, cols, pair, rows, x, i=0, k0=0, nk=KD, kw=P, step=0, parts=None):
            if i is not None:
                nc.tensor.wait_ge(w_lo, i + (u + 1))
            hi, lo = wHi[:, u % 2, :], wLo[:, u % 2, :]
            for k in range(nk):
                if step:
                    nc.tensor.wait_ge(parts or n_lo, step + k)
                c = slice((k0 + k) * kw, (k0 + k) * kw + cols)
                for z, (w, xx) in enumerate(((hi, x[0]), (hi, x[1]), (lo, x[0]))):
                    for a in range(2):
                        ins = nc.tensor.matmul(pair[rows, a, 0:HT], w[:, c], xx[:, k, a * HT:(a + 1) * HT],
                                               start=(k == 0 and z == 0), stop=(k == nk - 1 and z == 2))
            return ins

        def sp_weight(u, src, i=0):
            if u >= 2:
                nc.sync.wait_ge(w_lo, i + (u - 1))
            nc.sync.dma_start(ring[:, u % 2, 0:src.shape[-1]], src).then_inc(w_in_[u % 2], 16)

        def sp_weight_loop(u0, n, src):
            pairs = src.rearrange("(f j) p n -> j f p n", j=2)
            with nc.sync.Fori(0, n // 2) as f:
                for j in range(2):
                    sp_weight(u0 + j, pairs[j, bass.ds(f, 1), :, :].rearrange("a p n -> p (a n)"), f * 2)

        units = [(h, i) for h in range(2 * H) for i in range(4)]

        def heads(h):
            if h < H:
                return QT[LO, h, :], KT[LO, h, :], vA
            r = slice((h % 2) * HD, (h % 2) * HD + HD)
            c = (h - H) // 2
            return uT[r, U_QS + c, :], uT[r, U_KS + c, :], vB

        ABSORB = 48
        W_WIDE, QB_WIDE, PL_WIDE = KD * P, KQ * HQ, (KD + 2) * P
        DN_WIDE = tuple(n * P for n in HALVES)

        block = ctx.enter_context(nc.Block())

        @block.sync
        def _(sp):
            sp.dma_start(hT[:, 0:2, :], x[:, 0:2, :]).then_inc(s_x[0], 16)
            sp.dma_start(G[:, :], gains).then_inc(s_g, 16)
            sp.dma_start(C[:, 0:C_MA], cst[:, 0:C_MA]).then_inc(s_c, 16)
            for k in range(1, KD // 2):
                sp.dma_start(hT[:, 2 * k:2 * k + 2, :], x[:, 2 * k:2 * k + 2, :]).then_inc(s_x[k], 16)
            for u in range(2):
                sp_weight(W_IN + u, win[u])
            sp.dma_start(C[:, C_MA:], cst[:, C_MA:]).then_inc(s_c2, 16)
            sp.dma_start(wK[:, :, :], wk).then_inc(s_wk, 16)
            sp.dma_start(wV[:, :, :], wv).then_inc(s_wk, 16)
            sp.dma_start(ptab[:, :], pt).then_inc(s_pt, 16)
            for u in range(2, NIN):
                sp_weight(W_IN + u, win[u])
            for u in range(H):
                sp_weight(W_QB + u, wqb[u])
            for u in range(2):
                sp_weight(W_O + u, wo[u])
            def page_numbers(b, ts):
                return {t: sp.value_load(ptab[0:1, bass.ds(b * NPG + t, 1)], min_val=0, max_val=POOL - 1) for t in ts}

            def load_page_T(page, t):
                src = bass.ds(page[t], 1)
                sp.dma_start(pgT[:, t % PR, :], pgt[src, :, :].rearrange("a p n -> p (a n)")).then_inc(pg_in[t % PR], 16)
                sp.dma_start(pgR[MID, t % PR, :], pgk[src, :, :].rearrange("a p n -> p (a n)")).then_inc(pg_in[t % PR], 16)

            def load_swa_k(b):
                sp.dma_start(cK, ck[bass.ds(b, 1), :, :, PAST - 896:PAST].rearrange("a c p n -> p (a c) n")).then_inc(ck_in, 16)

            def load_swa_v(b):
                sp.dma_start(cVr, cv[bass.ds(b, 1), PAST - REC:PAST, :].rearrange("a (j p) n -> p (a j) n", p=P)).then_inc(cv_in, 16)
                sp.dma_start(cVs, cv[bass.ds(b, 1), 0:PAST - REC, :].rearrange("a (g r) n -> g (a r) n", r=16)[:, 0:4, :]).then_inc(cv_in, 16)

            def load_latent(page):
                for t in range(NPG):
                    sp.dma_start(pgL[:, t, :], pgl[bass.ds(page[t], 1), :, :].rearrange("a p n -> p (a n)")).then_inc(pl_in, 16)

            sp.wait_ge(s_pt, 16)
            first = page_numbers(0, range(NPG))
            sp.wait_ge(cq_lo, KQ)
            for t in range(PR):
                load_page_T(first, t)
            sp.wait_ge(a_pv, 4 * H)
            sp.dma_start(wkT, wkt).then_inc(s_wkt, 16)
            load_latent(first)
            sp.wait_ge(p_read, 2)
            load_swa_k(0)
            sp.wait_ge(a_o, H)
            sp.wait_ge(out_s, 80)
            sp.wait_ge(p_all, 1)
            load_swa_v(0)

            def later_pages(b):
                page = page_numbers(b, range(PR, NPG))
                for t in range(PR, NPG):
                    sp.wait_ge(r_used, b * NPG + (t - PR + 1))
                    load_page_T(page, t)

            with sp.Fori(0, NB - 1) as b:
                sp.wait_ge(w_sc, b + 1)
                load_swa_k(b + 1)
                later_pages(b)
                page = page_numbers(b + 1, range(NPG))
                sp.wait_ge(m_sc, b + 1 + FIRST)
                for t in range(PR):
                    load_page_T(page, t)
                sp.wait_ge(w_pv, b + 1)
                load_swa_v(b + 1)
                sp.wait_ge(m_pv, b + 1)
                load_latent(page)
            later_pages(NB - 1)
            for u in range(2, KD):
                sp_weight(W_O + u, wo[u])
            sp.wait_ge(w_pv, NB)
            sp.dma_start(plT, plt).then_inc(s_plt, 16)
            sp_weight_loop(W_GU, 2 * HALVES[0], wgu[0:2 * HALVES[0]])
            sp_weight_loop(W_DN, KD, wdn)
            sp_weight_loop(W_GU2, 2 * HALVES[1], wgu[2 * HALVES[0]:])
            sp_weight_loop(W_DN2, KD, wdn2)
            sp_weight_loop(W_PL, KD, wpl)
            for m in range(KD):
                sp.wait_ge(pl_ev[m % 2], m // 2 + 1)
                sp.dma_start(y[m], hT[:, m, :]).then_inc(out_y, 16)
            sp.wait_ge(out_y, 16 * KD)

        @block.gpsimd
        def _(pool):
            HALF = (PAST - NQ) // 2

            def copy_k(b, z):
                c = slice(2 * z, 2 * z + 2)
                pool.dma_start(o_ck[b, c].rearrange("c p n -> (c p n)").rearrange("(a n) -> a n", a=32),
                               ck[b, c].rearrange("c p n -> (c p n)").rearrange("(a n) -> a n", a=32)).then_inc(out_c, 16)

            def copy_v(b, z):
                pool.dma_start(o_cv[b, z * HALF:(z + 1) * HALF, :],
                               cv[b, NQ + z * HALF:NQ + (z + 1) * HALF, :]).then_inc(out_c, 16)

            for k in range(8):
                pool.wait_ge(w_used, 2 * k + 1)
                copy_k(k // 2, k % 2)
            pool.wait_ge(s_c2, 16)
            pool_cos(g_kr)
            for g in packs[P_S]:
                pool_cos(g)
            for g in g_qh:
                pool_cos(g)
            pool.wait_ge(n_rope, 1 + len(packs[P_S]))
            pool.dma_start(o_lat, uT[:, U_LAT:U_LAT + KC, :]).then_inc(out_s, 16)
            pool.dma_start(o_kr, uT[MID, U_KR, :]).then_inc(out_s, 16)
            pool.dma_start(o_ks, uT[:, U_KS:U_KS + HP, :]).then_inc(out_s, 16)
            pool.wait_ge(vs_ev, 5)
            pool.dma_start(o_vs.rearrange("(t p) n -> p t n", p=P), vB).then_inc(out_s, 16)
            pool.dma_start(o_cv[:, PAST - NQ:PAST, :].rearrange("b q n -> b (q n)"),
                           vNew[:, :]).then_inc(out_s, 16)
            pool.wait_ge(out_s, 80)
            for k in range(8):
                pool.wait_ge(a_s, 8 * k + 1)
                copy_v(k // 2, k % 2)
            pool.wait_ge(p_all, 1)
            with pool.Fori(0, NB) as b:
                pool.wait_ge(m_sc, b + FIRST)
                pool.tensor_copy(qa[:, :], qaAll[:, bass.ds(b, 1), :].rearrange("p a n -> p (a n)")).then_inc(q_st, 1)
                pool.wait_ge(q_st, b * 4 + 1)
                pool.tensor_copy(qr[MID, :], qrAll[MID, bass.ds(b, 1), :].rearrange("p a n -> p (a n)")).then_inc(q_st, 1)
                pool.wait_ge(q_st, b * 4 + 2)
                pool.tensor_copy(qw[:, 0:160].rearrange("p (c n) -> p c n", n=40)[:, :, 0:8],
                                 qwAll[:, bass.ds(b, 1), :].rearrange("p a (c n) -> p (a c) n", c=HP)).then_inc(q_st, 1)
                pool.wait_ge(q_st, b * 4 + 3)
                pool.tensor_copy(mNew[:, :], C[0:NS, bass.ds(b * 32 + C_MX, 32)]).then_inc(q_st, 1)
                pool.wait_ge(q_st, b * 4 + 4)
                pool.wait_ge(m_mx, b + 1)
                pool.sem_inc(passed, 1)
                pool.partition_all_reduce(mxa[:, :], mx[:, :], P, MAX_ALL).then_inc(m_ar, 1)
            for b in range(4, NB):
                for k in range(4):
                    pool.wait_ge(w_used, W_GU + 14 * (b - 4) + 3 * k + 1)
                    (copy_v if k % 2 else copy_k)(b, k // 2)
            pool.wait_ge(out_c, 16 * 4 * NB)

        @block.scalar
        def _(act):
            act.sem_inc(k_sq, FIRST)
            act.wait_ge(s_g, 16)
            act.wait_ge(s_c, 16)
            act_norm_split(P_X, lambda: (act_weight(0, W_WIDE), act_weight(1, W_WIDE)))

            def in_copy(m):
                act.wait_ge(w_used, W_IN + m + 1)
                rows = MID if m == U_KR else FULL
                dst = uT[rows, m, :] if m < NU else QT[:, m - NU, :]
                act.activation(dst.rearrange("p (a n) -> p a n", a=2), ps[m % 2][rows, :, 0:HT], ACT.Copy).then_inc(in_ev, 1)
                act_weight(m + 2, W_WIDE if m + 2 < NIN else QB_WIDE)

            for m in range(U_QS + 2):
                in_copy(m)
            act.wait_ge(in_ev, U_QS)
            for g in packs[P_IN]:
                norm_squares(g)
            norm_root(P_IN)
            for m in range(U_QS + 2, NIN):
                in_copy(m)
            for k in range(KQ):
                act.wait_ge(n_out, g_cq + 1)
                act.activation(aHi[:, k, :], uT[:, k, :], ACT.Copy).then_inc(cq_hi, 1)
            for t in range(5):
                act.wait_ge(vs_mm, t + 1)
                act.activation(vB[:, t, :] if t < 4 else vNew[:, :], ps[1][0:P if t < 4 else NS, t % 2, :], ACT.Copy).then_inc(vs_ev, 1)
            for h in range(H):
                norm_squares(packs[P_S][h])
                act.wait_ge(w_used, W_QB + h + 1)
                act.activation(QT[LO, h, :].rearrange("p (a n) -> p a n", a=2), ps[h % 2][LO, :, 0:HT], ACT.Copy).then_inc(qb_ev, 1)
                if h + 2 < H:
                    act_weight(W_QB + h + 2, QB_WIDE)
            norm_root(P_S)
            for h in range(H):
                act.wait_ge(qb_ev, h + 1)
                norm_squares(g_qh[h])
            norm_root(P_QH)
            act.wait_ge(w_used, W_QB + H)
            for h in range(H):
                act.wait_ge(k_mm, h + 1)
                act.activation(KT[LOW, h, 0:NP_], ps[0][LOW, h % 2, :], ACT.Copy).then_inc(k_ev, 1)
            for h in range(H):
                act.wait_ge(k_ev, h + 1)
                norm_squares(g_kh[h])
            norm_root(P_KH)
            for t in range(4):
                act.wait_ge(v_mm, t + 1)
                act.activation(vA[:, t, :], ps[0][:, t % 2, :], ACT.Copy).then_inc(v_ev, 1)
            act.wait_ge(v_mm, 5)
            act.wait_ge(n_rope, ropes_before[-1])
            act.activation(tmp[0:NS, 0, 0:512], ps[0][0:NS, 0, :], ACT.Square).then_inc(kn_sq, 1)
            act.wait_ge(tn_mm, 1)
            act.activation(latNew[:, :], ps[0][0:NS, 1, 0:KVL], ACT.Copy).then_inc(tn_ev, 1)
            act.wait_ge(kn_ss, 1)
            act.activation(rkN[:, :], rkN[:, :], ACT.Sqrt, scale=1.0 / NOPE, bias=G[0:NS, G_EPS:G_EPS + 1]).then_inc(k_rt, 1)

            for n in range(len(units) + 4):
                if n >= 4:
                    m = n - 4
                    w = (units[m][1] + 1) * P
                    act.wait_ge(a_t, m + 1)
                    if m >= 2:
                        act.wait_ge(a_pv, m - 1)
                    act.activation(prT[:, m % 2, 0:w], ps[1][:, m % 2, 0:w], ACT.Copy).then_inc(a_tc, 1)
                if n < len(units):
                    w = (units[n][1] + 1) * P
                    k = n % 4
                    act.wait_ge(a_nm, n + 1)
                    act.activation(pr[:, k, 0:w], pr[:, k, 0:w], ACT.Exp, bias=st[:, k:k + 1],
                                   accum_out=st[:, 4 + k:5 + k]).then_inc(a_e, 1)
                if n == 12:
                    act.wait_ge(s_wk, 32)
                    act.wait_ge(w_used, W_QB + H)
                    act.activation(wkHi[:, :, :], wK[:, :, :], ACT.Copy).then_inc(wk_hi, 1)

            with act.Fori(0, NB) as b:
                def page_hi(t):
                    act.wait_ge(pg_in[t % PR], b * 64 + (32 if t < PR else 64))
                    if t < 2:
                        act.wait_ge(k_raw, b * NPG + FIRST)
                    else:
                        act.wait_ge(k_raw, b * NPG + (t - 1) + FIRST)
                    act.activation(pgHi[:, t % 2, :], pgT[:, t % PR, :], ACT.Copy).then_inc(p_hi, 1)

                page_hi(0)
                page_hi(1)
                for t in range(NPG):
                    act.wait_ge(k_raw, b * NPG + (t + 1) + FIRST)
                    if t >= 2:
                        act.wait_ge(k_ss, b * NPG + (t - 1) + FIRST)
                    else:
                        act.wait_ge(k_ss, b * NPG + FIRST)
                    act.activation(sqK[:, t % 2, :], ps[0][:, t % 2, :], ACT.Square).then_inc(k_sq, 1)
                    if t + 2 < NPG:
                        page_hi(t + 2)
                    if t == EXP_AT:
                        act.wait_ge(w_nm, b + 1)
                        act.activation(Sw[:, :], Sw[:, :], ACT.Exp, bias=sm[:, 5:6], accum_out=sm[:, 3:4]).then_inc(w_e, 1)
                    if t == TURN_AT + 1:
                        act.wait_ge(w_t, b + 1)
                        act.activation(Rf[:, 0:256], ps[2][:, 0, 0:256], ACT.Copy)
                        act.activation(Rf[0:NS, 256:288], ps[2][0:NS, 0, 256:288], ACT.Copy).then_inc(w_tc, 1)
                act.wait_ge(k_ss, b * NPG + NPG + FIRST)
                act.activation(ssq[:, :], ssq[:, :], ACT.Sqrt, scale=1.0 / NOPE, bias=G[:, G_EPS:G_EPS + 1]).then_inc(k_rt, 1)
                act.wait_ge(m_sub, b + 1)
                act.activation(E, S, ACT.Exp, scale=SC_A).then_inc(m_e, 1)
            sqrt_table()
            act.wait_ge(oa_mm, 1)
            act.activation(aT[:, 0:HP, NP_:T], ps[0][:, 0, 0:HP * NS].rearrange("p (c n) -> p c n", c=HP), ACT.Copy).then_inc(oa_ev, 1)
            act.wait_ge(oa_ev, 1)
            act.wait_ge(w_o, NB + FIRST)
            norm_squares(g_oa)
            act_weight(W_O, W_WIDE)
            norm_root(P_OA)
            norm_squares(g_ob)
            act_weight(W_O + 1, W_WIDE)
            act_hi(g_oa)
            norm_root(P_OB)
            act_hi(g_ob)
            for m in range(KD + 1):
                if m < KD - 1:
                    act_weight(W_O + m + 2, W_WIDE)
                if m:
                    act.wait_ge(wo_ev, m)
                    acc_square(g_f, m - 1)
            act_norm_split(P_F, lambda: act_weight(W_GU + 1, W_WIDE))

            def act_ffn(w0, wd, tiles, width, before, after):
                def gate_up(f, j, nxt):
                    act_weight(w0 + 2 * j + 2, nxt[0], f * 4)
                    act.wait_ge(w_used, f * 4 + (w0 + 2 * j + 2))
                    act.wait_ge(h_tmp, f * 2 + (before + j) + FIRST)
                    act.activation(tmp[:, j, :].rearrange("p (a n) -> p a n", a=2), ps[2 * j][:, :, 0:HT],
                                   ACT.Silu).then_inc(gu_act, 1)
                    act_weight(w0 + 2 * j + 3, nxt[1], f * 4)
                    act.wait_ge(h_tmp, f * 2 + (before + j + 1) + FIRST)
                    dst = hidHi[:, bass.ds(f * 2 + j, 1), :].rearrange("p a n -> p (a n)")
                    act.activation(dst, sq[:, j, :], ACT.Copy).then_inc(h_hi, 1)

                with act.Fori(0, tiles // 2 - 1) as f:
                    for j in range(2):
                        gate_up(f, j, (W_WIDE, W_WIDE))
                f = tiles // 2 - 1
                gate_up(f, 0, (W_WIDE, W_WIDE))
                gate_up(f, 1, (width, width))

                def down(m, j, u, wide, i, split=True):
                    if split:
                        act_weight(u, wide, i)
                    if before and not (isinstance(m, int) and m + j == 0):
                        act.wait_ge(dn_ev[1 - j], KD // 2 + (m // 2 + j if isinstance(m, int) else m // 2 + j))
                        acc_square(g_p, j + 1, m - 2) if not isinstance(m, int) else acc_square(g_p, m + j - 1)

                down(0, 0, wd + 2, width, 0)
                down(0, 1, wd + 3, width, 0)
                with act.Fori(2, KD - 2, 2) as m:
                    for j in range(2):
                        down(m, j, wd + j + 2, width, m)
                down(KD - 2, 0, wd + KD, after, 0)
                if before:
                    sqrt_table()
                down(KD - 2, 1, wd + KD + 1, after, 0, not before)

            act_ffn(W_GU, W_DN, HALVES[0], DN_WIDE[0], 0, W_WIDE)
            act_ffn(W_GU2, W_DN2, HALVES[1], DN_WIDE[1], HALVES[0], PL_WIDE)
            for j in range(2):
                act.wait_ge(dn_ev[j], KD)
            act.wait_ge(s_plt, 16)
            acc_square(g_p, KD - 1)
            act_norm_split(P_P, lambda: (act.activation(plHi[:, :, :], plT, ACT.Copy).then_inc(pl_hi, 1),
                                         act_weight(W_PL + 1, PL_WIDE)))

            def act_ple(m, j, more):
                act.wait_ge(w_used, m + (W_PL + j + 1))
                act.wait_ge(pl_mul, m + j + FIRST)
                act.activation(tmp[:, j, :].rearrange("p (a n) -> p a n", a=2), ps[2 * j][:, :, 0:HT],
                               ACT.Sigmoid, bias=G[:, bass.ds(m + (B_PLE + j), 1)]).then_inc(pl_act, 1)
                if more:
                    act_weight(W_PL + j + 2, PL_WIDE, m)

            with act.Fori(0, KD - 2, 2) as m:
                for j in range(2):
                    act_ple(m, j, True)
            for j in range(2):
                act_ple(KD - 2, j, False)

        @block.tensor
        def _(pe):
            mm = nc.tensor.matmul
            pe.sem_inc(k_raw, FIRST)
            pe.sem_inc(m_sc, FIRST)
            pe.wait_ge(s_c, 16)
            pe_norm(g_x)

            def in_tile(m):
                if m >= 2:
                    pe.wait_ge(in_ev, m - 1)
                cols, rows = (HQ, LO) if m == U_KR else (P, FULL)
                mm3(W_IN + m, cols, ps[m % 2], rows, a_split, step=1 if m == 0 else 0).then_inc(w_used, 1)

            for m in range(U_QS + 2):
                in_tile(m)
            for g in packs[P_IN]:
                pe_norm(g)
            for m in range(U_QS + 2, NIN):
                in_tile(m)
                if m - U_QS - 4 == 0:
                    pe.wait_ge(s_c2, 16)
                if m - U_QS - 4 in range(3):
                    pe_spread(packs[P_IN][m - U_QS - 4])
            pe.wait_ge(in_ev, NIN)

            def query(h):
                mm3(W_QB + h, HQ, ps[h % 2], LO, a_split, nk=KQ, kw=HQ, step=0 if h else 1, parts=cq_lo).then_inc(w_used, 1)

            query(0)
            for t in range(5):
                n = P if t < 4 else NS
                if t >= 2:
                    pe.wait_ge(vs_ev, t - 1)
                for c in range(HP):
                    last = pe.transpose(ps[1][0:n, t % 2, c * P:(c + 1) * P], QT[:, c, t * P:t * P + n], cm(C_ID))
                last.then_inc(vs_mm, 1)
            pe.wait_ge(vs_ev, 5)
            pe.wait_ge(s_c2, 16)
            pe_rot(g_kr)
            pe_norm(packs[P_S][0])
            pe.wait_ge(n_rope, 1)
            for h in range(1, H):
                if h >= 2:
                    pe.wait_ge(qb_ev, h - 1)
                query(h)
                pe_norm(packs[P_S][h])
            for g in g_qh:
                pe_norm(g)
            pe.wait_ge(s_wk, 32)
            pe.wait_ge(qb_ev, H)
            for h in range(H):
                pe_spread(packs[P_S][h])
                if h >= 2:
                    pe.wait_ge(k_ev, h - 1)
                for k in range(KC):
                    last = mm(ps[0][LOW, h % 2, :], wK[:, k, h * NOPE:(h + 1) * NOPE], uT[:, U_LAT + k, 0:NP_],
                              start=(k == 0), stop=(k == KC - 1))
                last.then_inc(k_mm, 1)
                if h:
                    pe_rot(packs[P_S][h - 1])
            for h in range(H):
                pe_spread(g_qh[h])
                pe_norm(g_kh[h])
                pe_rot((packs[P_S] + g_qh)[H + h - 1])
            pe_rot(g_qh[-1])
            for t in range(5):
                pe.wait_ge(k_ev, H) if t < 2 else pe.wait_ge(v_ev, t - 1)
                n = P if t < 4 else NS
                for k in range(KC):
                    last = mm(ps[0][0:n, t % 2, :], uT[:, U_LAT + k, t * P:t * P + n], (wV if t < 4 else wK)[:, k, :],
                              start=(k == 0), stop=(k == KC - 1))
                last.then_inc(v_mm, 1)
            pe.wait_ge(v_ev, 4)
            for k in range(KC):
                last = pe.transpose(ps[0][0:NS, 1, k * P:(k + 1) * P], uT[:, U_LAT + k, NP_:T], cm(C_ID))
            last.then_inc(tn_mm, 1)
            for g in g_kh:
                pe_spread(g)

            pe.wait_ge(kr_b, 1)
            pe.wait_ge(n_rope, ropes_before[-1])
            pe.wait_ge(n_out, g_kh[-1] + 1)
            pe.wait_ge(tn_ev, 1)
            pe.wait_ge(kn_sq, 1)
            for n in range(len(units) + 5):
                if n < len(units):
                    h, i = units[n]
                    q, k, _v = heads(h)
                    if n >= 2:
                        pe.wait_ge(a_sm, n - 1)
                    mm(ps[0][:, n % 2, 0:(i + 1) * P], q[:, i * P:(i + 1) * P], k[:, 0:(i + 1) * P],
                       start=True, stop=True).then_inc(a_s, 1)
                if n >= 3 and n - 3 < len(units):
                    m = n - 3
                    h, i = units[m]
                    pe.wait_ge(a_p, m + 1)
                    if m >= 2:
                        pe.wait_ge(a_tc, m - 1)
                    for j in range(i + 1):
                        last = pe.transpose(ps[1][:, m % 2, j * P:(j + 1) * P], pr[:, m % 4, j * P:(j + 1) * P], cm(C_ID))
                    last.then_inc(a_t, 1)
                if n >= 5:
                    m = n - 5
                    h, i = units[m]
                    _q, _k, v = heads(h)
                    pe.wait_ge(a_tc, m + 1)
                    if i == 0 and h % 2 == 0 and h >= 4:
                        pe.wait_ge(a_o, h // 2 - 1)
                    r = slice((h % 2) * HD, (h % 2) * HD + HD)
                    for j in range(i + 1):
                        last = mm(ps[2][r, (h // 2) % 2, i * P:(i + 1) * P], v[:, j, (h % H) * HD:(h % H + 1) * HD],
                                  prT[:, m % 2, j * P:(j + 1) * P], start=(j == 0), stop=(j == i))
                    last.then_inc(a_pv, 1)
                if n == ABSORB:
                    pe.wait_ge(s_wkt, 16)
                    pe.wait_ge(p_read, 1)
                    for c in range(KC):
                        for h in range(H):
                            o = (c * H + h) * NS
                            last = mm(ps[3][:, 0, o:o + NS], wkT[:, h, c * P:(c + 1) * P], qg[:, h, :], start=True, stop=True)
                    last.then_inc(p_ab, 1)

            def swa_scores(b):
                pe.wait_ge(q_st, b * 4 + 3)
                pe.wait_ge(ck_in, b * 16 + 16)
                for bank, lo, n in ((0, 384, 512), (1, 0, 384), (1, None, NS)):
                    o = 384 if lo is None else 0
                    for c in range(HP):
                        rhs = uT[:, U_KS + c, NP_:T] if lo is None else cK[:, c, lo:lo + n]
                        last = mm(ps[2][0:NS, bank, o:o + n], qw[:, c * 32:(c + 1) * 32], rhs, start=(c == 0), stop=(c == HP - 1))
                last.then_inc(w_sc, 1)

            def sequence(b, last_one):
                for t in range(NPG + 1):
                    new = t == NPG
                    grp = t // 4
                    n = NS if new else P
                    if not new:
                        pe.wait_ge(p_lo, b * NPG + (t + 1))
                        if t < 2:
                            pe.wait_ge(k_sq, b * NPG + FIRST)
                        else:
                            pe.wait_ge(k_sq, b * NPG + (t - 1) + FIRST)
                        for c in range(KC):
                            for z, (x_, w_) in enumerate(((pgHi, wkHi), (pgHi, wkLo), (pgLo, wkHi))):
                                last = mm(ps[0][:, t % 2, :], x_[:, t % 2, c * P:(c + 1) * P], w_[:, c, :],
                                          start=(c == 0 and z == 0), stop=(c == KC - 1 and z == 2))
                        last.then_inc(k_raw, 1)
                    if t == 4:
                        pe.wait_ge(w_o, b + FIRST)
                    if t % 4 == 0:
                        pe.wait_ge(m_cp, b * 5 + max(grp - 1, 0) + FIRST)
                    o = (t % 4) * 64
                    bank = ps[1][0:n, grp % 2, :]
                    for c in range(KC):
                        lhs = uT[:, U_LAT + c, NP_:T] if new else pgT[:, t % PR, c * P:(c + 1) * P]
                        mm(bank[:, o:o + 32], lhs, qa[:, c * 32:(c + 1) * 32], start=(c == 0), stop=(c == KC - 1))
                    lhs = uT[MID, U_KR, NP_:T] if new else pgR[MID, t % PR, :]
                    last = mm(bank[:, o + 32:o + 64], lhs, qr[MID, :], start=True, stop=True)
                    if not new:
                        last.then_inc(r_used, 1)
                    else:
                        last.then_inc(m_sc, 1)
                    if t == TURN_AT:
                        pe.wait_ge(w_e, b + 1)
                        pe.sem_inc(passed_t, 1)
                        for u in range(NT_W):
                            lo = u * STR if u < 4 else 384 + (u - 4) * P
                            n = P if u < 8 else NS
                            last = pe.transpose(ps[2][0:n, 0, u * 32:(u + 1) * 32], Sw[:, lo:lo + n], C[0:NS, C_ID:C_ID + NS])
                        last.then_inc(w_t, 1)
                pe.wait_ge(w_tc, b + 1)
                pe.wait_ge(cv_in, b * 32 + 32)
                for t in range(NT_W):
                    if t < 4:
                        lhs, rhs = Ew[0:STR, t, :], cVs[:, t, :]
                    elif t < 8:
                        lhs, rhs = Ew[:, t, :], cVr[:, t - 4, :]
                    else:
                        lhs, rhs = Ew[0:NS, t, :], vNew[:, :]
                    last = mm(ps[3][0:NS, 1, :], lhs, rhs, start=(t == 0), stop=(t == NT_W - 1))
                last.then_inc(w_pv, 1)
                pe.wait_ge(pl_in, b * (16 * NPG) + 16 * NPG)
                pe.wait_ge(m_es, b + 1)
                for t in range(NPG + 1):
                    lhs, rhs = (E[:, t, :], pgL[:, t, :]) if t < NPG else (E[0:NS, t, :], latNew[:, :])
                    mm(ps[3][0:NS, 0, 0:KVL], lhs, rhs, start=(t == 0), stop=(t == NPG))
                mm(ps[3][0:NS, 0, KVL:KVL + 1], es[:, :], C[:, C_ONE:C_ONE + 1], start=True, stop=True).then_inc(m_pv, 1)
                if not last_one:
                    swa_scores(b + 1)
                pe.wait_ge(m_cp, b * 5 + 4 + FIRST)
                pe.wait_ge(w_on, b + 1)
                pe.sem_inc(passed_t, 1)
                for c in range(HP):
                    last = pe.transpose(ps[1][:, 1, c * 32:(c + 1) * 32], On[:, KVL + c * P:KVL + (c + 1) * P], C[0:NS, C_ID:C_ID + NS])
                last.then_inc(w_tt, 1)
                pe.wait_ge(m_on, b + 1)
                pe.wait_ge(m_o, b + FIRST)
                pe.sem_inc(passed_t, 1)
                for c in range(KC):
                    last = pe.transpose(ps[2][:, 1, 448 + c * 32:448 + (c + 1) * 32], On[:, c * P:(c + 1) * P], C[0:NS, C_ID:C_ID + NS])
                last.then_inc(m_tt, 1)

            pe.wait_ge(a_o, H)
            pe.wait_ge(p_all, 1)
            pe.wait_ge(wk_lo, 1)
            swa_scores(0)
            with pe.Fori(0, NB - 1) as b:
                sequence(b, False)
            sequence(NB - 1, True)

            pe.wait_ge(m_o, NB + FIRST)
            for h in range(H):
                r = slice((h % 2) * HD, (h % 2) * HD + HD)
                for c in range(KC):
                    last = mm(ps[0][r, 0, (h // 2) * NS:(h // 2 + 1) * NS], wV[:, c, h * HD:(h + 1) * HD], oAbs[:, c, h, :],
                              start=(c == 0), stop=(c == KC - 1))
            last.then_inc(oa_mm, 1)
            pe_norm(g_oa)
            pe_norm(g_ob)
            for m in range(KD):
                if m >= 2:
                    pe.wait_ge(wo_ev, m - 1)
                mm3(W_O + m, P, ps[m % 2], FULL, a_split, step=0 if m else splits_before[g_oa] + 1).then_inc(w_used, 1)
            pe_norm(g_f)

            def pe_ffn(w0, wd, tiles, before):
                def gate_up(f, j, step=0):
                    pe.wait_ge(gu_ev[j], f + before // 2)
                    for z in range(2):
                        if before and j == 0:
                            pe.wait_ge(dn_ev[z], KD // 2)
                        mm3(w0 + 2 * j + z, P, ps[2 * j + z], FULL, a_split, i=f * 4, step=0 if z else step).then_inc(w_used, 1)

                if not before:
                    gate_up(0, 0, splits_before[g_f] + 1)
                    gate_up(0, 1)
                with pe.Fori(0 if before else 1, tiles // 2) as f:
                    for j in range(2):
                        gate_up(f, j)

                def down(m, j, **ready):
                    mm3(wd + j, P, ps[j], FULL, (hidHi, hidLo), i=m * 2, nk=tiles, **ready).then_inc(w_used, 1)

                pe.wait_ge(gu_ev[0], (before + tiles) // 2)
                down(0, 0, step=before + 1, parts=h_lo)
                down(0, 1)
                with pe.Fori(1, KD // 2) as m:
                    for j in range(2):
                        pe.wait_ge(dn_ev[j], m + (KD // 2 if before else 0))
                        down(m, j)

            pe_ffn(W_GU, W_DN, HALVES[0], 0)
            pe_ffn(W_GU2, W_DN2, HALVES[1], HALVES[0])
            pe_norm(g_p)

            def ple(m, j, step=0):
                pe.wait_ge(pl_ev[j], m)
                mm3(W_PL + j, P, ps[2 * j], FULL, a_split, i=m * 2, step=step)
                if step:
                    pe.wait_ge(pl_lo, 1)
                mm3(W_PL + j, P, ps[2 * j + 1], FULL, (plHi, plLo), i=None, k0=KD, nk=2).then_inc(w_used, 1)

            ple(0, 0, splits_before[g_p] + 1)
            ple(0, 1)
            with pe.Fori(1, KD // 2) as m:
                for j in range(2):
                    ple(m, j)

        @block.vector
        def _(v):
            for used in (m_cp, w_o, m_o, k_ss, h_tmp, pl_mul):
                v.sem_inc(used, FIRST)
            for k in range(KD // 2):
                v.wait_ge(s_x[k], 16)
            v.wait_ge(s_g, 16)
            v.wait_ge(s_c, 16)
            dve_norm_split(P_X, {1: lambda: dve_weight(0, W_WIDE), 4: lambda: dve_weight(1, W_WIDE)})

            def in_weight(m):
                dve_weight(m + 2, W_WIDE if m + 2 < NIN else QB_WIDE)

            for m in range(U_QS + 2):
                in_weight(m)
            dve_recip(P_IN)
            for m in range(U_QS + 2, NIN):
                in_weight(m)
                if m - U_QS - 3 in range(3):
                    dve_scale(packs[P_IN][m - U_QS - 3])
            v.wait_ge(w_used, NIN)
            for k in range(KQ):
                v.wait_ge(cq_hi, k + 1)
                v.tensor_tensor(aLo[:, k, :], uT[:, k, :], aHi[:, k, :].bitcast(F32), ALU.subtract).then_inc(cq_lo, 1)
            v.wait_ge(s_c2, 16)
            dve_rope(g_kr)
            for u in range(2, H):
                dve_weight(W_QB + u, QB_WIDE)
            dve_recip(P_S)
            turned = packs[P_S] + g_qh
            for h in range(H):
                dve_scale(turned[h])
                if h:
                    dve_rope(turned[h - 1])
                if h == 1:
                    dve_recip(P_QH)
            v.wait_ge(n_rope, 1)
            v.wait_ge(w_used, W_QB + H)
            v.tensor_copy(KT[MID, :, 0:NP_], uT[MID, U_KR:U_KR + 1, 0:NP_].broadcast_to([ROPE, H, NP_])).then_inc(kr_b, 1)
            for h in range(H):
                dve_scale(g_qh[h])
                dve_rope(turned[H + h - 1])
            dve_rope(g_qh[-1])
            dve_recip(P_KH)
            for g in g_kh:
                dve_scale(g)
            v.wait_ge(kn_sq, 1)
            v.tensor_reduce(rkN[:, :], tmp[0:NS, 0, 0:512].rearrange("p (h d) -> p h d", h=H), AX.X, ALU.add).then_inc(kn_ss, 1)
            v.wait_ge(k_rt, 1)
            link(v.reciprocal(rkN[:, :], rkN[:, :]))
            for n in range(len(units) + 5):
                if n >= 2 and n - 2 < len(units):
                    m = n - 2
                    k = m % 4
                    w = (units[m][1] + 1) * P
                    v.wait_ge(a_e, m + 1)
                    link(v.reciprocal(st[:, 12 + k:13 + k], st[:, 4 + k:5 + k]))
                    v.tensor_scalar(pr[:, k, 0:w], pr[:, k, 0:w], st[:, 12 + k:13 + k], None, ALU.mult).then_inc(a_p, 1)
                if n < len(units):
                    h, i = units[n]
                    w = (i + 1) * P
                    k = n % 4
                    mask = (C_MA if h < H else C_MB) + (3 - i) * P
                    v.wait_ge(a_s, n + 1)
                    if n >= 4:
                        v.wait_ge(a_t, n - 3)
                    v.tensor_tensor_reduce(pr[:, k, 0:w], ps[0][:, n % 2, 0:w], C[:, mask:mask + w],
                                           SC_A if h < H else SC_B, NEG * 4, ALU.add, ALU.max,
                                           st[:, 8 + k:9 + k]).then_inc(a_sm, 1)
                    v.wait_ge(a_sm, n + 1)
                    v.tensor_scalar(st[:, k:k + 1], st[:, 8 + k:9 + k], -1.0, None, ALU.mult).then_inc(a_nm, 1)
                if n >= 5:
                    h, i = units[n - 5]
                    if i == 3 and h % 2 == 1:
                        c = h // 2
                        v.wait_ge(a_pv, n - 4)
                        v.tensor_copy(aT[:, c, 0:NP_], ps[2][:, c % 2, :]).then_inc(a_o, 1)
                if n == 13:
                    v.wait_ge(wk_hi, 1)
                    v.tensor_tensor(wkLo[:, :, :], wK[:, :, :], wkHi[:, :, :].bitcast(F32), ALU.subtract).then_inc(wk_lo, 1)
                if n == 16:
                    v.memset(S, NEG)
                    v.memset(qw[:, :], 0.0)
                    link(v.memset(qwAll, 0.0))
                if n == 20:
                    v.wait_ge(n_rope, ropes_before[-1])
                    v.tensor_scalar(qg[:, :, :], QT[LOW, :, NP_:T], G[LOW, G_K:G_K + 1], None, ALU.mult).then_inc(p_read, 1)
                    v.tensor_copy(qrAll[MID, :, :].rearrange("p b (h q) -> p h b q", h=H),
                                  QT[MID, :, NP_:T].rearrange("p h (b q) -> p h b q", q=NQ)).then_inc(p_read, 1)
                if n == 24:
                    for z in range(2):
                        r = slice(z * HD, (z + 1) * HD)
                        link(v.tensor_copy(qwAll[r, :, :].rearrange("p b (c z q) -> p c z b q", c=HP, z=2)[:, :, z],
                                           uT[r, U_QS:U_QS + HP, NP_:T].rearrange("p c (b q) -> p c b q", q=NQ)))
                if n == ABSORB + 1:
                    v.wait_ge(p_ab, 1)
                    v.tensor_copy(qaAll.rearrange("p b (c q) -> p c b q", q=NQ),
                                  ps[3][:, 0, :].rearrange("p (c b q) -> p c b q", b=NB, q=NQ)).then_inc(p_all, 1)
            before = chain["n"]

            def page_lo(b, t):
                v.wait_ge(p_hi, b * NPG + (t + 1))
                v.tensor_tensor(pgLo[:, t % 2, :], pgT[:, t % PR, :], pgHi[:, t % 2, :].bitcast(F32), ALU.subtract).then_inc(p_lo, 1)

            def sequence(b, last_one):
                chain["base"], chain["n"] = b * LOOP_LINKS + before, 0
                v.wait_ge(w_sc, b + 1)
                v.wait_ge(q_st, b * 4 + 4)
                v.sem_inc(passed_v, 1)
                for j, (out, src, mask) in enumerate((
                        (Sw[:, 384:896], ps[2][0:NS, 0, :], C[0:NS, C_MW + 384:C_MW + 896]),
                        (Sw[:, 0:384], ps[2][0:NS, 1, 0:384], C[0:NS, C_MW:C_MW + 384]),
                        (Sw[:, 896:NKW], ps[2][0:NS, 1, 384:416], mNew[:, :]))):
                    last = v.tensor_tensor_reduce(out, src, mask, SC_B, NEG * 4, ALU.add, ALU.max, sm[:, j:j + 1])
                link(last)
                link(v.tensor_reduce(sm[:, 7:8], sm[:, 0:3], AX.X, ALU.max))
                v.tensor_scalar(sm[:, 5:6], sm[:, 7:8], -1.0, None, ALU.mult).then_inc(w_nm, 1)
                for t in range(NPG):
                    v.wait_ge(k_sq, b * NPG + (t + 1) + FIRST)
                    v.tensor_reduce(ssq[:, t * H:(t + 1) * H], sqK[:, t % 2, :].rearrange("p (h d) -> p h d", h=H), AX.X,
                                    ALU.add).then_inc(k_ss, 1)
                    if t + 2 < NPG:
                        page_lo(b, t + 2)
                    if t % 4 == 3:
                        g = t // 4
                        v.wait_ge(r_used, b * NPG + (t + 1))
                        v.tensor_copy(sRaw[:, 4 * g:4 * g + 4, :], ps[1][:, g % 2, 0:256].rearrange("p (t c) -> p t c", c=64)).then_inc(m_cp, 1)
                v.wait_ge(m_sc, b + 1 + FIRST)
                link(v.tensor_tensor(sN[:, :].rearrange("p (h q) -> p h q", q=NQ),
                                     ps[1][0:NS, 0, 0:32].rearrange("p (h q) -> p h q", q=NQ),
                                     rkN[:, :].unsqueeze(2).broadcast_to([NS, H, NQ]), ALU.mult))
                link(v.tensor_tensor(sN[:, :], ps[1][0:NS, 0, 32:64], sN[:, :], ALU.add))
                v.tensor_tensor(S[0:NS, NPG, :], sN[:, :], C[0:NS, bass.ds(b * 32 + C_MN, 32)], ALU.add).then_inc(m_cp, 1)
                v.wait_ge(k_rt, b + 2)
                link(v.reciprocal(ssq[:, :], ssq[:, :]))
                v.wait_ge(m_cp, b * 5 + 5 + FIRST)
                link(v.tensor_tensor(S[:, 0:NPG, :].rearrange("p t (h q) -> p t h q", q=NQ),
                                     sRaw[:, :, 0:32].rearrange("p t (h q) -> p t h q", q=NQ),
                                     ssq[:, :].rearrange("p (t h) -> p t h", h=H).unsqueeze(3).broadcast_to([P, NPG, H, NQ]), ALU.mult))
                link(v.tensor_tensor(S[:, 0:NPG, :], S[:, 0:NPG, :], sRaw[:, :, 32:64], ALU.add))
                v.tensor_reduce(mx[:, :], S.rearrange("p t c -> p c t"), AX.X, ALU.max).then_inc(m_mx, 1)
                v.wait_ge(w_e, b + 1)
                link(v.reciprocal(sm[:, 4:5], sm[:, 3:4]))
                v.wait_ge(m_ar, b + 1)
                v.tensor_tensor(S, S, mxa[:, :].unsqueeze(1).broadcast_to([P, NPG + 1, 32]), ALU.subtract).then_inc(m_sub, 1)
                v.wait_ge(m_e, b + 1)
                v.tensor_reduce(es[:, :], E.rearrange("p t c -> p c t"), AX.X, ALU.add).then_inc(m_es, 1)
                v.wait_ge(w_pv, b + 1)
                v.tensor_scalar(On[:, KVL:], ps[3][0:NS, 1, :], sm[:, 4:5], None, ALU.mult).then_inc(w_on, 1)
                v.wait_ge(m_pv, b + 1)
                link(v.reciprocal(sm[:, 6:7], ps[3][0:NS, 0, KVL:KVL + 1]))
                v.tensor_scalar(On[:, 0:KVL], ps[3][0:NS, 0, 0:KVL], sm[:, 6:7], None, ALU.mult).then_inc(m_on, 1)
                if not last_one:
                    page_lo(b + 1, 0)
                    page_lo(b + 1, 1)
                v.wait_ge(w_tt, b + 1)
                for z in range(2):
                    r = slice(z * HD, (z + 1) * HD)
                    o = ps[1][r, 1, 0:160].rearrange("p (c n) -> p c n", n=40)[:, :, 4 * z:4 * z + NQ]
                    last = v.tensor_copy(aT[r, HP:KD, bass.ds(b * NQ + NP_, NQ)], o)
                last.then_inc(w_o, 1)
                v.wait_ge(m_tt, b + 1)
                v.tensor_copy(oAbs[:, :, :, bass.ds(b * NQ, NQ)].rearrange("p c h q -> p (c h) q"),
                              ps[2][:, 1, 448:512].rearrange("p (x q) -> p x q", q=NQ)).then_inc(m_o, 1)
                assert chain["n"] == LOOP_LINKS, chain

            page_lo(0, 0)
            page_lo(0, 1)
            with v.Fori(0, NB - 1) as b:
                sequence(b, False)
            sequence(NB - 1, True)
            chain["base"], chain["n"] = before + NB * LOOP_LINKS, 0
            v.wait_ge(oa_ev, 1)
            dve_weight(W_O, W_WIDE)
            dve_norm_split(P_OA, {3: lambda: dve_weight(W_O + 1, W_WIDE)})
            dve_norm_split(P_OB)
            acc_clear(g_f)
            for m in range(KD):
                v.wait_ge(w_used, W_O + m + 1)
                v.tensor_tensor(hT[:, m, :].rearrange("p (a n) -> p a n", a=2), ps[m % 2][:, :, 0:HT],
                                hT[:, m, :].rearrange("p (a n) -> p a n", a=2), ALU.add).then_inc(wo_ev, 1)
                if m < KD - 1:
                    dve_weight(W_O + m + 2, W_WIDE)
                if m:
                    dve_accumulate(g_f, m - 1)
            dve_accumulate(g_f, KD - 1)
            v.wait_ge(wo_ev, KD)
            dve_norm_split(P_F, {4: lambda: dve_weight(W_GU + 1, W_WIDE)})
            v.wait_ge(out_s, 80)

            def dve_ffn(w0, wd, tiles, width, before, after):
                def gate_up(f, j, nxt):
                    dve_weight(w0 + 2 * j + 2, nxt, f * 4)
                    v.wait_ge(gu_act, f * 2 + (before + j + 1))
                    v.tensor_tensor(sq[:, j, :].rearrange("p (a n) -> p a n", a=2), ps[2 * j + 1][:, :, 0:HT],
                                    tmp[:, j, :].rearrange("p (a n) -> p a n", a=2), ALU.mult).then_inc(h_tmp, 1)
                    dve_weight(w0 + 2 * j + 3, nxt, f * 4)
                    v.wait_ge(h_hi, f * 2 + (before + j + 1))
                    one = bass.ds(f * 2 + j, 1)
                    v.tensor_tensor(hidLo[:, one, :].rearrange("p a n -> p (a n)"), sq[:, j, :],
                                    hidHi[:, one, :].rearrange("p a n -> p (a n)").bitcast(F32), ALU.subtract).then_inc(h_lo, 1)
                    v.sem_inc(gu_ev[j], 1)

                with v.Fori(0, tiles // 2 - 1) as f:
                    for j in range(2):
                        gate_up(f, j, W_WIDE)
                f = tiles // 2 - 1
                gate_up(f, 0, W_WIDE)
                gate_up(f, 1, width)

                def down(m, j, u, wide, i, split=True):
                    v.wait_ge(w_used, m + (wd + j + 1))
                    h2 = hT[:, bass.ds(m + j, 1), :].rearrange("p t (a n) -> p (t a) n", a=2)
                    v.tensor_tensor(h2, ps[j][:, :, 0:HT], h2, ALU.add).then_inc(dn_ev[j], 1)
                    if split:
                        dve_weight(u, wide, i)
                    if before and not (isinstance(m, int) and m + j == 0):
                        dve_accumulate(g_p, m + j - 1) if isinstance(m, int) else dve_accumulate(g_p, j + 1, m - 2)

                if before:
                    acc_clear(g_p)
                for j in range(2):
                    down(0, j, wd + j + 2, width, 0)
                with v.Fori(2, KD - 2, 2) as m:
                    for j in range(2):
                        down(m, j, wd + j + 2, width, m)
                for j in range(2):
                    down(KD - 2, j, wd + KD + j, after, 0, not (before and j))
                for j in range(2):
                    v.wait_ge(dn_ev[j], KD if before else KD // 2)

            dve_ffn(W_GU, W_DN, HALVES[0], DN_WIDE[0], 0, W_WIDE)
            dve_ffn(W_GU2, W_DN2, HALVES[1], DN_WIDE[1], HALVES[0], PL_WIDE)
            dve_accumulate(g_p, KD - 1)

            def ple_rest():
                dve_weight(W_PL + 1, PL_WIDE)
                v.wait_ge(pl_hi, 1)
                v.tensor_tensor(plLo[:, :, :], plT, plHi[:, :, :].bitcast(F32), ALU.subtract).then_inc(pl_lo, 1)

            dve_norm_split(P_P, {4: ple_rest})

            def ple(m, j, more):
                v.wait_ge(pl_act, m + (j + 1))
                t2 = tmp[:, j, :].rearrange("p (a n) -> p a n", a=2)
                o2 = sq[:, j, :].rearrange("p (a n) -> p a n", a=2)
                v.tensor_tensor(o2, ps[2 * j + 1][:, :, 0:HT], t2, ALU.mult).then_inc(pl_mul, 1)
                if more:
                    dve_weight(W_PL + j + 2, PL_WIDE, m)
                v.wait_ge(pl_mul, m + (j + 1) + FIRST)
                h2 = hT[:, bass.ds(m + j, 1), :].rearrange("p t (a n) -> p (t a) n", a=2)
                v.tensor_tensor(h2, o2, h2, ALU.add).then_inc(pl_ev[j], 1)

            with v.Fori(0, KD - 2, 2) as m:
                for j in range(2):
                    ple(m, j, True)
            for j in range(2):
                ple(KD - 2, j, False)


def constants():
    import numpy as np
    c = np.zeros((P, NC_), np.float32)
    i = np.arange(P)
    c[:, C_ONE:C_ONE + P] = 1
    c[:64, Z_64 + 15] = c[64:, Z_64 + 16] = 1 / HD
    c[:64, Z_96 + 15], c[64:96, Z_96 + 16] = 1 / NOPE, 1 / ROPE
    c[:, Z_CQ + 15:Z_CQ + 17] = 1 / QL
    c[:, Z_LAT + 15:Z_LAT + 17] = 1 / KVL
    c[W_ROW:W_ROW + 16, C_W:C_W + H * P] = np.arange(16)[:, None] == np.arange(H * P)[None] // 64
    c[:, C_ID:C_ID + P] = np.eye(P)
    pos = np.concatenate([np.arange(NP_), np.tile(PAST + np.arange(NQ), NB)]).astype(np.float32)

    def rope(rot, cs, sn, starts, half, theta):
        inv = np.float32(theta) ** (-np.arange(half, dtype=np.float32) / np.float32(half))
        ang = pos[None] * inv[:, None]
        c[:, cs:cs + T] = 1
        for s0 in starts:
            for j in range(half):
                a, b = s0 + j, s0 + half + j
                c[b, rot + a] = -1
                c[a, rot + b] = 1
                c[a, cs:cs + T] = c[b, cs:cs + T] = np.cos(ang[j])
                c[a, sn:sn + T] = c[b, sn:sn + T] = np.sin(ang[j])

    rope(C_RS, C_CS, C_SS, (0, 64), 8, 500000.0)
    rope(C_RQ, C_CQ, C_SQ, (64,), 16, 10000.0)

    def multiplicity(dist):
        n = sum((dist >= 0) & (dist <= w) & (dist % d == 0) for w, d in ((128, 1), (512, 4), (2048, 16)))
        return np.where(n > 0, np.log(np.maximum(n, 1)) / SC_B, NEG)

    for blk in range(4):
        dist = (3 - blk) * P + i[:, None] - i[None]
        c[:, C_MA + blk * P:C_MA + (blk + 1) * P] = np.where(dist >= 0, 0, NEG)
        c[:, C_MB + blk * P:C_MB + (blk + 1) * P] = multiplicity(dist)
    q = np.arange(NQ)
    older = 16 * np.arange(STR)[None] + np.arange(4)[:, None]
    key = np.concatenate([older.ravel(), np.arange(PAST - REC, PAST)])
    c[:NS, C_MW:C_MW + 896] = np.tile(multiplicity(PAST + q[:, None] - key[None]), (H, 1))
    for b in range(NB):
        same_t = (np.arange(NS)[None] // NQ == b)
        dist_t = q[:, None] - np.arange(NS)[None] % NQ
        same = (np.arange(NS)[:, None] // NQ == b)
        dist = q[None] - np.arange(NS)[:, None] % NQ
        c[:, C_MN + b * 32:C_MN + (b + 1) * 32] = NEG
        c[:NS, C_MN + b * 32:C_MN + (b + 1) * 32] = np.tile(np.where(same & (dist >= 0), 0, NEG), (1, H))
        c[:NS, C_MX + b * 32:C_MX + (b + 1) * 32] = np.tile(np.where(same_t, multiplicity(dist_t), NEG), (H, 1))
    return c


def kernel(**inputs):
    import numpy as np
    import concourse.bacc as bacc
    from concourse.bass_utils import run_bass_kernel_spmd as run

    a = {k: np.asarray(v) for k, v in inputs.items()}

    def tiles(w, width, start=0):
        k = w.shape[0] // P
        return w[:, start:start + width].reshape(k, P, width).transpose(1, 0, 2).reshape(P, k * width)

    def feat(x):
        return x.T.reshape(-1, P, x.shape[0]).transpose(1, 0, 2)

    w_in, w_kvb = a["w_in"][0], a["w_kvb"][0].reshape(KVL, H, 2, NOPE)
    a_end = QL + KVL + ROPE
    starts = [P * m for m in range(8)] + [a_end - HQ] + [a_end + P * m for m in range(12)]
    gate, up = a["w_gate"][0], a["w_up"][0]
    down = a["w_down"][0]
    gains = np.zeros((P, NG), np.float32)
    for name, col in (("g_attn", G_ATT), ("g_ffn", G_FFN), ("g_ple", G_PLE), ("b_ple_gate", B_PLE), ("g_qa", G_QA),
                      ("g_kva", G_KVA), ("g_oa", G_OA), ("g_ob", G_OB)):
        g = a[name][0].reshape(-1, P).T
        gains[:, col:col + g.shape[1]] = g
    gains[:NOPE, G_Q], gains[NOPE:HQ, G_Q] = a["g_qn"][0], a["g_qr"][0]
    gains[:NOPE, G_K], gains[NOPE:HQ, G_K] = a["g_kn"][0], a["g_kr"][0]
    for name, col in (("g_qs", G_QS), ("g_ks", G_KS)):
        gains[:HD, col] = gains[HD:, col] = a[name][0]
    gains[:, G_EPS] = EPS

    lat = a["cache_latent"][0]
    ck = a["cache_swa_k"][0].reshape(NB, PAST, HP, P)
    old = np.arange(PAST - REC).reshape(STR, 16).T
    order = np.concatenate([old[4:].ravel(), old[:4].ravel(), np.arange(PAST - REC, PAST)])
    tok = lambda p, s: np.concatenate([p.reshape(NP_, -1), s.reshape(NS, -1)])
    arr = dict(
        x=feat(tok(a["x_prompt"], a["x_sample"])),
        cst=constants(),
        gains=gains,
        win=np.stack([tiles(w_in, P, s) for s in starts]),
        wqb=np.stack([tiles(a["w_qb"][0], HQ, HQ * h) for h in range(H)]),
        wk=w_kvb[:, :, 0].reshape(KC, P, 512).transpose(1, 0, 2),
        wv=w_kvb[:, :, 1].reshape(KC, P, 512).transpose(1, 0, 2),
        wkt=w_kvb[:, :, 0].transpose(2, 1, 0),
        wo=np.stack([tiles(a["w_o"][0], P, P * m) for m in range(KD)]),
        wgu=np.stack([tiles(w, P, P * m) for m in range(KF) for w in (gate, up)]),
        wdn=np.stack([tiles(down[:HALVES[0] * P], P, P * m) for m in range(KD)]),
        wdn2=np.stack([tiles(down[HALVES[0] * P:], P, P * m) for m in range(KD)]),
        wpl=np.stack([np.concatenate([tiles(a["w_ple_gate"][0], P, P * m), tiles(a["w_ple_proj"][0], P, P * m)], 1)
                      for m in range(KD)]),
        plt=feat(tok(a["p_prompt"], a["p_sample"])),
        pgt=lat.reshape(POOL, PAGE, KC, P).transpose(0, 3, 2, 1).reshape(POOL, P, KC * PAGE),
        pgk=a["cache_krope"][0].transpose(0, 2, 1),
        pgl=lat,
        ck=ck[:, order].transpose(0, 2, 3, 1),
        cv=a["cache_swa_v"][0].reshape(NB, PAST, 512),
        pt=a["page_table"].reshape(1, NB * NPG),
    )
    arr = {k: np.ascontiguousarray(v) for k, v in arr.items()}
    outs = dict(y=(KD, P, T), o_lat=(P, KC, T), o_kr=(ROPE, T), o_ks=(P, HP, T), o_vs=(NP_, 512),
                o_ck=(NB, HP, P, PAST), o_cv=(NB, PAST, 512))
    nc = bacc.Bacc("TRN2", target_bir_lowering=False, num_devices=1)
    args = [nc.dram_tensor(f"in_{k}", v.shape, mybir.dt.from_np(v.dtype), kind="ExternalInput").ap() for k, v in arr.items()]
    args += [nc.dram_tensor(f"out_{k}", s, F32, kind="ExternalOutput").ap() for k, s in outs.items()]
    build(nc, *args)
    r = run(nc, [{f"in_{k}": v for k, v in arr.items()}], core_ids=[0]).results[0]
    o = {k: np.asarray(r[f"out_{k}"]) for k in outs}

    def rows(x, width):
        x = x.reshape(width, T).T
        return x[:NP_], x[NP_:]

    yp, ys = rows(o["y"], D)
    lp, ls = rows(o["o_lat"].transpose(1, 0, 2), KVL)
    kp, ks = rows(o["o_kr"], ROPE)
    sp, ss = rows(o["o_ks"].transpose(1, 0, 2), 512)
    back = np.empty(PAST, np.int64)
    back[order] = np.arange(PAST)
    kold = o["o_ck"].reshape(NB, 512, PAST)[:, :, back[NQ:]].transpose(0, 2, 1)
    swk = np.concatenate([kold, ss.reshape(NB, NQ, 512)], 1)
    return (yp.reshape(1, NP_, D), ys.reshape(NB, NQ, D), lp.reshape(1, 1, NP_, KVL), kp.reshape(1, 1, NP_, ROPE),
            sp.reshape(1, 1, NP_, H, HD), o["o_vs"].reshape(1, 1, NP_, H, HD), ls.reshape(1, NB, NQ, KVL),
            ks.reshape(1, NB, NQ, ROPE), swk.reshape(1, NB, PAST, H, HD), o["o_cv"].reshape(1, NB, PAST, H, HD))
```
